# Optimizing a Trainium2 kernel written in Bass

```python
import math
import jax, jax.numpy as jnp
from jax import lax
import numpy as np

D_MODEL = 1024
BATCH = 1
SEQ = 128
DEPTH = 2
DEC_BATCH = 1
DEC_SEQ = 128
PAST_LEN = 128

GRID_W = 64
N_EVEN = (DEPTH + 1) // 2
N_ODD = DEPTH // 2
EPS = 1e-6

SSD_HEADS = 16
SSD_HEAD_DIM = 64
D_SSD = SSD_HEADS * SSD_HEAD_DIM
SSD_GROUPS = 2
SSD_STATE = 128
SSD_CONV = 5
SSD_CHUNK = 128
CONV_DIM = D_SSD + 2 * SSD_GROUPS * SSD_STATE

ATT_HEADS = 16
ATT_KV_HEADS = 4
ATT_REP = ATT_HEADS // ATT_KV_HEADS
ATT_HEAD_DIM = 64
D_ATT = ATT_HEADS * ATT_HEAD_DIM
ATT_KV_DIM = ATT_KV_HEADS * ATT_HEAD_DIM
WINDOW = 128
ATT_BLOCK = 128
ATT_SCALE = ATT_HEAD_DIM ** -0.5
ROPE_BASE = 10000.0

GLA_HEADS = 4
GLA_DK = D_MODEL // 2
GLA_DV = D_MODEL
GLA_HEAD_K = GLA_DK // GLA_HEADS
GLA_HEAD_V = GLA_DV // GLA_HEADS
GLA_LOWRANK = 16
GLA_GATE_NORM = 16.0
GLA_CHUNK = 64

N_EXPERT_GROUPS = 4
EXPERTS_PER_GROUP = 4
N_EXPERTS = N_EXPERT_GROUPS * EXPERTS_PER_GROUP
TOP_K = 2
D_EXPERT = 512

EVEN_SPLITS = (D_SSD, D_SSD + CONV_DIM, D_SSD + CONV_DIM + 2 * SSD_HEADS,
               D_SSD + CONV_DIM + 2 * SSD_HEADS + D_ATT,
               D_SSD + CONV_DIM + 2 * SSD_HEADS + D_ATT + ATT_KV_DIM)
D_IN_EVEN = D_SSD + CONV_DIM + 2 * SSD_HEADS + D_ATT + 2 * ATT_KV_DIM
ODD_SPLITS = (GLA_DK, 2 * GLA_DK, 2 * GLA_DK + GLA_DV, 2 * GLA_DK + 2 * GLA_DV,
              2 * GLA_DK + 2 * GLA_DV + GLA_LOWRANK)
D_IN_ODD = 2 * GLA_DK + 2 * GLA_DV + 2 * GLA_LOWRANK

kernel_name = 'hybrid_ssd_swa_gla_hmoe_prefix_ctx'

F32 = jnp.float32

def rms_norm(x, w):
    xf = x.astype(F32)
    y = xf * lax.rsqrt(jnp.mean(xf * xf, axis=-1, keepdims=True) + EPS)
    return (y * w.astype(F32)).astype(x.dtype)

def adaln_params(cond, w, b):
    m = jax.nn.silu(cond) @ w + b
    return jnp.split(m[:, None, :], 6, axis=-1)

def modulate(x, norm_w, shift, scale):
    return rms_norm(x, norm_w) * (1 + scale) + shift

def flip(t):
    return jnp.flip(t, axis=1)

def centred_dwconv(x, w, b):
    pad = w.shape[0] // 2
    xp = jnp.pad(x, ((0, 0), (pad, pad), (0, 0)))
    y = lax.conv_general_dilated(xp, w[:, None, :], window_strides=(1,), padding='VALID',
                                 dimension_numbers=('NWC', 'WIO', 'NWC'),
                                 feature_group_count=x.shape[-1])
    return y + b

def ssd_scan(x, dt, A, Bm, Cm, h0):
    b, l, h, p = x.shape
    g, n = Bm.shape[2], Bm.shape[3]
    r = h // g
    L = SSD_CHUNK
    nc = l // L
    xc = (x.astype(F32) * dt[..., None]).reshape(b, nc, L, g, r, p)
    Bc = Bm.astype(F32).reshape(b, nc, L, g, n)
    Cc = Cm.astype(F32).reshape(b, nc, L, g, n)
    a_cs = jnp.cumsum((dt * A).reshape(b, nc, L, g, r), axis=2)
    causal = jnp.tril(jnp.ones((L, L), bool))[:, :, None, None]
    seg = a_cs[:, :, :, None] - a_cs[:, :, None, :]
    decay = jnp.exp(jnp.where(causal, seg, -jnp.inf))
    cb = jnp.einsum('bclgn,bcsgn->bclsg', Cc, Bc)
    y_diag = jnp.einsum('bclsg,bclsgr,bcsgrp->bclgrp', cb, decay, xc)
    to_end = jnp.exp(a_cs[:, :, -1:] - a_cs)
    chunk_states = jnp.einsum('bclgn,bclgr,bclgrp->bcgrpn', Bc, to_end, xc)
    chunk_decay = jnp.exp(a_cs[:, :, -1])

    def step(hprev, inp):
        st, dec = inp
        return dec[..., None, None] * hprev + st, hprev

    h_final, h_prev = lax.scan(step, h0.astype(F32).reshape(b, g, r, p, n),
                               (jnp.moveaxis(chunk_states, 1, 0), jnp.moveaxis(chunk_decay, 1, 0)))
    h_prev = jnp.moveaxis(h_prev, 0, 1)
    y_off = jnp.einsum('bclgn,bclgr,bcgrpn->bclgrp', Cc, jnp.exp(a_cs), h_prev)
    return (y_diag + y_off).reshape(b, l, h, p), h_final.reshape(b, h, p, n)

def ssd_mixer(z, xbc, dt_raw, conv_w, conv_b, dt_bias_f, dt_bias_b, a_log_f, a_log_b, d_skip, norm_w, h0_f, h0_b):
    b, l, _ = z.shape
    xbc = jax.nn.silu(centred_dwconv(xbc, conv_w, conv_b))
    xs, Bm, Cm = jnp.split(xbc, (D_SSD, D_SSD + SSD_GROUPS * SSD_STATE), axis=-1)
    xs = xs.reshape(b, l, SSD_HEADS, SSD_HEAD_DIM)
    Bm = Bm.reshape(b, l, SSD_GROUPS, SSD_STATE)
    Cm = Cm.reshape(b, l, SSD_GROUPS, SSD_STATE)
    dtf = dt_raw.astype(F32)
    dt_f = jax.nn.softplus(dtf[..., :SSD_HEADS] + dt_bias_f.astype(F32))
    dt_b = jax.nn.softplus(dtf[..., SSD_HEADS:] + dt_bias_b.astype(F32))
    A_f = -jnp.exp(a_log_f.astype(F32))
    A_b = -jnp.exp(a_log_b.astype(F32))
    y_f, s_f = ssd_scan(xs, dt_f, A_f, Bm, Cm, h0_f)
    y_b, s_b = ssd_scan(flip(xs), flip(dt_b), A_b, flip(Bm), flip(Cm), h0_b)
    y = y_f + flip(y_b) + d_skip.astype(F32)[:, None] * xs.astype(F32)
    y = rms_norm(y.reshape(b, l, D_SSD) * jax.nn.silu(z.astype(F32)), norm_w)
    return y.astype(z.dtype), s_f, s_b

def axial_rope(t, rows):
    half = t.shape[-1] // 2
    quarter = half // 2
    row = jnp.repeat(jnp.arange(rows), GRID_W)
    col = jnp.tile(jnp.arange(GRID_W), rows)
    inv = ROPE_BASE ** (-jnp.arange(quarter, dtype=F32) / quarter)

    def rot(u, pos):
        ang = pos.astype(F32)[:, None] * inv[None, :]
        cos = jnp.cos(ang)[None, :, None, :]
        sin = jnp.sin(ang)[None, :, None, :]
        u1, u2 = u[..., :quarter], u[..., quarter:]
        return jnp.concatenate([u1 * cos - u2 * sin, u1 * sin + u2 * cos], axis=-1)

    tf = t.astype(F32)
    return jnp.concatenate([rot(tf[..., :half], row), rot(tf[..., half:], col)], axis=-1).astype(t.dtype)

def sink_softmax(scores, sink):
    sk = jnp.broadcast_to(sink.astype(F32).reshape(ATT_KV_HEADS, ATT_REP)[None, :, :, None, None],
                          scores.shape[:-1] + (1,))
    p = jax.nn.softmax(jnp.concatenate([sk, scores], axis=-1), axis=-1)
    return p[..., 1:]

def context_attention(q, k, v, sink):
    b, l = q.shape[:2]
    nb = l // ATT_BLOCK
    qb = jnp.moveaxis(q.reshape(b, nb, ATT_BLOCK, ATT_KV_HEADS, ATT_REP, ATT_HEAD_DIM), 1, 0)
    vf = v.astype(F32)

    def one(q_blk):
        s = jnp.einsum('bqkrd,bskd->bkrqs', q_blk, k, preferred_element_type=F32) * ATT_SCALE
        p = sink_softmax(s, sink)
        return jnp.einsum('bkrqs,bskd->bqkrd', p, vf)

    o = lax.map(one, qb)
    return jnp.moveaxis(o, 0, 1).reshape(b, l, D_ATT).astype(q.dtype)

def latent_attention(q, q_nopos, k, v, ck, cv, sink):
    b, l = q.shape[:2]
    B = ATT_BLOCK
    nb = l // B
    n_ctx = ck.shape[1]
    shp = (b, nb, B, ATT_KV_HEADS, ATT_REP, ATT_HEAD_DIM)
    qb = jnp.moveaxis(q.reshape(shp), 1, 0)
    qnb = jnp.moveaxis(q_nopos.reshape(shp), 1, 0)

    def windows(t):
        tb = t.reshape(b, nb, B, ATT_KV_HEADS, ATT_HEAD_DIM)
        zero = jnp.zeros_like(tb[:, :1])
        win = jnp.concatenate([jnp.concatenate([zero, tb[:, :-1]], axis=1), tb,
                               jnp.concatenate([tb[:, 1:], zero], axis=1)], axis=2)
        return jnp.moveaxis(win, 1, 0)

    kw, vw = windows(k), windows(v)
    qpos = jnp.arange(B)
    kpos = jnp.arange(3 * B) - B
    band = jnp.abs(qpos[:, None] - kpos[None, :]) <= WINDOW
    cvf = cv.astype(F32)

    def one(args):
        q_blk, qn_blk, k_win, v_win, blk = args
        s_ctx = jnp.einsum('bqkrd,bskd->bkrqs', qn_blk, ck, preferred_element_type=F32) * ATT_SCALE
        s_win = jnp.einsum('bqkrd,bskd->bkrqs', q_blk, k_win, preferred_element_type=F32) * ATT_SCALE
        kabs = blk * B + kpos
        ok = band & ((kabs >= 0) & (kabs < l))[None, :]
        s_win = jnp.where(ok, s_win, -jnp.inf)
        p = sink_softmax(jnp.concatenate([s_ctx, s_win], axis=-1), sink)
        return (jnp.einsum('bkrqs,bskd->bqkrd', p[..., :n_ctx], cvf)
                + jnp.einsum('bkrqs,bskd->bqkrd', p[..., n_ctx:], v_win.astype(F32)))

    o = lax.map(one, (qb, qnb, kw, vw, jnp.arange(nb)))
    return jnp.moveaxis(o, 0, 1).reshape(b, l, D_ATT).astype(q.dtype)

def even_mixer_context(h, w_in, conv_w, conv_b, dtb_f, dtb_b, al_f, al_b, d_skip, ssd_nw, sink, w_out):
    b, l, _ = h.shape
    z, xbc, dtr, q, k, v = jnp.split(h @ w_in, EVEN_SPLITS, axis=-1)
    h0 = jnp.zeros((b, SSD_HEADS, SSD_HEAD_DIM, SSD_STATE), F32)
    y_ssd, s_f, s_b = ssd_mixer(z, xbc, dtr, conv_w, conv_b, dtb_f, dtb_b, al_f, al_b, d_skip, ssd_nw, h0, h0)
    q = q.reshape(b, l, ATT_HEADS, ATT_HEAD_DIM)
    k = k.reshape(b, l, ATT_KV_HEADS, ATT_HEAD_DIM)
    v = v.reshape(b, l, ATT_KV_HEADS, ATT_HEAD_DIM)
    y_att = context_attention(q, k, v, sink)
    out = jnp.concatenate([y_ssd, y_att], axis=-1) @ w_out
    return out, k, v, s_f, s_b

def even_mixer_latent(h, ck, cv, h0_f, h0_b, rows, w_in, conv_w, conv_b, dtb_f, dtb_b, al_f, al_b, d_skip, ssd_nw, sink, w_out):
    b, l, _ = h.shape
    z, xbc, dtr, q, k, v = jnp.split(h @ w_in, EVEN_SPLITS, axis=-1)
    y_ssd, _, _ = ssd_mixer(z, xbc, dtr, conv_w, conv_b, dtb_f, dtb_b, al_f, al_b, d_skip, ssd_nw, h0_f, h0_b)
    q = q.reshape(b, l, ATT_HEADS, ATT_HEAD_DIM)
    k = k.reshape(b, l, ATT_KV_HEADS, ATT_HEAD_DIM)
    v = v.reshape(b, l, ATT_KV_HEADS, ATT_HEAD_DIM)
    y_att = latent_attention(axial_rope(q, rows), q, axial_rope(k, rows), v, ck, cv, sink)
    return jnp.concatenate([y_ssd, y_att], axis=-1) @ w_out

def gla_scan(q, k, v, g, s0):
    b, l, h, dk = q.shape
    dv = v.shape[-1]
    C = GLA_CHUNK
    nc = l // C
    qc = q.astype(F32).reshape(b, nc, C, h, dk)
    kc = k.astype(F32).reshape(b, nc, C, h, dk)
    vc = v.astype(F32).reshape(b, nc, C, h, dv)
    cs = jnp.cumsum(g.reshape(b, nc, C, h, dk), axis=2)
    q_t = qc * jnp.exp(cs)
    k_t = kc * jnp.exp(-cs)
    causal = jnp.tril(jnp.ones((C, C), bool))
    att = jnp.where(causal, jnp.einsum('bclhd,bcshd->bchls', q_t, k_t), 0.0)
    y_intra = jnp.einsum('bchls,bcshv->bclhv', att, vc)
    chunk_kv = jnp.einsum('bcshd,bcshv->bchdv', kc * jnp.exp(cs[:, :, -1:] - cs), vc)
    chunk_decay = jnp.exp(cs[:, :, -1])

    def step(sprev, inp):
        kv, dec = inp
        return dec[..., None] * sprev + kv, sprev

    s_final, s_prev = lax.scan(step, s0.astype(F32),
                               (jnp.moveaxis(chunk_kv, 1, 0), jnp.moveaxis(chunk_decay, 1, 0)))
    y_inter = jnp.einsum('bclhd,bchdv->bclhv', q_t, jnp.moveaxis(s_prev, 0, 1))
    return (y_intra + y_inter).reshape(b, l, h, dv), s_final

def gla_layer(h, w_in, w_gk2_f, b_gk_f, w_gk2_b, b_gk_b, norm_w, w_out, s0_f, s0_b):
    b, l, _ = h.shape
    q, k, v, r, lr_f, lr_b = jnp.split(h @ w_in, ODD_SPLITS, axis=-1)
    q = q.reshape(b, l, GLA_HEADS, GLA_HEAD_K) * GLA_HEAD_K ** -0.5
    k = k.reshape(b, l, GLA_HEADS, GLA_HEAD_K)
    v = v.reshape(b, l, GLA_HEADS, GLA_HEAD_V)
    g_f = (jax.nn.log_sigmoid((lr_f @ w_gk2_f + b_gk_f).astype(F32)) / GLA_GATE_NORM).reshape(b, l, GLA_HEADS, GLA_HEAD_K)
    g_b = (jax.nn.log_sigmoid((lr_b @ w_gk2_b + b_gk_b).astype(F32)) / GLA_GATE_NORM).reshape(b, l, GLA_HEADS, GLA_HEAD_K)
    y_f, s_f = gla_scan(q, k, v, g_f, s0_f)
    y_b, s_b = gla_scan(flip(q), flip(k), flip(v), flip(g_b), s0_b)
    y = rms_norm(y_f + flip(y_b), norm_w).reshape(b, l, GLA_DV) * jax.nn.silu(r.astype(F32))
    return y.astype(h.dtype) @ w_out, s_f, s_b

def hier_moe(h, w_rg, b_rg, w_re, b_re, w_gate, w_up, w_down):
    b, l, d = h.shape
    t = h.reshape(-1, d)
    n_tok = t.shape[0]
    g_logit = (t @ w_rg + b_rg).astype(F32)
    g_sel = jnp.argmax(g_logit, axis=-1)
    g_prob = jnp.take_along_axis(jax.nn.softmax(g_logit, axis=-1), g_sel[:, None], axis=-1)
    e_logit = (t @ w_re + b_re).astype(F32).reshape(n_tok, N_EXPERT_GROUPS, EXPERTS_PER_GROUP)
    e_logit = jnp.take_along_axis(e_logit, g_sel[:, None, None], axis=1)[:, 0]
    top_v, top_i = lax.top_k(jax.nn.softmax(e_logit, axis=-1), TOP_K)
    top_v = top_v / jnp.sum(top_v, axis=-1, keepdims=True)
    local = jnp.einsum('tk,tke->te', top_v, jax.nn.one_hot(top_i, EXPERTS_PER_GROUP, dtype=F32))
    combine = (jax.nn.one_hot(g_sel, N_EXPERT_GROUPS, dtype=F32)[:, :, None] * local[:, None, :]
               * g_prob[:, :, None]).reshape(n_tok, N_EXPERTS).astype(t.dtype)
    hg = jnp.einsum('td,edf->tef', t, w_gate)
    hu = jnp.einsum('td,edf->tef', t, w_up)
    act = jax.nn.silu(hg) * hu * combine[:, :, None]
    return jnp.einsum('tef,efd->td', act, w_down).reshape(b, l, d)

def setup_inputs(seed: int = 0) -> dict:
    key = jax.random.key(seed)
    keys = iter(jax.random.split(key, 64))
    D = D_MODEL

    def nrm(shape, scale):
        return jax.random.normal(next(keys), shape, F32) * scale

    dt0 = jnp.exp(jax.random.uniform(next(keys), (2, N_EVEN, SSD_HEADS), F32,
                                     minval=math.log(1e-3), maxval=math.log(1e-1)))
    dt_bias = dt0 + jnp.log(-jnp.expm1(-dt0))
    a_log = jnp.log(jax.random.uniform(next(keys), (2, N_EVEN, SSD_HEADS), F32, minval=1.0, maxval=16.0))
    return {
        'x_prompt': nrm((BATCH, SEQ, D), 1.0),
        'x_sample': nrm((DEC_BATCH, DEC_SEQ, D), 1.0),
        'cache_k_attn': nrm((DEC_BATCH, N_EVEN, PAST_LEN, ATT_KV_HEADS, ATT_HEAD_DIM), 1.0),
        'cache_v_attn': nrm((DEC_BATCH, N_EVEN, PAST_LEN, ATT_KV_HEADS, ATT_HEAD_DIM), 1.0),
        'state_ssd_fwd': nrm((DEC_BATCH, N_EVEN, SSD_HEADS, SSD_HEAD_DIM, SSD_STATE), 0.1),
        'state_ssd_bwd': nrm((DEC_BATCH, N_EVEN, SSD_HEADS, SSD_HEAD_DIM, SSD_STATE), 0.1),
        'state_gla_fwd': nrm((DEC_BATCH, N_ODD, GLA_HEADS, GLA_HEAD_K, GLA_HEAD_V), 0.5),
        'state_gla_bwd': nrm((DEC_BATCH, N_ODD, GLA_HEADS, GLA_HEAD_K, GLA_HEAD_V), 0.5),
        'c': nrm((DEC_BATCH, D), 1.0),
        'c_ctx': nrm((D,), 1.0),
        'w_ada': nrm((DEPTH, D, 6 * D), 0.5 * D ** -0.5),
        'b_ada': nrm((DEPTH, 6 * D), 0.02),
        'norm_mix_w': 1.0 + nrm((DEPTH, D), 0.02),
        'norm_ffn_w': 1.0 + nrm((DEPTH, D), 0.02),
        'w_in_even': nrm((N_EVEN, D, D_IN_EVEN), D ** -0.5),
        'conv_w': nrm((N_EVEN, SSD_CONV, CONV_DIM), SSD_CONV ** -0.5),
        'conv_b': nrm((N_EVEN, CONV_DIM), 0.02),
        'dt_bias_fwd': dt_bias[0],
        'dt_bias_bwd': dt_bias[1],
        'a_log_fwd': a_log[0],
        'a_log_bwd': a_log[1],
        'd_skip': 1.0 + nrm((N_EVEN, SSD_HEADS), 0.1),
        'ssd_norm_w': 1.0 + nrm((N_EVEN, D_SSD), 0.02),
        'attn_sink': nrm((N_EVEN, ATT_HEADS), 0.5),
        'w_out_even': nrm((N_EVEN, D_SSD + D_ATT, D), (D_SSD + D_ATT) ** -0.5),
        'w_in_odd': nrm((N_ODD, D, D_IN_ODD), D ** -0.5),
        'w_gk2_fwd': nrm((N_ODD, GLA_LOWRANK, GLA_DK), GLA_LOWRANK ** -0.5),
        'b_gk_fwd': nrm((N_ODD, GLA_DK), 0.1),
        'w_gk2_bwd': nrm((N_ODD, GLA_LOWRANK, GLA_DK), GLA_LOWRANK ** -0.5),
        'b_gk_bwd': nrm((N_ODD, GLA_DK), 0.1),
        'gla_norm_w': 1.0 + nrm((N_ODD, GLA_HEAD_V), 0.02),
        'w_out_odd': nrm((N_ODD, GLA_DV, D), GLA_DV ** -0.5),
        'w_router_group': nrm((DEPTH, D, N_EXPERT_GROUPS), D ** -0.5),
        'b_router_group': nrm((DEPTH, N_EXPERT_GROUPS), 0.01),
        'w_router_expert': nrm((DEPTH, D, N_EXPERTS), D ** -0.5),
        'b_router_expert': nrm((DEPTH, N_EXPERTS), 0.01),
        'w_gate_exp': nrm((DEPTH, N_EXPERTS, D, D_EXPERT), D ** -0.5),
        'w_up_exp': nrm((DEPTH, N_EXPERTS, D, D_EXPERT), D ** -0.5),
        'w_down_exp': nrm((DEPTH, N_EXPERTS, D_EXPERT, D), D_EXPERT ** -0.5),
        'final_norm_w': 1.0 + nrm((D,), 0.02),
    }

def reference(x_prompt, x_sample, cache_k_attn, cache_v_attn, state_ssd_fwd, state_ssd_bwd,
              state_gla_fwd, state_gla_bwd, c, c_ctx, w_ada, b_ada, norm_mix_w, norm_ffn_w,
              w_in_even, conv_w, conv_b, dt_bias_fwd, dt_bias_bwd, a_log_fwd, a_log_bwd, d_skip,
              ssd_norm_w, attn_sink, w_out_even, w_in_odd, w_gk2_fwd, b_gk_fwd, w_gk2_bwd, b_gk_bwd,
              gla_norm_w, w_out_odd, w_router_group, b_router_group, w_router_expert, b_router_expert,
              w_gate_exp, w_up_exp, w_down_exp, final_norm_w):
    rows = x_sample.shape[1] // GRID_W
    xc, xl = x_prompt, x_sample
    ks, vs, sfs, sbs, gfs, gbs = [], [], [], [], [], []
    for i in range(DEPTH):
        j = i // 2
        mc = adaln_params(c_ctx[None, :], w_ada[i], b_ada[i])
        ml = adaln_params(c, w_ada[i], b_ada[i])
        hc = modulate(xc, norm_mix_w[i], mc[0], mc[1])
        hl = modulate(xl, norm_mix_w[i], ml[0], ml[1])
        if i % 2 == 0:
            oc, k_new, v_new, s_f, s_b = even_mixer_context(
                hc, w_in_even[j], conv_w[j], conv_b[j], dt_bias_fwd[j], dt_bias_bwd[j],
                a_log_fwd[j], a_log_bwd[j], d_skip[j], ssd_norm_w[j], attn_sink[j], w_out_even[j])
            ol = even_mixer_latent(
                hl, cache_k_attn[:, j], cache_v_attn[:, j], state_ssd_fwd[:, j], state_ssd_bwd[:, j], rows,
                w_in_even[j], conv_w[j], conv_b[j], dt_bias_fwd[j], dt_bias_bwd[j],
                a_log_fwd[j], a_log_bwd[j], d_skip[j], ssd_norm_w[j], attn_sink[j], w_out_even[j])
            ks.append(k_new)
            vs.append(v_new)
            sfs.append(s_f)
            sbs.append(s_b)
        else:
            z0 = jnp.zeros((xc.shape[0], GLA_HEADS, GLA_HEAD_K, GLA_HEAD_V), F32)
            oc, g_f, g_b = gla_layer(hc, w_in_odd[j], w_gk2_fwd[j], b_gk_fwd[j], w_gk2_bwd[j], b_gk_bwd[j],
                                     gla_norm_w[j], w_out_odd[j], z0, z0)
            ol, _, _ = gla_layer(hl, w_in_odd[j], w_gk2_fwd[j], b_gk_fwd[j], w_gk2_bwd[j], b_gk_bwd[j],
                                 gla_norm_w[j], w_out_odd[j], state_gla_fwd[:, j], state_gla_bwd[:, j])
            gfs.append(g_f)
            gbs.append(g_b)
        xc = xc + mc[2] * oc
        xl = xl + ml[2] * ol
        xc = xc + mc[5] * hier_moe(modulate(xc, norm_ffn_w[i], mc[3], mc[4]), w_router_group[i], b_router_group[i],
                                   w_router_expert[i], b_router_expert[i], w_gate_exp[i], w_up_exp[i], w_down_exp[i])
        xl = xl + ml[5] * hier_moe(modulate(xl, norm_ffn_w[i], ml[3], ml[4]), w_router_group[i], b_router_group[i],
                                   w_router_expert[i], b_router_expert[i], w_gate_exp[i], w_up_exp[i], w_down_exp[i])
    y_prompt = rms_norm(xc, final_norm_w)
    y_sample = rms_norm(xl, final_norm_w)
    new_cache_k_attn = jnp.stack(ks, axis=1)
    new_cache_v_attn = jnp.stack(vs, axis=1)
    new_state_ssd_fwd = jnp.stack(sfs, axis=1)
    new_state_ssd_bwd = jnp.stack(sbs, axis=1)
    new_state_gla_fwd = jnp.stack(gfs, axis=1)
    new_state_gla_bwd = jnp.stack(gbs, axis=1)
    return (y_prompt, y_sample, new_cache_k_attn, new_cache_v_attn, new_state_ssd_fwd, new_state_ssd_bwd, new_state_gla_fwd, new_state_gla_bwd)


_drawn_inputs = setup_inputs


def setup_inputs(seed=0):
    import zlib

    import numpy as np

    out = dict(_drawn_inputs(seed))
    spreads = {}
    factors = {'cache_k_attn': 3.364,
     'state_gla_fwd': 8.0,
     'state_gla_bwd': 8.0,
     'norm_ffn_w': 3.755,
     'd_skip': 4.231,
     'ssd_norm_w': 7.798,
     'attn_sink': 8.0,
     'gla_norm_w': 8.0,
     'b_router_group': 4.413,
     'b_router_expert': 8.0,
     'final_norm_w': 2.718}
    for name, (base, spread) in spreads.items():
        noise = np.random.default_rng([zlib.crc32(name.encode()), seed]).standard_normal(out[name].shape)
        drawn = base * np.exp(spread * noise) if base else spread * noise
        out[name] = __import__('jax').numpy.asarray(drawn.astype(out[name].dtype))
    for name, factor in factors.items():
        out[name] = (out[name] * factor).astype(out[name].dtype)
    return out
```

```python
from contextlib import ExitStack

import numpy as np
import concourse.bass as bass
from concourse import mybir

F32 = mybir.dt.float32
ACT = mybir.ActivationFunctionType
ALU = mybir.AluOpType
AX = mybir.AxisListType

P = 128
D = 1024
KT = D // P
T = 256
NS = 2
GRID_W = 64
EPS = 1e-6
HEADS, HP, NST = 16, 64, 128
CONV_TILES = 12
TAPS = 5
KVH = 4
SCALE = 0.125
GH, GK, GV, CH = 4, 128, 256, 64
GLA_SCALE = float(GK) ** -0.5
NE, FE = 16, 512
FT = FE // P
CHUNK = 2048
RING = 6
PER_EXPERT = 6
assert RING == PER_EXPERT
COMBOS = ((0, 0, 0), (0, 0, 1), (0, 1, 1), (0, 1, 0), (1, 0, 0), (1, 1, 1))

BADA, NMIX, NFFN = 0, 96, 112
CONVW, CONVB, SSDN, GLAN, FINN, CVEC, CCTX = 128, 188, 200, 208, 210, 218, 226

(IDENT, ONES, MEAN_D, MEAN_V, LE, GE, GT, LT, BLE, BGE, BGT, BLT, COS, SIN, ROT) = range(15)
NCONST = 15


def constants():
    i = np.arange(P)
    k, m = i[:, None], i[None, :]
    c = np.zeros((NCONST, P, P), np.float32)
    same = (k // CH) == (m // CH)
    c[IDENT] = k == m
    c[ONES] = 1.0
    c[MEAN_D] = 1.0 / D
    c[MEAN_V] = 1.0 / GV
    c[LE], c[GE], c[GT], c[LT] = k <= m, k >= m, k > m, k < m
    for n, cond in ((BLE, k <= m), (BGE, k >= m), (BGT, k > m), (BLT, k < m)):
        c[n] = (cond & same) / 16.0
    quarter = 16
    inv = (np.float32(10000.0) ** (-np.arange(quarter, dtype=np.float32) / np.float32(quarter))).astype(np.float32)
    d = i % 64
    pos = np.where(d[:, None] < 32, m // GRID_W, m % GRID_W).astype(np.float32)
    ang = (pos * inv[d % quarter][:, None]).astype(np.float32)
    c[COS], c[SIN] = np.cos(ang), np.sin(ang)
    for q in range(P):
        if q % 32 < quarter:
            c[ROT][q + quarter, q] = -1.0
        else:
            c[ROT][q - quarter, q] = 1.0
    return np.ascontiguousarray(c.transpose(1, 0, 2))



DTX, DTA, DTT, DTE, DTU, DTL, DT, TE, WS = 0, 64, 128, 192, 256, 320, 384, 448, 480
CBM = 512
MX, NEGM, RSUM, SNKD, SNKE, RINV = 0, 16, 32, 48, 64, 80
(LG, GMAX, OHG, GEX, EPR, EL, EMX, OH1, P2, M2, OH2, DEN, GPR, LOC, CMB, VAL, VMX) = \
    (0, 40, 48, 56, 64, 96, 104, 120, 128, 136, 144, 152, 156, 160, 192, 224, 232)


def build(nc, A, O):
    with ExitStack() as ctx:
        def sb(name, shape):
            return ctx.enter_context(nc.sbuf_tensor(name, shape, F32))

        sems = {}

        def S(name):
            if name not in sems:
                sems[name] = ctx.enter_context(nc.semaphore(name))
            return sems[name]

        ring = sb("ring", [P, RING, CHUNK])
        cst = sb("cst", [P, NCONST, P])
        xT = sb("xT", [P, KT, T])
        hT = sb("hT", [P, KT, T])
        rows = sb("rows", [P, 2, P])
        feat = sb("feat", [P, 2 * P])
        csilu = sb("csilu", [P, KT, NS])
        mods = sb("mods", [P, 2, 48, NS])
        rstd = sb("rstd", [P, GH, T])
        xpad = sb("xpad", [P, CONV_TILES, NS, P + TAPS - 1])
        xbc = sb("xbc", [P, CONV_TILES, T])
        zs = sb("zs", [P, KT, T])
        yatt = sb("yatt", [P, KT, T])
        qT = sb("qT", [P, KT, T])
        kv = sb("kv", [P, NS, 512])
        xtok = sb("xtok", [P, NS, D])
        btok = sb("btok", [P, 2 * P])
        wide = sb("wide", [P, 6, 2048])
        wdt = sb("wdt", [P, KT, 32])
        wlr = sb("wlr", [P, KT, 32])
        wr = sb("wr", [P, 2, KT, 20])
        br = sb("br", [P, 2, 20])
        dtb = sb("dtb", [P, 32])
        alog = sb("alog", [P, 32])
        dskb = sb("dskb", [P, HEADS])
        dsk = sb("dsk", [P, KT])
        sink = sb("sink", [P, HEADS])
        ckv = sb("ckv", [P, 2, 256])
        wg = sb("wg", [HEADS, 2, 512])
        bg = sb("bg", [1, 2, 512])
        lr = sb("lr", [HEADS, 2 * T])
        tiny = sb("tiny", [P, 1024])
        pref = sb("pref", [P, 4])
        eps = sb("eps", [P, 1])
        ps = ctx.enter_context(nc.psum_tensor("ps", [P, 8, 512], F32))

        zero = rows[:, :, :].rearrange("p a b -> p (a b)")

        def C(n):
            return cst[:, n, :]

        def W(i):
            return wide[:, i, :]

        xpf = xpad[:, :, :, :].rearrange("p a b c -> p (a b c)")
        hTf = hT[:, :, :].rearrange("p k t -> p (k t)")
        xbf = xbc[:, :, :].rearrange("p k t -> p (k t)")
        yaf = yatt[:, :, :].rearrange("p k t -> p (k t)")
        U = xpf[:, 0:2048]
        KTC, KTL, KTP = xpf[:, 0:512], xpf[:, 512:1024], xpf[:, 1024:1536]
        QR, KR = xpf[:, 1536:2560], xpf[:, 2560:3072]
        ATT = xpf[:, 0:1024].rearrange("p (s h t) -> p s h t", s=NS, h=GH)
        ATB = xpf[:, 1024:2048].rearrange("p (s h t) -> p s h t", s=NS, h=GH)
        COMB = wide[:, 0:2, :].rearrange("p a b -> p (a b)").rearrange("p (e t) -> p e t", e=NE)
        SIL = W(4)[:, 0:1024].rearrange("p (f t) -> p f t", f=FT)
        PROD = W(4)[:, 1024:2048].rearrange("p (f t) -> p f t", f=FT)
        HACT = W(5)[:, 0:1024].rearrange("p (f t) -> p f t", f=FT)

        def tk(s):
            return slice(s * P, (s + 1) * P)

        def heads(ap, n=HEADS):
            return ap.rearrange("p (h w) -> p h w", h=n)

        w_in = (A["w_in_even"][0], A["w_in_odd"][0])
        w_out = (A["w_out_even"][0], A["w_out_odd"][0])
        IN = ([1024 + 256 * i for i in range(6)] + [3616, 3872] + [2592 + 256 * i for i in range(4)]
              + [256 * i for i in range(4)],
              [256 * i for i in range(12)])
        n_ada = 6 * D // 256
        n_out = (w_out[0].shape[0] // 256, w_out[1].shape[0] // 256)
        pos, at = {}, 0
        for name, n in (("ada0", n_ada), ("in0", len(IN[0])), ("out0", n_out[0]), ("moe0", NE * PER_EXPERT),
                        ("ada1", n_ada), ("in1", len(IN[1])), ("out1", n_out[1]), ("moe1", NE * PER_EXPERT)):
            pos[name] = at
            at += n

        def slot(n, k):
            return ring[:, n % RING, :].rearrange("p (k n) -> p k n", k=k)

        def wait_landed(pe, n, rounds=0):
            pe.wait_ge(S(f"landed{n % RING}"), rounds * 16 + 16 * (n // RING + 1))

        def stepper(eng, name):
            count = [0]

            def step(ins):
                count[0] += 1
                ins.then_inc(S(name), 1)
                eng.wait_ge(S(name), count[0])
            return step

        def place(i, n):
            return (i % 2) * (n // 2) + i // 2

        def mm(pe, out, lhsT, rhs, first, last, shared=False):
            return pe.matmul(out, lhsT, rhs, start=first, stop=last, skip_group_check=shared)

        block = ctx.enter_context(nc.Block())

        @block.sync
        def _(sp):
            def load(n, src, k, rounds=0):
                sp.dma_start(slot(n, k), src).then_inc(S(f"landed{n % RING}"), 16)

            def wait_free(n, rounds=0):
                sp.wait_ge(S("slot_used"), rounds * RING + (n + 1 - RING))

            def ada(l, c, rounds):
                src = A["w_ada"][l].rearrange("(k p) n -> p k n", p=P)
                return src[:, :, bass.ds(rounds * (RING * 256) + c * 256, 256)]

            for l in range(2):
                base = pos[f"ada{l}"]
                for c in range(RING):
                    if base + c >= RING:
                        wait_free(base + c)
                    load(base + c, ada(l, c, 0), KT)
                with sp.Fori(1, n_ada // RING) as i:
                    for c in range(RING):
                        wait_free(base + c, i)
                        load(base + c, ada(l, c, i), KT)
                for j, c0 in enumerate(IN[l]):
                    wait_free(pos[f"in{l}"] + j)
                    load(pos[f"in{l}"] + j, w_in[l][:, c0:c0 + 256].rearrange("(k p) n -> p k n", p=P), KT)
                for j in range(n_out[l]):
                    wait_free(pos[f"out{l}"] + j)
                    load(pos[f"out{l}"] + j, w_out[l][256 * j:256 * j + 256, :].rearrange("(k p) n -> p k n", p=P), 2)
                base = pos[f"moe{l}"]
                wgu = [A[w][l].rearrange("e (k p) f -> p e k f", p=P) for w in ("w_gate_exp", "w_up_exp")]
                wd = A["w_down_exp"][l].rearrange("e (j k p) d -> p e j k d", p=P, k=2)
                with sp.Fori(0, NE) as e:
                    for c in range(PER_EXPERT):
                        wait_free(base + c, e)
                        if c < 4:
                            src = wgu[c // 2][:, bass.ds(e, 1), :, (c % 2) * 256:(c % 2 + 1) * 256]
                            load(base + c, src.rearrange("p a k f -> p (a k) f"), KT)
                        else:
                            src = wd[:, bass.ds(e, 1), c - 4, :, :]
                            load(base + c, src.rearrange("p a k d -> p (a k) d"), 2)
            for s in range(NS):
                sp.wait_ge(S("y_tok"), 2 * s + 2)
                sp.dma_start(O[s][0], xtok[:, s, :]).then_inc(S("y_stored"), 16)
            sp.wait_ge(S("y_stored"), 32)

        SMALL = 16 * (7 + 8 + 2 + 1 + 4)

        @block.gpsimd
        def _(pool):
            def load(dst, src):
                pool.dma_start(dst, src).then_inc(S("small_in"), 16)

            def spread(src, n):
                return src.rearrange("(a n) -> a n", a=1).broadcast_to([P, n])

            pool.memset(xpf, 0.0).then_inc(S("pad_zero"), 1)
            load(wdt[:, :, :], w_in[0][:, 2560:2592].rearrange("(k p) n -> p k n", p=P))
            load(dtb[:, 0:16], spread(A["dt_bias_fwd"][0], 16))
            load(dtb[:, 16:32], spread(A["dt_bias_bwd"][0], 16))
            load(alog[:, 0:16], spread(A["a_log_fwd"][0], 16))
            load(alog[:, 16:32], spread(A["a_log_bwd"][0], 16))
            load(dskb[:, :], spread(A["d_skip"][0], 16))
            load(sink[:, :], spread(A["attn_sink"][0], 16))
            for l in range(2):
                load(wr[:, l, :, 0:4], A["w_router_group"][l].rearrange("(k p) n -> p k n", p=P))
                load(wr[:, l, :, 4:20], A["w_router_expert"][l].rearrange("(k p) n -> p k n", p=P))
                load(br[:, l, 0:4], spread(A["b_router_group"][l], 4))
                load(br[:, l, 4:20], spread(A["b_router_expert"][l], 16))
            load(ckv[:, 0, :], A["cache_k_attn"][0, 0].rearrange("t h d -> t (h d)"))
            load(ckv[:, 1, :], A["cache_v_attn"][0, 0].rearrange("t h d -> t (h d)"))
            load(wlr[:, :, :], w_in[1][:, 3072:3104].rearrange("(k p) n -> p k n", p=P))
            load(wg[0:16, 0, :], A["w_gk2_fwd"][0])
            load(wg[0:16, 1, :], A["w_gk2_bwd"][0])
            load(bg[0:1, 0, :], A["b_gk_fwd"])
            load(bg[0:1, 1, :], A["b_gk_bwd"])
            pool.wait_ge(S("proj_free"), 8)
            pool.wait_ge(S("small_in"), SMALL)
            for n, keys in enumerate((kv[:, 0, 0:256], kv[:, 1, 0:256], ckv[:, 0, :])):
                pool.tensor_copy(W(5)[:, n * 512:(n + 1) * 512].rearrange("p (j a d) -> p j a d", j=KVH, a=2),
                                 keys.rearrange("p (j d) -> p j d", j=KVH)[:, :, None, :].broadcast_to([P, KVH, 2, 64])).then_inc(S("keys_twice"), 1)
            after = (0, 4, 8, 16)
            pool.wait_ge(S("dtA"), 1)
            pool.wait_ge(S("conv_done"), CONV_TILES)
            pool.wait_ge(S("consts_in"), 16)
            for n in range(4):
                if n:
                    pool.wait_ge(S("seg_raw"), after[n])
                a0 = DTA + 16 * n
                pool.tensor_tensor(heads(U), C(GE if n % 2 else LE)[:, None, :].broadcast_to([P, HEADS, P]),
                                   tiny[:, a0:a0 + 16][:, :, None].broadcast_to([P, HEADS, P]),
                                   ALU.mult).then_inc(S("U_ready"), 1)

        @block.tensor
        def _(pe):
            def used(ins):
                ins.then_inc(S("slot_used"), 1)

            def turn(out, in_, n=P):
                return pe.transpose(out, in_, cst[0:n, IDENT, 0:n])

            pe.wait_ge(S("consts_in"), 16)
            pe.wait_ge(S("rows_in"), 160)
            turn(ps[:, 0, 0:P], rows[:, 0, :])
            turn(ps[:, 0, P:P + 106], rows[0:106, 1, :], 106).then_inc(S("rows_turned"), 1)
            pe.wait_ge(S("x_in"), 32)
            for g in range(4):
                for k in range(4):
                    last = turn(ps[:, 1 + g, k * P:(k + 1) * P], xtok[:, g // 2, ((g % 2) * 4 + k) * P:((g % 2) * 4 + k + 1) * P])
                last.then_inc(S("x_turned"), 1)

            def ada(l):
                if l == 0:
                    pe.wait_ge(S("csilu"), 2)
                with pe.Fori(0, n_ada // RING) as i:
                    for c in range(RING):
                        n = pos[f"ada{l}"] + c
                        wait_landed(pe, n, i)
                        for m in range(2):
                            for k in range(KT):
                                last = mm(pe, ps[:, 7, bass.ds(i * (4 * RING) + (4 * c + 2 * m), 2)],
                                          slot(n, KT)[:, k, m * P:(m + 1) * P], csilu[:, k, :], k == 0, k == KT - 1)
                        used(last)

            def norm(i):
                pe.wait_ge(S("sq"), i + 1)
                for k in range(KT):
                    last = mm(pe, ps[:, 0, 0:T], C(MEAN_D), hT[:, k, :], k == 0, k == KT - 1)
                last.then_inc(S("ss"), 1)

            def project(n, b, by_token):
                wait_landed(pe, n)
                for m in range(2):
                    for k in range(KT):
                        if by_token:
                            last = mm(pe, ps[:, b, m * T:(m + 1) * T], hT[:, k, tk(m)], slot(n, KT)[:, k, :], k == 0, k == KT - 1)
                        else:
                            last = mm(pe, ps[:, b, m * T:(m + 1) * T], slot(n, KT)[:, k, m * P:(m + 1) * P], hT[:, k, :], k == 0, k == KT - 1)
                used(last)

            def projections(l):
                done = 0 if l == 0 else len(IN[0])
                for j in range(len(IN[l])):
                    if done + j >= 4:
                        pe.wait_ge(S("proj_free"), done + j - 3)
                    project(pos[f"in{l}"] + j, 1 + j % 4, j in ((6, 7) if l == 0 else range(2, 8)))

            def out_project(l, src):
                for c in range(n_out[l]):
                    n = pos[f"out{l}"] + c
                    wait_landed(pe, n)
                    for k in range(2):
                        t = 2 * c + k
                        for m in range(KT):
                            last = mm(pe, ps[:, 4 + m // 2, (m % 2) * T:(m % 2 + 1) * T], slot(n, 2)[:, k, m * P:(m + 1) * P],
                                      src(t), t == 0 and m % 2 == 0, t == 2 * n_out[l] - 1, shared=True)
                    used(last)

            def even():
                pe.wait_ge(S("h_ready"), 1)
                pe.wait_ge(S("small_in"), SMALL)
                for s in range(NS):
                    for k in range(KT):
                        last = mm(pe, ps[:, 0, T + 32 * s:T + 32 * s + 32], hT[:, k, tk(s)], wdt[:, k, :], k == 0, k == KT - 1)
                last.then_inc(S("dt_raw"), 1)
                projections(0)
                for g in range(5):
                    pe.wait_ge(S("xbc_ready"), (2 + 2 * (g % 2)) if g < 4 else 5)
                    if g >= 3:
                        pe.wait_ge(S("tok_copied"), g - 2)
                    for k in range(4 if g < 4 else 2):
                        in_ = xbc[:, (g % 2) * 4 + k, tk(g // 2)] if g < 4 else xbc[:, 8 + k, tk(0)]
                        last = turn(ps[:, 5 + g % 3, k * P:(k + 1) * P], in_)
                    last.then_inc(S("tok_turned"), 1)
                pe.wait_ge(S("h0_in"), 32)
                pe.wait_ge(S("proj_free"), 16)
                for g in range(4):
                    for k in range(4):
                        last = turn(ps[:, 1 + g, k * P:(k + 1) * P], W(2)[:, (4 * g + k) * P:(4 * g + k + 1) * P])
                    last.then_inc(S("h0_turned"), 1)
                pe.wait_ge(S("dtA"), 1)
                pe.wait_ge(S("tok_copied"), 5)
                for d in range(2):
                    last = mm(pe, ps[:, 7, 256 + 16 * d:272 + 16 * d], C(LT if d else GT), tiny[:, DTA + 16 * d:DTA + 16 * d + 16], True, True)
                last.then_inc(S("te_raw"), 1)
                unit = 0
                for s in range(NS):
                    pe.wait_ge(S("xbc_ready"), 6)
                    if s:
                        pe.wait_ge(S("cbm"), 1)
                    for g in range(2):
                        last = mm(pe, ps[:, 0, g * P:(g + 1) * P], xbc[:, 8 + g, tk(s)], xbc[:, 10 + g, tk(s)], True, True)
                    last.then_inc(S("cb_raw"), 1)
                    for d in range(2):
                        pe.wait_ge(S("U_ready"), 2 * s + d + 1)
                        for w in range(1 + s):
                            for q in range(4):
                                if unit < 4:
                                    pe.wait_ge(S("h0_copied"), unit + 1)
                                elif unit < 8 or unit >= 12:
                                    pe.wait_ge(S("seg_exp"), unit - 3)
                                else:
                                    pe.wait_ge(S("st_copied"), q + 1)
                                mm(pe, ps[:, 1 + unit % 4, :], C(ONES) if w else C(LT if d else GT),
                                   U[:, q * 512:(q + 1) * 512], True, True).then_inc(S("seg_raw"), 1)
                                unit += 1
                    if s == 0:
                        pe.wait_ge(S("xw_ready"), 1)
                        pe.wait_ge(S("tok_copied"), 5)
                        pe.wait_ge(S("seg_exp"), 8)
                        for i in range(16):
                            g = (i % 8) // 4
                            last = mm(pe, ps[:, 1 + i // 4, (i % 4) * P:(i % 4 + 1) * P], W(3)[:, i * P:(i + 1) * P],
                                      btok[:, g * P:(g + 1) * P], True, True)
                            if i % 4 == 3:
                                last.then_inc(S("st_raw"), 1)
                    pe.wait_ge(S("M_ready"), s + 1)
                    if s:
                        pe.wait_ge(S("y_gated"), 1)
                    for h in range(HEADS):
                        out = ps[64 * (h % 2):64 * (h % 2) + 64, 5 + h // 8, (h // 2 % 4) * P:(h // 2 % 4 + 1) * P]
                        terms = [(W(4)[:, d * D + h * HP:d * D + (h + 1) * HP], W(d)[:, h * P:(h + 1) * P]) for d in range(2)]
                        if s:
                            terms += [(hTf[:, d * D + h * HP:d * D + (h + 1) * HP], W(2 + d)[:, h * P:(h + 1) * P]) for d in range(2)]
                        for n, (a, b) in enumerate(terms):
                            last = mm(pe, out, a, b, n == 0, n == len(terms) - 1)
                    last.then_inc(S("y_raw"), 1)
                pe.wait_ge(S("ysq"), 1)
                for k in range(KT):
                    last = mm(pe, ps[:, 0, 0:T], C(MEAN_D), W(4)[:, k * T:(k + 1) * T], k == 0, k == KT - 1)
                last.then_inc(S("yss"), 1)

                pe.wait_ge(S("seg_exp"), 24)
                pe.wait_ge(S("keys_twice"), 3)
                for n in range(3):
                    for j in range(KVH):
                        last = turn(ps[:, 1 + n, j * P:(j + 1) * P], W(5)[:, (4 * n + j) * P:(4 * n + j + 1) * P])
                    last.then_inc(S("keys_turned"), 1)
                pe.wait_ge(S("keys_copied"), 2)
                pe.wait_ge(S("y_gated"), 2)
                mm(pe, ps[:, 4, :], C(ROT), KTL, True, True)
                for b in range(2):
                    last = mm(pe, ps[:, 5 + b, :], C(ROT), qT[:, 4 * b:4 * b + 4, tk(1)], True, True)
                last.then_inc(S("rotated"), 1)
                pe.wait_ge(S("keys_copied"), 3)
                pe.wait_ge(S("rope"), 1)
                pe.wait_ge(S("yssd"), 1)
                for g in range(3):
                    if g:
                        pe.wait_ge(S("yatt"), g + 1)
                    nh = 8 if g else 16
                    for i in range(nh):
                        h = 8 * (g - 1) + i if g else i
                        b, j = 64 * (h % 2), (h // 4) * P
                        i = place(i, nh)
                        if g == 0:
                            last = mm(pe, ps[:, i // 4, (i % 4) * P:(i % 4 + 1) * P], qT[b:b + 64, h // 2, tk(0)], KTC[b:b + 64, j:j + P], True, True)
                        else:
                            mm(pe, ps[:, i // 2, (i % 2) * T:(i % 2) * T + P], qT[b:b + 64, h // 2, tk(1)], KTP[b:b + 64, j:j + P], True, True)
                            last = mm(pe, ps[:, i // 2, (i % 2) * T + P:(i % 2) * T + T], QR[b:b + 64, (h // 2) * P:(h // 2 + 1) * P], KR[b:b + 64, j:j + P], True, True)
                    last.then_inc(S("scores"), 1)
                    pe.wait_ge(S("probs"), g + 1)
                    if g:
                        pe.wait_ge(S("pT_copied"), 4 * g)
                    for i in range(16):
                        last = turn(ps[:, 4 + i // 4, (i % 4) * P:(i % 4 + 1) * P], W(0)[:, i * P:(i + 1) * P])
                    last.then_inc(S("probs_turned"), 1)
                    pe.wait_ge(S("pT_copied"), 4 * (g + 1))
                    for i in range(nh):
                        h = 8 * (g - 1) + i if g else i
                        v0 = (h // 4) * 64
                        out = ps[64 * (h % 2):64 * (h % 2) + 64, (i // 8) if g == 0 else 0, (h // 2 % 4) * P:(h // 2 % 4 + 1) * P]
                        i = place(i, nh)
                        if g == 0:
                            last = mm(pe, out, kv[:, 0, 256 + v0:320 + v0], W(1)[:, i * P:(i + 1) * P], True, True)
                        else:
                            mm(pe, out, ckv[:, 1, v0:v0 + 64], W(1)[:, 2 * i * P:(2 * i + 1) * P], True, False)
                            last = mm(pe, out, kv[:, 1, 256 + v0:320 + v0], W(1)[:, (2 * i + 1) * P:(2 * i + 2) * P], False, True)
                    last.then_inc(S("att_raw"), 1)
                pe.wait_ge(S("yatt"), 4)
                out_project(0, lambda t: zs[:, t, :] if t < KT else yatt[:, t - KT, :])

            def odd():
                pe.wait_ge(S("h_ready"), 3)
                for d in range(2):
                    for k in range(KT):
                        last = mm(pe, ps[0:16, 0, d * T:(d + 1) * T], wlr[:, k, 16 * d:16 * d + 16], hT[:, k, :], k == 0, k == KT - 1)
                last.then_inc(S("lr_raw"), 1)
                projections(1)
                pe.wait_ge(S("proj_free"), 16 + 4)
                for s in range(NS):
                    for h in range(GH):
                        last = turn(ps[:, 5 + s, h * P:(h + 1) * P], kv[:, s, h * P:(h + 1) * P])
                    last.then_inc(S("gk_turned"), 1)
                pe.wait_ge(S("gk_copied"), 2)
                pe.wait_ge(S("lr"), 1)
                for c in range(4):
                    b, d = (5 + c) % 8, c % 2
                    mm(pe, ps[:, b, :], lr[:, d * T + (c // 2) * P:d * T + (c // 2 + 1) * P], wg[0:16, d, :], True, False)
                    mm(pe, ps[:, b, :], cst[0:1, ONES, :], bg[0:1, d, :], False, True).then_inc(S("gate_raw"), 1)
                pe.wait_ge(S("proj_free"), 28)
                pe.wait_ge(S("g_ready"), 4)
                for c in range(4):
                    for h in range(GH):
                        last = mm(pe, ps[:, c, h * P:(h + 1) * P], W(0)[:, c * 512 + h * P:c * 512 + (h + 1) * P], C(BGE if c % 2 else BLE), True, True)
                    last.then_inc(S("cs_raw"), 1)
                for c in range(4):
                    mm(pe, ps[:, 4 + c, :], C(BLT if c % 2 else BGT), W(0)[:, c * 512:(c + 1) * 512], True, True).then_inc(S("rest_raw"), 1)
                pe.wait_ge(S("ecs"), 8)
                pe.wait_ge(S("qk_ready"), 4)
                for c in range(4):
                    for h in range(GH):
                        for ch in range(2):
                            r, o = c * 512 + h * P + CH * ch, h * P + CH * ch
                            last = mm(pe, ps[CH * ch:CH * ch + CH, c, o:o + CH], W(4)[:, r:r + CH], W(3)[:, r:r + CH], True, True)
                    last.then_inc(S("gatt_raw"), 1)
                pe.wait_ge(S("kdec"), 4)
                for n, (s, d, ch) in enumerate(COMBOS):
                    if n >= 2:
                        pe.wait_ge(S("state"), n - 1)
                    for h in range(GH):
                        r = (2 * s + d) * 512 + h * P
                        last = mm(pe, ps[:, 4 + 2 * (n % 2) + h // 2, (h % 2) * T:(h % 2 + 1) * T], W(0)[CH * ch:CH * ch + CH, r:r + P],
                                  xtok[CH * ch:CH * ch + CH, s, h * GV:(h + 1) * GV], True, True)
                    last.then_inc(S("kv_raw"), 1)
                pe.wait_ge(S("gatt"), 2)
                pe.wait_ge(S("state"), 6)
                for s in range(NS):
                    for h in range(GH):
                        for v in range(2):
                            i = 2 * h + v
                            b, o = 2 * s + i // 4, (i % 4) * P
                            terms = [(xtok[:, s, h * GV + v * P:h * GV + (v + 1) * P], ATT[:, s, h, :], 0, P)]
                            for d in range(2):
                                for ch in range(2):
                                    q = W(3)[:, (2 * s + d) * 512 + h * P + CH * ch:(2 * s + d) * 512 + h * P + CH * ch + CH]
                                    so = d * D + h * GV + v * P
                                    if ch != d:
                                        st = (W(2) if s == 0 else xbf)[:, so:so + P]
                                    elif s:
                                        st = W(5)[:, so:so + P]
                                    else:
                                        continue
                                    terms.append((st, q, CH * ch, CH))
                            for n, (a, q, c0, w) in enumerate(terms):
                                last = mm(pe, ps[:, b, o + c0:o + c0 + w], a, q, n == 0, n == len(terms) - 1, shared=True)
                    last.then_inc(S("gy_raw"), 1)
                pe.wait_ge(S("gsq"), 1)
                for h in range(GH):
                    for v in range(2):
                        last = mm(pe, ps[:, 4 + h // 2, (h % 2) * T:(h % 2 + 1) * T], C(MEAN_V), W(3)[:, (2 * h + v) * T:(2 * h + v + 1) * T], v == 0, v == 1)
                last.then_inc(S("gss"), 1)
                pe.wait_ge(S("gyn"), 1)
                out_project(1, lambda t: yatt[:, t, :])

            def moe(l):
                pe.wait_ge(S("h_ready"), 2 * l + 2)
                for s in range(NS):
                    for k in range(KT):
                        last = mm(pe, ps[:, 0, T + 32 * s:T + 32 * s + 20], hT[:, k, tk(s)], wr[:, l, k, :], k == 0, k == KT - 1)
                last.then_inc(S("logits"), 1)
                pe.wait_ge(S("zeroed"), 1)
                for b in range(8):
                    mm(pe, ps[:, 4 + b // 2, (b % 2) * T:(b % 2 + 1) * T], C(IDENT), zero, b % 2 == 0, True, shared=True)
                pe.wait_ge(S("cmb_diag"), 2 * (l + 1))
                for q in range(8):
                    if q >= 4:
                        pe.wait_ge(S("comb"), 8 * l + q - 3)
                    mm(pe, ps[:, q % 4, :], C(ONES), W(2 + q // 4)[:, (q % 4) * 512:(q % 4 + 1) * 512], True, True).then_inc(S("comb_raw"), 1)
                pe.wait_ge(S("comb"), 8 * l + 8)
                base = pos[f"moe{l}"]
                with pe.Fori(0, NE) as e:
                    for c in range(4):
                        wait_landed(pe, base + c, e)
                        for m in range(2):
                            f = 2 * (c % 2) + m
                            for k in range(KT):
                                last = mm(pe, ps[:, f, (c // 2) * T:(c // 2 + 1) * T], slot(base + c, KT)[:, k, m * P:(m + 1) * P], hT[:, k, :], k == 0, k == KT - 1)
                        used(last)
                    for c in range(2):
                        wait_landed(pe, base + 4 + c, e)
                        for k in range(2):
                            f = 2 * c + k
                            pe.wait_ge(S("hact"), e * FT + (l * NE * FT + f + 1))
                            for m in range(KT):
                                last = mm(pe, ps[:, 4 + m // 2, (m % 2) * T:(m % 2 + 1) * T], slot(base + 4 + c, 2)[:, k, m * P:(m + 1) * P],
                                          HACT[:, f, :], False, False, shared=True)
                        used(last)

            ada(0)
            norm(0)
            even()
            norm(1)
            moe(0)
            pe.wait_ge(S("x_ready"), 3)
            ada(1)
            norm(2)
            odd()
            norm(3)
            moe(1)
            norm(4)
            pe.wait_ge(S("h_ready"), 5)
            for g in range(4):
                for k in range(4):
                    last = turn(ps[:, 1 + g, k * P:(k + 1) * P], hT[:, (g % 2) * 4 + k, tk(g // 2)])
                last.then_inc(S("y_turned"), 1)

        @block.scalar
        def _(act):
            def load(dst, src, name):
                act.dma_start(dst, src).then_inc(S(name), 16)

            load(cst[:, :, :], A["consts"], "consts_in")
            for lo, src in ((BADA, A["b_ada"].rearrange("l (r p) -> (l r) p", p=P)),
                            (NMIX, A["norm_mix_w"].rearrange("l (r p) -> (l r) p", p=P)),
                            (NFFN, A["norm_ffn_w"].rearrange("l (r p) -> (l r) p", p=P)),
                            (CONVW, A["conv_w"][0].rearrange("t (r p) -> (t r) p", p=P)),
                            (CONVB, A["conv_b"][0].rearrange("(r p) -> r p", p=P)),
                            (SSDN, A["ssd_norm_w"][0].rearrange("(r p) -> r p", p=P)),
                            (GLAN, A["gla_norm_w"][0].rearrange("(r p) -> r p", p=P)),
                            (FINN, A["final_norm_w"].rearrange("(r p) -> r p", p=P)),
                            (CVEC, A["c"][0].rearrange("(r p) -> r p", p=P)),
                            (CCTX, A["c_ctx"].rearrange("(r p) -> r p", p=P))):
                load(rows[lo % P:lo % P + src.shape[0], lo // P, :], src, "rows_in")
            load(xtok[:, 0, :], A["x_prompt"][0], "x_in")
            load(xtok[:, 1, :], A["x_sample"][0], "x_in")
            for d, name in enumerate(("state_ssd_fwd", "state_ssd_bwd")):
                load(W(2)[:, d * D:(d + 1) * D].rearrange("p (i n) -> p i n", i=8),
                     A[name][0, 0].rearrange("(i a) q n -> (a q) i n", a=2), "h0_in")
            act.wait_ge(S("feat_ready"), 1)
            act.activation(csilu[:, :, 0], feat[:, CCTX:CCTX + KT], ACT.Silu).then_inc(S("csilu"), 1)
            act.activation(csilu[:, :, 1], feat[:, CVEC:CVEC + KT], ACT.Silu).then_inc(S("csilu"), 1)

            def norm(i):
                act.wait_ge(S("x_ready"), i + 1)
                if i == 3:
                    act.wait_ge(S("gla_stored"), 32)
                act.activation(hT[:, :, :], xT[:, :, :], ACT.Square).then_inc(S("sq"), 1)
                act.wait_ge(S("eps"), 1)
                act.wait_ge(S("ss"), i + 1)
                act.activation(rstd[:, 0, :], ps[:, 0, 0:T], ACT.Sqrt, bias=eps[:, :]).then_inc(S("rms"), 1)

            def even():
                act.wait_ge(S("dt_abs"), 1)
                act.activation(tiny[:, DTE:DTE + 64], tiny[:, DTT:DTT + 64], ACT.Exp, scale=-1.0).then_inc(S("dt_exp"), 1)
                act.activation(alog[:, :], alog[:, :], ACT.Exp).then_inc(S("dt_exp"), 1)
                act.wait_ge(S("dt_u"), 1)
                act.activation(tiny[:, DTL:DTL + 64], tiny[:, DTU:DTU + 64], ACT.Ln).then_inc(S("dt_ln"), 1)
                for j in range(16):
                    act.wait_ge(S("slot_used"), pos["in0"] + j + 1)
                    b = ps[:, 1 + j % 4, :]
                    b2 = b.rearrange("p (a t) -> p a t", a=2)
                    if j == 0:
                        act.wait_ge(S("pad_zero"), 1)
                    dst, src, f = ((xpad[:, 2 * j:2 * j + 2, :, 2:2 + P], b.rearrange("p (a s t) -> p a s t", a=2, s=NS), ACT.Copy) if j < 6 else
                                   (kv[:, :, (j - 6) * 256:(j - 5) * 256], b2, ACT.Copy) if j < 8 else
                                   (qT[:, 2 * (j - 8):2 * (j - 8) + 2, :], b2, ACT.Copy) if j < 12 else
                                   (zs[:, 2 * (j - 12):2 * (j - 12) + 2, :], b2, ACT.Silu))
                    act.activation(dst, src, f).then_inc(S("proj_free"), 1)
                    if 6 <= j < 12:
                        p = 2 * (j - 6)
                        act.wait_ge(S("conv_done"), p + 2)
                        act.activation(xbc[:, p:p + 2, :], xbc[:, p:p + 2, :], ACT.Silu).then_inc(S("xbc_ready"), 1)
                    if j == 7:
                        act.wait_ge(S("proj_free"), 8)
                        act.dma_start(O[2][0, 0].rearrange("t h d -> t (h d)"), kv[:, 0, 0:256]).then_inc(S("cache_stored"), 16)
                        act.dma_start(O[3][0, 0].rearrange("t h d -> t (h d)"), kv[:, 0, 256:512]).then_inc(S("cache_stored"), 16)
                for g in range(5):
                    act.wait_ge(S("tok_turned"), g + 1)
                    dst = xtok[:, g // 2, (g % 2) * 512:(g % 2 + 1) * 512] if g < 4 else btok[:, :]
                    act.activation(dst, ps[:, 5 + g % 3, 0:512 if g < 4 else 256], ACT.Copy).then_inc(S("tok_copied"), 1)
                for g in range(4):
                    act.wait_ge(S("h0_turned"), g + 1)
                    act.activation(hTf[:, g * 512:(g + 1) * 512], ps[:, 1 + g, :], ACT.Copy).then_inc(S("h0_copied"), 1)
                act.wait_ge(S("te_raw"), 1)
                act.activation(tiny[:, TE:TE + 32], ps[:, 7, 256:288], ACT.Exp).then_inc(S("te_exp"), 1)
                unit = 0
                for s in range(NS):
                    if s:
                        act.wait_ge(S("y_raw"), 1)
                    for d in range(2):
                        for w in range(1 + s):
                            for q in range(4):
                                act.wait_ge(S("seg_raw"), unit + 1)
                                act.activation(W(2 * w + d)[:, q * 512:(q + 1) * 512], ps[:, 1 + unit % 4, :], ACT.Exp).then_inc(S("seg_exp"), 1)
                                unit += 1
                    if s == 0:
                        for q in range(4):
                            act.wait_ge(S("st_raw"), q + 1)
                            act.activation(yaf[:, q * 512:(q + 1) * 512], ps[:, 1 + q, :], ACT.Copy).then_inc(S("st_copied"), 1)
                        act.wait_ge(S("st_copied"), 4)
                        for d in range(2):
                            act.dma_start(O[4 + d][0, 0].rearrange("(i a) q n -> (a q) i n", a=2),
                                          yaf[:, d * D:(d + 1) * D].rearrange("p (i n) -> p i n", i=8)).then_inc(S("ssd_stored"), 16)
                act.wait_ge(S("y_gated"), 2)
                act.activation(W(4), zs[:, :, :].rearrange("p k t -> p (k t)"), ACT.Square).then_inc(S("ysq"), 1)
                act.wait_ge(S("yss"), 1)
                act.activation(rstd[:, 1, :], ps[:, 0, 0:T], ACT.Sqrt, bias=eps[:, :]).then_inc(S("yrms"), 1)
                for n, dst in enumerate((KTC, KTL, KTP)):
                    act.wait_ge(S("keys_turned"), n + 1)
                    act.activation(dst, ps[:, 1 + n, :], ACT.Copy).then_inc(S("keys_copied"), 1)
                for g in range(3):
                    nh, w = (8, 256) if g else (16, 128)
                    act.wait_ge(S("negm"), g + 1)
                    sc = ps[:, 0:4, :].rearrange("p b (h w) -> p (b h) w", w=w)
                    pr = W(0).rearrange("p (h w) -> p h w", w=w)
                    if g:
                        act.wait_ge(S("probs_turned"), g)
                    for h in range(nh):
                        act.activation(pr[:, h, :], sc[:, h, :], ACT.Exp, scale=SCALE, bias=tiny[:, NEGM + h:NEGM + h + 1],
                                       accum_out=tiny[:, RSUM + h:RSUM + h + 1]).then_inc(S("p_exp"), 1)
                    act.activation(tiny[:, SNKE:SNKE + nh], tiny[:, SNKD:SNKD + nh], ACT.Exp).then_inc(S("p_exp"), 1)
                    act.wait_ge(S("probs_turned"), g + 1)
                    if g:
                        act.wait_ge(S("att_raw"), g)
                    for q in range(4):
                        act.activation(W(1)[:, q * 512:(q + 1) * 512], ps[:, 4 + q, :], ACT.Copy).then_inc(S("pT_copied"), 1)
                    act.wait_ge(S("att_raw"), g + 1)
                    if g == 0:
                        act.wait_ge(S("ssd_stored"), 32)
                        for b in range(2):
                            act.activation(yatt[:, 4 * b:4 * b + 4, tk(0)], ps[:, b, :].rearrange("p (a t) -> p a t", a=4), ACT.Copy).then_inc(S("yatt"), 1)
                    else:
                        act.activation(yatt[:, 4 * (g - 1):4 * g, tk(1)], ps[:, 0, :].rearrange("p (a t) -> p a t", a=4), ACT.Copy).then_inc(S("yatt"), 1)

            def odd():
                for d, name in enumerate(("state_gla_fwd", "state_gla_bwd")):
                    load(W(5)[:, d * D:(d + 1) * D].rearrange("p (h v) -> p h v", h=GH),
                         A[name][0, 0].rearrange("h k v -> k h v"), "s0_in")
                act.wait_ge(S("lr_raw"), 1)
                act.activation(lr[:, :], ps[0:16, 0, :], ACT.Copy).then_inc(S("lr"), 1)
                for j in range(12):
                    act.wait_ge(S("slot_used"), pos["in1"] + j + 1)
                    b2 = ps[:, 1 + j % 4, :].rearrange("p (a t) -> p a t", a=2)
                    dst, f = ((qT[:, 2 * j:2 * j + 2, :], ACT.Copy) if j < 2 else
                              (kv[:, :, (j - 2) * 256:(j - 1) * 256], ACT.Copy) if j < 4 else
                              (xtok[:, :, (j - 4) * 256:(j - 3) * 256], ACT.Copy) if j < 8 else
                              (zs[:, 2 * (j - 8):2 * (j - 8) + 2, :], ACT.Silu))
                    act.activation(dst, b2, f).then_inc(S("proj_free"), 1)
                act.wait_ge(S("gate_abs"), 4)
                act.activation(W(1), W(1), ACT.Exp, scale=-1.0).then_inc(S("gate_exp"), 1)
                act.wait_ge(S("gate_exp"), 1)
                act.activation(W(1), W(1), ACT.Ln, bias=1.0).then_inc(S("gate_exp"), 1)
                act.wait_ge(S("g_ready"), 4)
                for c in range(4):
                    act.wait_ge(S("cs_raw"), c + 1)
                    act.activation(W(1)[:, c * 512:(c + 1) * 512], ps[:, c, :], ACT.Exp).then_inc(S("ecs"), 1)
                    act.activation(W(2)[:, c * 512:(c + 1) * 512], ps[:, c, :], ACT.Exp, scale=-1.0).then_inc(S("ecs"), 1)
                act.wait_ge(S("rest_raw"), 4)
                for c in range(4):
                    act.activation(W(0)[:, c * 512:(c + 1) * 512], ps[:, 4 + c, :], ACT.Exp).then_inc(S("kde"), 1)
                act.wait_ge(S("state"), 4)
                for d in range(2):
                    act.dma_start(O[6 + d][0, 0].rearrange("h k v -> k h v"),
                                  hTf[:, d * D:(d + 1) * D].rearrange("p (h v) -> p h v", h=GH)).then_inc(S("gla_stored"), 16)
                act.wait_ge(S("gy"), 2)
                act.activation(W(3), yaf, ACT.Square).then_inc(S("gsq"), 1)
                act.wait_ge(S("gss"), 1)
                act.activation(rstd[:, :, :].rearrange("p (b h) t -> p b (h t)", b=2), ps[:, 4:6, :], ACT.Sqrt, bias=eps[:, :]).then_inc(S("grms"), 1)

            def moe(l):
                act.wait_ge(S("g_sub"), l + 1)
                act.activation(tiny[:, GEX:GEX + 8], tiny[:, GEX:GEX + 8], ACT.Exp).then_inc(S("g_exp"), 1)
                act.wait_ge(S("e_sub"), l + 1)
                act.activation(tiny[:, EL:EL + 8], tiny[:, EL:EL + 8], ACT.Exp).then_inc(S("e_exp"), 1)
                for q in range(8):
                    act.wait_ge(S("comb_raw"), 8 * l + q + 1)
                    s, e4 = q // 4, q % 4
                    act.activation(COMB[:, 4 * e4:4 * e4 + 4, tk(s)], ps[:, e4, :].rearrange("p (e t) -> p e t", e=4),
                                   ACT.Copy).then_inc(S("comb"), 1)
                with act.Fori(0, NE) as e:
                    for f in range(FT):
                        act.wait_ge(S("slot_used"), e * RING + (pos[f"moe{l}"] + 3 + f // 2))
                        act.activation(SIL[:, f, :], ps[:, f, 0:T], ACT.Silu).then_inc(S("sil"), 1)

            norm(0)
            even()
            norm(1)
            moe(0)
            norm(2)
            odd()
            norm(3)
            moe(1)
            norm(4)
            for g in range(4):
                act.wait_ge(S("y_turned"), g + 1)
                act.activation(xtok[:, g // 2, (g % 2) * 512:(g % 2 + 1) * 512], ps[:, 1 + g, :], ACT.Copy).then_inc(S("y_tok"), 1)
            act.wait_ge(S("cache_stored"), 32)

        @block.vector
        def _(dve):
            step = stepper(dve, "dve_step")
            tt, ts, stt = dve.tensor_tensor, dve.tensor_scalar, dve.scalar_tensor_tensor

            def t2(c, n, s=NS):
                return tiny[:, c:c + s * n].rearrange("p (s n) -> p s n", s=s)

            dve.memset(eps[:, :], EPS).then_inc(S("eps"), 1)
            for i in range(4):
                dve.memset(pref[:, i:i + 1], float(4 - i)).then_inc(S("pref"), 1)
            dve.wait_ge(S("rows_turned"), 1)
            dve.memset(zero, 0.0).then_inc(S("zeroed"), 1)
            dve.tensor_copy(feat[:, 0:234], ps[:, 0, 0:234]).then_inc(S("feat_ready"), 1)
            for g in range(4):
                dve.wait_ge(S("x_turned"), g + 1)
                step(dve.tensor_copy(xT[:, (g % 2) * 4:(g % 2) * 4 + 4, tk(g // 2)], ps[:, 1 + g, :].rearrange("p (k t) -> p k t", k=4)))
            dve.wait_ge(S("small_in"), SMALL)
            step(dve.tensor_copy(dsk[0:64, :], dskb[0:64, :].rearrange("p (i a) -> p a i", a=2)[:, 0, :]))
            dve.tensor_copy(dsk[64:128, :], dskb[64:128, :].rearrange("p (i a) -> p a i", a=2)[:, 1, :]).then_inc(S("x_ready"), 1)
            dve.wait_ge(S("x_ready"), 1)

            def ada(l):
                dve.wait_ge(S("slot_used"), pos[f"ada{l}"] + n_ada)
                b = BADA + 48 * l
                step(tt(mods[:, l], ps[:, 7, 0:96].rearrange("p (r s) -> p r s", s=NS),
                        feat[:, b:b + 48][:, :, None].broadcast_to([P, 48, NS]), ALU.add))
                for c, w in ((8, NMIX), (32, NFFN)):
                    step(stt(mods[:, l, c:c + 8], mods[:, l, c:c + 8], 1.0,
                             feat[:, w + 8 * l:w + 8 * l + 8][:, :, None].broadcast_to([P, 8, NS]), ALU.add, ALU.mult))

            def norm(i):
                dve.wait_ge(S("rms"), i + 1)
                step(dve.reciprocal(rstd[:, 0, :], rstd[:, 0, :]))
                step(tt(hT[:, :, :], xT[:, :, :], rstd[:, 0:1, :].broadcast_to([P, KT, T]), ALU.mult))
                if i == 4:
                    for k in range(KT):
                        last = ts(hT[:, k, :], hT[:, k, :], feat[:, FINN + k:FINN + k + 1], None, ALU.mult)
                        if k < KT - 1:
                            step(last)
                else:
                    l, c = i // 2, 24 * (i % 2)
                    for k in range(KT):
                        for s in range(NS):
                            last = ts(hT[:, k, tk(s)], hT[:, k, tk(s)], mods[:, l, c + 8 + k, s:s + 1], mods[:, l, c + k, s:s + 1], ALU.mult, ALU.add)
                            if (k, s) != (KT - 1, 1):
                                step(last)
                last.then_inc(S("h_ready"), 1)
                dve.wait_ge(S("h_ready"), i + 1)

            def residual(l, c, count):
                for k in range(KT):
                    for s in range(NS):
                        last = stt(xT[:, k, tk(s)], ps[:, 4 + k // 2, (k % 2) * T + s * P:(k % 2) * T + (s + 1) * P],
                                   mods[:, l, c + k, s:s + 1], xT[:, k, tk(s)], ALU.mult, ALU.add)
                        if (k, s) != (KT - 1, 1):
                            step(last)
                last.then_inc(S("x_ready"), 1)
                dve.wait_ge(S("x_ready"), count)

            def even():
                dve.wait_ge(S("dt_raw"), 1)
                X, TM, EX, U1, LN = (tiny[:, c:c + 64] for c in (DTX, DTT, DTE, DTU, DTL))
                step(tt(t2(DTX, 32), ps[:, 0, T:T + 64].rearrange("p (s n) -> p s n", s=NS), dtb[:, None, :].broadcast_to([P, NS, 32]), ALU.add))
                stt(TM, X, -1.0, X, ALU.mult, ALU.max).then_inc(S("dt_abs"), 1)
                dve.wait_ge(S("dt_exp"), 2)
                ts(U1, EX, 1.0, None, ALU.add).then_inc(S("dt_u"), 1)
                dve.wait_ge(S("dt_u"), 1)
                step(stt(TM, U1, -1.0, EX, ALU.add, ALU.subtract))
                step(dve.reciprocal(EX, U1))
                step(tt(TM, TM, EX, ALU.mult))
                dve.wait_ge(S("dt_ln"), 1)
                step(tt(TM, LN, TM, ALU.subtract))
                step(stt(tiny[:, DT:DT + 64], X, 0.0, TM, ALU.max, ALU.add))
                stt(t2(DTA, 32), t2(DT, 32), -1.0, alog[:, None, :].broadcast_to([P, NS, 32]), ALU.mult, ALU.mult).then_inc(S("dtA"), 1)
                for t in range(CONV_TILES):
                    dve.wait_ge(S("proj_free"), t // 2 + 1)
                    acc = xbc[:, t, :].rearrange("p (s t) -> p s t", s=NS)
                    cw = CONVW + t
                    step(ts(acc, xpad[:, t, :, 0:P], feat[:, cw:cw + 1], feat[:, CONVB + t:CONVB + t + 1], ALU.mult, ALU.add))
                    for j in range(1, TAPS):
                        last = stt(acc, xpad[:, t, :, j:j + P], feat[:, cw + CONV_TILES * j:cw + CONV_TILES * j + 1], acc, ALU.mult, ALU.add)
                        if j < TAPS - 1:
                            step(last)
                    last.then_inc(S("conv_done"), 1)
                for s in range(NS):
                    dve.wait_ge(S("tok_copied"), 5)
                    if s:
                        dve.wait_ge(S("y_raw"), 1)
                    for d in range(2):
                        step(tt(W(4)[:, d * D:(d + 1) * D].rearrange("p (h q) -> p h q", h=HEADS), heads(xtok[:, s, :]),
                                tiny[:, DT + 32 * s + 16 * d:DT + 32 * s + 16 * d + 16][:, :, None].broadcast_to([P, HEADS, HP]), ALU.mult))
                    if s == 0:
                        dve.wait_ge(S("te_exp"), 1)
                        for d in range(2):
                            last = tt(W(3)[:, d * D:(d + 1) * D].rearrange("p (h q) -> p h q", h=HEADS), W(4)[:, d * D:(d + 1) * D].rearrange("p (h q) -> p h q", h=HEADS),
                                      tiny[:, TE + 16 * d:TE + 16 * d + 16][:, :, None].broadcast_to([P, HEADS, HP]), ALU.mult)
                            if d == 0:
                                step(last)
                        last.then_inc(S("xw_ready"), 1)
                    dve.wait_ge(S("cb_raw"), s + 1)
                    cb = ps[:, 0, 0:2 * P].rearrange("p (g t) -> p g t", g=2)
                    for d in range(2):
                        last = tt(tiny[:, CBM + 256 * d:CBM + 256 * d + 256].rearrange("p (g t) -> p g t", g=2), cb,
                                  C(GE if d else LE)[:, None, :].broadcast_to([P, 2, P]), ALU.mult)
                        if d == 0:
                            step(last)
                    last.then_inc(S("cbm"), 1)
                    dve.wait_ge(S("cbm"), s + 1)
                    for d in range(2):
                        dve.wait_ge(S("seg_exp"), (8 + 8 * d + 4) if s else 4 * (d + 1))
                        for g in range(2):
                            m = W(d)[:, g * D:(g + 1) * D].rearrange("p (h t) -> p h t", h=8)
                            last = tt(m, m, tiny[:, CBM + 256 * d + P * g:CBM + 256 * d + P * g + P][:, None, :].broadcast_to([P, 8, P]), ALU.mult)
                            if s or (d, g) != (1, 1):
                                step(last)
                        if s:
                            dve.wait_ge(S("seg_exp"), 8 + 8 * d + 8)
                            for g in range(2):
                                m = W(2 + d)[:, g * D:(g + 1) * D].rearrange("p (h t) -> p h t", h=8)
                                last = tt(m, m, xbc[:, 10 + g, tk(1)][:, None, :].broadcast_to([P, 8, P]), ALU.mult)
                                if (d, g) != (1, 1):
                                    step(last)
                    last.then_inc(S("M_ready"), 1)
                    dve.wait_ge(S("y_raw"), s + 1)
                    for i in range(KT):
                        step(stt(xbc[:, i, tk(s)], xbc[:, i, tk(s)], dsk[:, i:i + 1], ps[:, 5 + i // 4, (i % 4) * P:(i % 4 + 1) * P], ALU.mult, ALU.add))
                    dve.wait_ge(S("proj_free"), 16)
                    tt(zs[:, :, tk(s)], zs[:, :, tk(s)], xbc[:, 0:KT, tk(s)], ALU.mult).then_inc(S("y_gated"), 1)
                dve.wait_ge(S("yrms"), 1)
                step(dve.reciprocal(rstd[:, 1, :], rstd[:, 1, :]))
                for k in range(KT):
                    last = stt(zs[:, k, :], zs[:, k, :], feat[:, SSDN + k:SSDN + k + 1], rstd[:, 1, :], ALU.mult, ALU.mult)
                    if k < KT - 1:
                        step(last)
                last.then_inc(S("yssd"), 1)
                dve.wait_ge(S("rotated"), 1)
                dve.wait_ge(S("keys_copied"), 2)
                q8 = QR.rearrange("p (k t) -> p k t", k=KT)
                w8 = W(2)[:, 0:D].rearrange("p (k t) -> p k t", k=KT)
                step(tt(w8, ps[:, 5:7, :].rearrange("p b (k t) -> p (b k) t", k=4), C(SIN)[:, None, :].broadcast_to([P, KT, P]), ALU.mult))
                step(tt(q8, qT[:, :, tk(1)], C(COS)[:, None, :].broadcast_to([P, KT, P]), ALU.mult))
                step(tt(q8, q8, w8, ALU.add))
                k4 = KR.rearrange("p (k t) -> p k t", k=4)
                w4 = W(2)[:, D:D + 512].rearrange("p (k t) -> p k t", k=4)
                step(tt(w4, ps[:, 4, :].rearrange("p (k t) -> p k t", k=4), C(SIN)[:, None, :].broadcast_to([P, 4, P]), ALU.mult))
                step(tt(k4, KTL.rearrange("p (k t) -> p k t", k=4), C(COS)[:, None, :].broadcast_to([P, 4, P]), ALU.mult))
                tt(k4, k4, w4, ALU.add).then_inc(S("rope"), 1)
                done = 0
                for g in range(3):
                    nh, w = (8, 256) if g else (16, 128)
                    h0 = 8 * (g - 1) if g else 0
                    dve.wait_ge(S("scores"), g + 1)
                    sc = ps[:, 0:4, :].rearrange("p b (h w) -> p (b h) w", w=w)
                    step(dve.tensor_reduce(tiny[:, MX:MX + nh], sc, AX.X, ALU.max))
                    sk = sink[:, h0:h0 + nh].rearrange("p (i a) -> p a i", a=2)

                    def eo(c):
                        return tiny[:, c:c + nh].rearrange("p (a i) -> p a i", a=2)
                    step(stt(eo(MX), eo(MX), SCALE, sk, ALU.mult, ALU.max))
                    step(ts(tiny[:, NEGM:NEGM + nh], tiny[:, MX:MX + nh], -1.0, None, ALU.mult))
                    tt(eo(SNKD), sk, eo(MX), ALU.subtract).then_inc(S("negm"), 1)
                    done += nh + 1
                    dve.wait_ge(S("p_exp"), done)
                    step(tt(tiny[:, RINV:RINV + nh], tiny[:, RSUM:RSUM + nh], tiny[:, SNKE:SNKE + nh], ALU.add))
                    step(dve.reciprocal(tiny[:, RINV:RINV + nh], tiny[:, RINV:RINV + nh]))
                    pr = W(0).rearrange("p (h w) -> p h w", w=w)
                    tt(pr, pr, tiny[:, RINV:RINV + nh][:, :, None].broadcast_to([P, nh, w]), ALU.mult).then_inc(S("probs"), 1)
                dve.wait_ge(S("slot_used"), pos["out0"] + n_out[0])
                residual(0, 16, 2)

            def odd():
                step(dve.memset(xpf[:, 0:1024], 0.0))
                for s in range(NS):
                    dve.wait_ge(S("gk_turned"), s + 1)
                    dve.tensor_copy(qT[:, 4:8, tk(s)], ps[:, 5 + s, :].rearrange("p (h t) -> p h t", h=GH)).then_inc(S("gk_copied"), 1)
                for c in range(4):
                    dve.wait_ge(S("gate_raw"), c + 1)
                    x, y = W(0)[:, c * 512:(c + 1) * 512], W(1)[:, c * 512:(c + 1) * 512]
                    step(dve.tensor_copy(x, ps[:, (5 + c) % 8, :]))
                    stt(y, x, -1.0, x, ALU.mult, ALU.max).then_inc(S("gate_abs"), 1)
                dve.wait_ge(S("gate_exp"), 2)
                for c in range(4):
                    x, y = W(0)[:, c * 512:(c + 1) * 512], W(1)[:, c * 512:(c + 1) * 512]
                    stt(x, x, 0.0, y, ALU.min, ALU.subtract).then_inc(S("g_ready"), 1)
                dve.wait_ge(S("gk_copied"), 2)
                dve.wait_ge(S("proj_free"), 16 + 4)
                for c in range(4):
                    dve.wait_ge(S("ecs"), 2 * c + 2)
                    s = c // 2

                    def h4(i):
                        return W(i)[:, c * 512:(c + 1) * 512].rearrange("p (h t) -> p h t", h=GH)
                    step(stt(h4(3), qT[:, 0:4, tk(s)], GLA_SCALE, h4(1), ALU.mult, ALU.mult))
                    tt(h4(4), qT[:, 4:8, tk(s)], h4(2), ALU.mult).then_inc(S("qk_ready"), 1)
                for c in range(4):
                    dve.wait_ge(S("kde"), c + 1)
                    x = W(0)[:, c * 512:(c + 1) * 512]
                    tt(x, x, kv[:, c // 2, :], ALU.mult).then_inc(S("kdec"), 1)
                for s in range(NS):
                    for d in range(2):
                        dve.wait_ge(S("gatt_raw"), 2 * s + d + 1)
                        for ch in range(2):
                            r = slice(CH * ch, CH * ch + CH)
                            src = ps[r, 2 * s + d, :].rearrange("p (h t) -> p h t", h=GH)[:, :, r]
                            step(tt((ATB if d else ATT)[r, s, :, r], src, cst[r, GE if d else LE, r][:, None, :].broadcast_to([CH, GH, CH]), ALU.mult))
                    for ch in range(2):
                        r = slice(CH * ch, CH * ch + CH)
                        last = tt(ATT[r, s, :, r], ATT[r, s, :, r], ATB[r, s, :, r], ALU.add)
                        if ch == 0:
                            step(last)
                    last.then_inc(S("gatt"), 1)
                dve.wait_ge(S("s0_in"), 32)
                for n, (s, d, ch) in enumerate(COMBOS):
                    dve.wait_ge(S("kv_raw"), n + 1)
                    b = 4 + 2 * (n % 2)
                    first = ch == d
                    dst = (W(2) if s == 0 else xbf) if first else hTf
                    if s == 0 and first:
                        dve.tensor_copy(dst[:, d * D:(d + 1) * D].rearrange("p (b w) -> p b w", b=2), ps[:, b:b + 2, :]).then_inc(S("state"), 1)
                        dve.wait_ge(S("state"), n + 1)
                    else:
                        before = W(5) if s else W(2)
                        for h in range(GH):
                            o = d * D + h * GV
                            dec = (2 * s + d) * 512 + h * P + CH * ch + (0 if d else CH - 1)
                            last = stt(dst[:, o:o + GV], before[:, o:o + GV], W(1)[:, dec:dec + 1],
                                       ps[:, b + h // 2, (h % 2) * T:(h % 2 + 1) * T], ALU.mult, ALU.add)
                            if h < GH - 1:
                                step(last)
                        last.then_inc(S("state"), 1)
                for s in range(NS):
                    dve.wait_ge(S("gy_raw"), s + 1)
                    dve.tensor_copy(yatt[:, :, tk(s)], ps[:, 2 * s:2 * s + 2, :].rearrange("p b (k t) -> p (b k) t", k=4)).then_inc(S("gy"), 1)
                dve.wait_ge(S("grms"), 1)
                step(dve.reciprocal(rstd[:, :, :], rstd[:, :, :]))
                for i in range(KT):
                    step(stt(yatt[:, i, :], yatt[:, i, :], feat[:, GLAN + i % 2:GLAN + i % 2 + 1], rstd[:, i // 2, :], ALU.mult, ALU.mult))
                dve.wait_ge(S("proj_free"), 28)
                tt(yatt[:, :, :], yatt[:, :, :], zs[:, :, :], ALU.mult).then_inc(S("gyn"), 1)
                dve.wait_ge(S("slot_used"), pos["out1"] + n_out[1])
                residual(1, 16, 4)

            def first_of_max(dst, src, mx):
                p4 = pref[:, None, :].broadcast_to([P, NS, 4])
                step(tt(t2(VAL, 4), src, mx.broadcast_to([P, NS, 4]), ALU.is_equal))
                step(tt(t2(VAL, 4), t2(VAL, 4), p4, ALU.mult))
                step(dve.tensor_reduce(tiny[:, VMX:VMX + 2], t2(VAL, 4), AX.X, ALU.max))
                step(tt(dst, t2(VAL, 4), t2(VMX, 1).broadcast_to([P, NS, 4]), ALU.is_equal))

            def moe(l):
                dve.wait_ge(S("pref"), 4)
                dve.wait_ge(S("logits"), l + 1)
                lg = t2(LG, 20)
                step(tt(lg, ps[:, 0, T:T + 64].rearrange("p (s n) -> p s n", s=NS)[:, :, 0:20], br[:, l:l + 1, :].broadcast_to([P, NS, 20]), ALU.add))
                step(dve.tensor_reduce(tiny[:, GMAX:GMAX + 2], lg[:, :, 0:4], AX.X, ALU.max))
                tt(t2(GEX, 4), lg[:, :, 0:4], t2(GMAX, 1).broadcast_to([P, NS, 4]), ALU.subtract).then_inc(S("g_sub"), 1)
                first_of_max(t2(OHG, 4), lg[:, :, 0:4], t2(GMAX, 1))
                for s in range(NS):
                    ep = tiny[:, EPR + 16 * s:EPR + 16 * s + 16]
                    step(tt(ep.rearrange("p (e g) -> p g e", g=4), lg[:, s, 4:20].rearrange("p (g e) -> p g e", g=4),
                            tiny[:, OHG + 4 * s:OHG + 4 * s + 4][:, :, None].broadcast_to([P, 4, 4]), ALU.mult))
                step(dve.tensor_reduce(tiny[:, EL:EL + 8], tiny[:, EPR:EPR + 32].rearrange("p (e g) -> p e g", g=4), AX.X, ALU.add))
                step(dve.tensor_reduce(tiny[:, EMX:EMX + 2], t2(EL, 4), AX.X, ALU.max))
                tt(t2(EL, 4), t2(EL, 4), t2(EMX, 1).broadcast_to([P, NS, 4]), ALU.subtract).then_inc(S("e_sub"), 1)
                dve.wait_ge(S("g_exp"), l + 1)
                step(dve.tensor_reduce(tiny[:, GPR:GPR + 2], t2(GEX, 4), AX.X, ALU.add))
                step(dve.reciprocal(tiny[:, GPR:GPR + 2], tiny[:, GPR:GPR + 2]))
                dve.wait_ge(S("e_exp"), l + 1)
                step(dve.tensor_reduce(tiny[:, EMX:EMX + 2], t2(EL, 4), AX.X, ALU.max))
                first_of_max(t2(OH1, 4), t2(EL, 4), t2(EMX, 1))
                step(stt(t2(P2, 4), t2(OH1, 4), -2.0, t2(EL, 4), ALU.mult, ALU.add))
                step(dve.tensor_reduce(tiny[:, M2:M2 + 2], t2(P2, 4), AX.X, ALU.max))
                first_of_max(t2(OH2, 4), t2(P2, 4), t2(M2, 1))
                step(tt(tiny[:, DEN:DEN + 2], tiny[:, EMX:EMX + 2], tiny[:, M2:M2 + 2], ALU.add))
                step(dve.reciprocal(tiny[:, DEN:DEN + 2], tiny[:, DEN:DEN + 2]))
                step(tt(tiny[:, DEN:DEN + 2], tiny[:, DEN:DEN + 2], tiny[:, GPR:GPR + 2], ALU.mult))
                step(tt(t2(OH1, 4), t2(OH1, 4), t2(OH2, 4), ALU.add))
                step(tt(t2(LOC, 4), t2(OH1, 4), t2(EL, 4), ALU.mult))
                step(tt(t2(LOC, 4), t2(LOC, 4), t2(DEN, 1).broadcast_to([P, NS, 4]), ALU.mult))
                for s in range(NS):
                    step(tt(tiny[:, CMB + 16 * s:CMB + 16 * s + 16].rearrange("p (g e) -> p g e", g=4),
                            tiny[:, OHG + 4 * s:OHG + 4 * s + 4][:, :, None].broadcast_to([P, 4, 4]),
                            tiny[:, LOC + 4 * s:LOC + 4 * s + 4][:, None, :].broadcast_to([P, 4, 4]), ALU.mult))
                for s in range(NS):
                    tt(W(2 + s).rearrange("p (e t) -> p e t", e=NE), tiny[:, CMB + 16 * s:CMB + 16 * s + 16][:, :, None].broadcast_to([P, NE, P]),
                       C(IDENT)[:, None, :].broadcast_to([P, NE, P]), ALU.mult).then_inc(S("cmb_diag"), 1)
                dve.wait_ge(S("comb"), 8 * l + 8)
                with dve.Fori(0, NE) as e:
                    for f in range(FT):
                        dve.wait_ge(S("sil"), e * FT + (l * NE * FT + f + 1))
                        tt(PROD[:, f, :], SIL[:, f, :], ps[:, f, T:2 * T], ALU.mult).then_inc(S("prod"), 1)
                        dve.wait_ge(S("prod"), e * FT + (l * NE * FT + f + 1))
                        tt(HACT[:, f:f + 1, :], PROD[:, f:f + 1, :], COMB[:, bass.ds(e, 1), :], ALU.mult).then_inc(S("hact"), 1)
                dve.wait_ge(S("slot_used"), pos[f"moe{l}"] + NE * PER_EXPERT)
                residual(l, 40, 2 * l + 3)

            ada(0)
            norm(0)
            even()
            norm(1)
            moe(0)
            ada(1)
            norm(2)
            odd()
            norm(3)
            moe(1)
            norm(4)


_INS = ['x_prompt', 'x_sample', 'cache_k_attn', 'cache_v_attn', 'state_ssd_fwd', 'state_ssd_bwd', 'state_gla_fwd',
        'state_gla_bwd', 'c', 'c_ctx', 'w_ada', 'b_ada', 'norm_mix_w', 'norm_ffn_w', 'w_in_even', 'conv_w', 'conv_b',
        'dt_bias_fwd', 'dt_bias_bwd', 'a_log_fwd', 'a_log_bwd', 'd_skip', 'ssd_norm_w', 'attn_sink', 'w_out_even',
        'w_in_odd', 'w_gk2_fwd', 'b_gk_fwd', 'w_gk2_bwd', 'b_gk_bwd', 'gla_norm_w', 'w_out_odd', 'w_router_group',
        'b_router_group', 'w_router_expert', 'b_router_expert', 'w_gate_exp', 'w_up_exp', 'w_down_exp', 'final_norm_w']
_OUTS = [(1, 128, 1024), (1, 128, 1024), (1, 1, 128, 4, 64), (1, 1, 128, 4, 64), (1, 1, 16, 64, 128), (1, 1, 16, 64, 128),
         (1, 1, 4, 128, 256), (1, 1, 4, 128, 256)]


def kernel(**inputs):
    import concourse.bacc as _bacc
    from concourse.bass_utils import run_bass_kernel_spmd as _run

    nc = _bacc.Bacc("TRN2", target_bir_lowering=False, num_devices=1)
    arrays, args = {}, {}
    for name in _INS:
        a = np.ascontiguousarray(inputs[name])
        arrays[f"in_{name}_dram"] = a
        args[name] = nc.dram_tensor(f"in_{name}_dram", a.shape, F32, kind="ExternalInput").ap()
    arrays["in_consts_dram"] = constants()
    args["consts"] = nc.dram_tensor("in_consts_dram", (P, NCONST, P), F32, kind="ExternalInput").ap()
    outs = [nc.dram_tensor(f"out_{i}_dram", shape, F32, kind="ExternalOutput").ap() for i, shape in enumerate(_OUTS)]
    build(nc, args, outs)
    r = _run(nc, [arrays], core_ids=[0])
    return tuple(r.results[0][f"out_{i}_dram"] for i in range(len(_OUTS)))
```

```python
from contextlib import ExitStack

import numpy as np
import concourse.bass as bass
from concourse import mybir

F32 = mybir.dt.float32
ACT = mybir.ActivationFunctionType
ALU = mybir.AluOpType
AX = mybir.AxisListType

P = 128
D = 1024
KT = D // P
T = 256
NS = 2
GRID_W = 64
EPS = 1e-6
HEADS, HP, NST = 16, 64, 128
CONV_TILES = 12
TAPS = 5
KVH = 4
SCALE = 0.125
LOWRANK = 16
GH, GK, GV, CH = 4, 128, 256, 64
GLA_SCALE = float(GK) ** -0.5
NE, FE = 16, 512
FT = FE // P
CHUNK = 2048
RING = 6
PER_EXPERT = 6
PAIRS = NE // 2
CAP = 64
PAIR_ORDER = [(a, c) for c in range(PER_EXPERT) for a in range(2)]
assert 2 * PER_EXPERT % RING == 0 and RING >= PER_EXPERT
COMBOS = ((0, 0, 0), (0, 0, 1), (0, 1, 1), (0, 1, 0), (1, 0, 0), (1, 1, 1))

BADA, NMIX, NFFN = 0, 96, 112
CONVW, CONVB, SSDN, GLAN, FINN, CVEC, CCTX = 128, 188, 200, 208, 210, 218, 226

(IDENT, ONES, MEAN_D, MEAN_V, LE, GE, GT, LT, BLE, BGE, BGT, BLT, COS, SIN, ROT, IOTA) = range(16)
NCONST = 17
ADA = 384
FAR = 1024.0


def constants():
    i = np.arange(P)
    k, m = i[:, None], i[None, :]
    c = np.zeros((NCONST, P, P), np.float32)
    same = (k // CH) == (m // CH)
    c[IDENT] = k == m
    c[ONES] = 1.0
    c[MEAN_D] = 1.0 / D
    c[MEAN_V] = 1.0 / GV
    c[LE], c[GE], c[GT], c[LT] = k <= m, k >= m, k > m, k < m
    for n, cond in ((BLE, k <= m), (BGE, k >= m), (BGT, k > m), (BLT, k < m)):
        c[n] = (cond & same) / 16.0
    c[IOTA], c[IOTA + 1] = m - FAR, m + P - FAR
    quarter = 16
    inv = (np.float32(10000.0) ** (-np.arange(quarter, dtype=np.float32) / np.float32(quarter))).astype(np.float32)
    d = i % 64
    pos = np.where(d[:, None] < 32, m // GRID_W, m % GRID_W).astype(np.float32)
    ang = (pos * inv[d % quarter][:, None]).astype(np.float32)
    c[COS], c[SIN] = np.cos(ang), np.sin(ang)
    for q in range(P):
        if q % 32 < quarter:
            c[ROT][q + quarter, q] = -1.0
        else:
            c[ROT][q - quarter, q] = 1.0
    return np.ascontiguousarray(c.transpose(1, 0, 2))



DTX, DTA, DTT, DTE, DTU, DTL, DT, TE, WS = 0, 64, 128, 192, 256, 320, 384, 448, 480
CBM = 512
MX, NEGM, RSUM, SNKD, SNKE, RINV = 0, 16, 32, 48, 64, 80
(LG, GMAX, OHG, GEX, EPR, EL, EMX, OH1, P2, M2, OH2, DEN, GPR, LOC, CMB, VAL, VMX, SEL, RK, CNT) = \
    (0, 40, 48, 56, 64, 96, 104, 120, 128, 136, 144, 152, 156, 160, 192, 224, 232, 256, 288, 320)


def build(nc, A, O):
    with ExitStack() as ctx:
        def sb(name, shape):
            return ctx.enter_context(nc.sbuf_tensor(name, shape, F32))

        sems = {}

        def S(name):
            if name not in sems:
                sems[name] = ctx.enter_context(nc.semaphore(name))
            return sems[name]

        ring = sb("ring", [P, RING, CHUNK])
        cst = sb("cst", [P, NCONST, P])
        xT = sb("xT", [P, KT, T])
        hT = sb("hT", [P, KT, T])
        rows = sb("rows", [P, 2, P])
        feat = sb("feat", [P, 2 * P])
        csilu = sb("csilu", [P, KT, NS])
        mods = sb("mods", [P, 2, 48, NS])
        rstd = sb("rstd", [P, GH, T])
        xpad = sb("xpad", [P, CONV_TILES, NS, P + TAPS - 1])
        xbc = sb("xbc", [P, CONV_TILES, T])
        zs = sb("zs", [P, KT, T])
        yatt = sb("yatt", [P, KT, T])
        qT = sb("qT", [P, KT, T])
        kv = sb("kv", [P, NS, 512])
        xtok = sb("xtok", [P, NS, D])
        btok = sb("btok", [P, 2 * P])
        wide = sb("wide", [P, 6, 2048])
        wdt = sb("wdt", [P, KT, 32])
        wlr = sb("wlr", [P, KT, 32])
        wr = sb("wr", [P, 2, KT, 20])
        br = sb("br", [P, 2, 20])
        dtb = sb("dtb", [P, 32])
        alog = sb("alog", [P, 32])
        dskb = sb("dskb", [P, HEADS])
        dsk = sb("dsk", [P, KT])
        sink = sb("sink", [P, HEADS])
        ckv = sb("ckv", [P, 2, 256])
        wg = sb("wg", [LOWRANK + 1, 2, 512])
        lr = sb("lr", [LOWRANK + 1, 2 * T])
        tiny = sb("tiny", [P, 1024])
        need = ctx.enter_context(nc.sbuf_tensor("need", [P, 2], mybir.dt.int32))
        pref = sb("pref", [P, 4])
        eps = sb("eps", [P, 1])
        ps = ctx.enter_context(nc.psum_tensor("ps", [P, 8, 512], F32))

        zero = rows[:, :, :].rearrange("p a b -> p (a b)")

        def C(n):
            return cst[:, n, :]

        def W(i):
            return wide[:, i, :]

        xpf = xpad[:, :, :, :].rearrange("p a b c -> p (a b c)")
        hTf = hT[:, :, :].rearrange("p k t -> p (k t)")
        xbf = xbc[:, :, :].rearrange("p k t -> p (k t)")
        yaf = yatt[:, :, :].rearrange("p k t -> p (k t)")
        U = xpf[:, 0:2048]
        KTC, KTL, KTP = xpf[:, 0:512], xpf[:, 512:1024], xpf[:, 1024:1536]
        QR, KR = xpf[:, 1536:2560], xpf[:, 2560:3072]
        ATT = xpf[:, 0:1024].rearrange("p (s h t) -> p s h t", s=NS, h=GH)
        ATB = xpf[:, 1024:2048].rearrange("p (s h t) -> p s h t", s=NS, h=GH)
        CT = W(0).rearrange("p (i t) -> p i t", i=PAIRS)
        DISP, DISW = W(2), W(3)
        HG = W(1)[:, 0:1024].rearrange("p (k c) -> p k c", k=KT)
        YS = W(1)[:, 1024:2048]
        HACT, SIL = W(4)[:, 0:FE], W(4)[:, FE:2 * FE]
        HT = W(5)[:, 0:FE].rearrange("p (f c) -> p f c", f=FT)
        O_HG = W(4)[:, 1024:1536].rearrange("p (k c) -> p k c", k=KT)
        O_ACT, O_SIL = W(5)[0:CAP, 512:1024], W(5)[0:CAP, 1024:1536]
        O_HT = W(4)[:, 1536:1792].rearrange("p (f c) -> p f c", f=FT)
        O_CT = W(5)[0:CAP, 1536:1792]
        O_DISP, O_DISW = W(5)[:, 1792:1920], W(5)[:, 1920:2048]
        O_YS = W(1)[0:CAP, 0:1024]

        def tk(s):
            return slice(s * P, (s + 1) * P)

        def heads(ap, n=HEADS):
            return ap.rearrange("p (h w) -> p h w", h=n)

        w_in = (A["w_in_even"][0], A["w_in_odd"][0])
        w_out = (A["w_out_even"][0], A["w_out_odd"][0])
        IN = ([1024 + 256 * i for i in range(6)] + [3616, 3872] + [2592 + 256 * i for i in range(4)]
              + [256 * i for i in range(4)],
              [256 * i for i in range(12)])
        n_ada = 6 * D // 256
        n_first = 2 * D // 256
        n_out = (w_out[0].shape[0] // 256, w_out[1].shape[0] // 256)
        per_pair = n_ada // PAIRS
        a_slots = ((W(0), W(1), W(3)), tuple(x[:, :, :].rearrange("p k t -> p (k t)") for x in (zs, yatt, qT)))
        a_sums = (W(4).rearrange("p (c g n) -> p c g n", c=4, g=NS), xbf[:, 0:3 * 512].rearrange("p (c g n) -> p c g n", c=3, g=NS))
        def dve_tiles(n):
            return 5 if n < n_first else 6 if n < n_ada else KT

        def summed(n, rounds=0):
            return rounds * (per_pair * KT * NS) + NS * sum(dve_tiles(x) for x in range(n + 1))

        pos, at = {}, 0
        for name, n in (("in0", len(IN[0])), ("out0", n_out[0]), ("moe0", NE * PER_EXPERT), ("in1", len(IN[1])), ("out1", n_out[1]), ("moe1", NE * PER_EXPERT)):
            pos[name] = at
            at += n

        def slot(n, k):
            return ring[:, n % RING, :].rearrange("p (k n) -> p k n", k=k)

        def wait_landed(pe, n, rounds=0):
            pe.wait_ge(S(f"landed{n % RING}"), rounds * 16 + 16 * (n // RING + 1))

        def stepper(eng, name):
            count = [0]

            def step(ins):
                count[0] += 1
                ins.then_inc(S(name), 1)
                eng.wait_ge(S(name), count[0])
            return step

        def place(i, n):
            return (i % 2) * (n // 2) + i // 2

        def mm(pe, out, lhsT, rhs, first, last, shared=False):
            return pe.matmul(out, lhsT, rhs, start=first, stop=last, skip_group_check=shared)

        block = ctx.enter_context(nc.Block())

        @block.sync
        def _(sp):
            def load(n, src, k, rounds=0):
                sp.dma_start(slot(n, k), src).then_inc(S(f"landed{n % RING}"), 16)

            def wait_free(n, rounds=0):
                sp.wait_ge(S("slot_used"), rounds * RING + (n + 1 - RING))

            def ada(l, c):
                if l == 0:
                    n, rounds = c, 0
                else:
                    n, (rounds, c) = n_ada + c[1], (c[0], c[0] * per_pair + c[1])
                if l or n >= 3:
                    sp.wait_ge(S("mac_summed"), rounds * per_pair + (n - 2))
                src = A["w_ada"][l].rearrange("(k p) n -> p k n", p=P)[:, :, bass.ds(c * 256, 256)]
                sp.dma_start(a_slots[l][n % 3].rearrange("p (k n) -> p k n", k=KT), src).then_inc(S(f"ada_landed{n % 3}"), 16)

            def w_in_load(l, j):
                n = pos[f"in{l}"] + j
                if n >= RING:
                    wait_free(n)
                load(n, w_in[l][:, IN[l][j]:IN[l][j] + 256].rearrange("(k p) n -> p k n", p=P), KT)

            for c in range(3):
                ada(0, c)
            for c in range(3, n_ada):
                if c - 3 < len(IN[0]):
                    w_in_load(0, c - 3)
                ada(0, c)
            for l in range(2):
                if l:
                    for j in range(len(IN[1])):
                        w_in_load(1, j)
                for j in range(n_out[l]):
                    wait_free(pos[f"out{l}"] + j)
                    load(pos[f"out{l}"] + j, w_out[l][256 * j:256 * j + 256, :].rearrange("(k p) n -> p k n", p=P), 2)
                base = pos[f"moe{l}"]
                wgu = [A[w][l].rearrange("e (k p) f -> p e k f", p=P) for w in ("w_gate_exp", "w_up_exp")]
                wd = A["w_down_exp"][l].rearrange("e (j k p) d -> p e j k d", p=P, k=2)

                def expert(e, c, n):
                    if c < 4:
                        src = wgu[c // 2][:, bass.ds(e, 1), 4 * (c % 2):4 * (c % 2) + 4, :]
                        return slot(n, 4), src.rearrange("p a k f -> p (a k) f")
                    src = wd[:, bass.ds(e, 1), c - 4, :, :]
                    return slot(n, 2), src.rearrange("p a k d -> p (a k) d")

                if l == 0:
                    sp.wait_ge(S("slot_used"), pos["out0"] + n_out[0])
                with sp.Fori(0, PAIRS) as i:
                    for n, (a, c) in enumerate(PAIR_ORDER):
                        if l == 0 and n in (2, 4, 6):
                            ada(1, (i, n // 2 - 1))
                        wait_free(base + n, i * (2 * PER_EXPERT // RING))
                        dst, src = expert(i * 2 + a, c, base + n)
                        sp.dma_start(dst, src).then_inc(S(f"landed{(base + n) % RING}"), 16)
                sp.wait_ge(S("need"), l + 1)
                most = sp.value_load(need[0:1, l:l + 1], min_val=0, max_val=T)
                with sp.If(most > CAP):
                    sp.wait_ge(S("slot_used"), base + NE * PER_EXPERT)
                    with sp.Fori(0, NE) as e:
                        with sp.Fori(1, T // CAP) as r:
                            it = e * (T // CAP - 1) + r
                            for c in range(PER_EXPERT):
                                sp.wait_ge(S(f"o{l}_used"), it * PER_EXPERT + (c + 1 - PER_EXPERT))
                                dst, src = expert(e, c, c)
                                sp.dma_start(dst, src).then_inc(S(f"o{l}_landed{c}"), 16)
                    sp.wait_ge(S(f"o{l}_used"), (NE * (T // CAP - 1) + 1) * PER_EXPERT)
            for s in range(NS):
                sp.wait_ge(S("y_tok"), 2 * s + 2)
                sp.dma_start(O[s][0], xtok[:, s, :]).then_inc(S("y_stored"), 16)
            sp.wait_ge(S("y_stored"), 32)

        O_STEPS = 6
        SMALL = 16 * (7 + 8 + 2 + 1 + 4)

        @block.gpsimd
        def _(pool):
            def load(dst, src):
                pool.dma_start(dst, src).then_inc(S("small_in"), 16)

            def spread(src, n):
                return src.rearrange("(a n) -> a n", a=1).broadcast_to([P, n])

            pool.memset(xpf, 0.0).then_inc(S("pad_zero"), 1)
            load(wdt[:, :, :], w_in[0][:, 2560:2592].rearrange("(k p) n -> p k n", p=P))
            load(dtb[:, 0:16], spread(A["dt_bias_fwd"][0], 16))
            load(dtb[:, 16:32], spread(A["dt_bias_bwd"][0], 16))
            load(alog[:, 0:16], spread(A["a_log_fwd"][0], 16))
            load(alog[:, 16:32], spread(A["a_log_bwd"][0], 16))
            load(dskb[:, :], spread(A["d_skip"][0], 16))
            load(sink[:, :], spread(A["attn_sink"][0], 16))
            for l in range(2):
                load(wr[:, l, :, 0:4], A["w_router_group"][l].rearrange("(k p) n -> p k n", p=P))
                load(wr[:, l, :, 4:20], A["w_router_expert"][l].rearrange("(k p) n -> p k n", p=P))
                load(br[:, l, 0:4], spread(A["b_router_group"][l], 4))
                load(br[:, l, 4:20], spread(A["b_router_expert"][l], 16))
            load(ckv[:, 0, :], A["cache_k_attn"][0, 0].rearrange("t h d -> t (h d)"))
            load(ckv[:, 1, :], A["cache_v_attn"][0, 0].rearrange("t h d -> t (h d)"))
            load(wlr[:, :, :], w_in[1][:, 3072:3104].rearrange("(k p) n -> p k n", p=P))
            load(wg[0:16, 0, :], A["w_gk2_fwd"][0])
            load(wg[0:16, 1, :], A["w_gk2_bwd"][0])
            load(wg[16:17, 0, :], A["b_gk_fwd"])
            load(wg[16:17, 1, :], A["b_gk_bwd"])
            pool.wait_ge(S("proj_free"), 8)
            pool.wait_ge(S("small_in"), SMALL)
            for n, keys in enumerate((kv[:, 0, 0:256], kv[:, 1, 0:256], ckv[:, 0, :])):
                pool.tensor_copy(W(5)[:, n * 512:(n + 1) * 512].rearrange("p (j a d) -> p j a d", j=KVH, a=2),
                                 keys.rearrange("p (j d) -> p j d", j=KVH)[:, :, None, :].broadcast_to([P, KVH, 2, 64])).then_inc(S("keys_twice"), 1)
            after = (0, 4, 8, 16)
            pool.wait_ge(S("dtA"), 1)
            pool.wait_ge(S("conv_done"), CONV_TILES)
            pool.wait_ge(S("consts_in"), 16)
            for n in range(4):
                if n:
                    pool.wait_ge(S("seg_raw"), after[n])
                a0 = DTA + 16 * n
                pool.tensor_tensor(heads(U), C(GE if n % 2 else LE)[:, None, :].broadcast_to([P, HEADS, P]),
                                   tiny[:, a0:a0 + 16][:, :, None].broadcast_to([P, HEADS, P]),
                                   ALU.mult).then_inc(S("U_ready"), 1)

        @block.tensor
        def _(pe):
            def used(ins):
                ins.then_inc(S("slot_used"), 1)

            def turn(out, in_, n=P):
                return pe.transpose(out, in_, cst[0:n, IDENT, 0:n])

            pe.wait_ge(S("consts_in"), 16)
            pe.wait_ge(S("rows_in"), 160)
            turn(ps[:, 0, 0:P], rows[:, 0, :])
            turn(ps[:, 0, P:P + 106], rows[0:106, 1, :], 106).then_inc(S("rows_turned"), 1)
            pe.wait_ge(S("x_in"), 32)
            for g in range(4):
                for k in range(4):
                    last = turn(ps[:, 1 + g, k * P:(k + 1) * P], xtok[:, g // 2, ((g % 2) * 4 + k) * P:((g % 2) * 4 + k + 1) * P])
                last.then_inc(S("x_turned"), 1)

            def ada(bank, col, sums, n, rounds=0):
                direct = range(dve_tiles(n), KT)
                if direct:
                    w = a_slots[0][n % 3].rearrange("p (k n) -> p k n", k=KT)
                    pe.wait_ge(S(f"ada_landed{n % 3}"), 16 * (n // 3 + 1))
                for m in range(2):
                    for k in direct:
                        mm(pe, ps[:, bank, col + 2 * m:col + 2 * m + 2], w[:, k, m * P:(m + 1) * P], csilu[:, k, :], k == direct[0], False, shared=True)
                    if m == 0:
                        pe.wait_ge(S("mac"), summed(n, rounds))
                    for g in range(NS):
                        last = mm(pe, ps[:, bank, col + 2 * m + g:col + 2 * m + g + 1], sums[:, g, m * P:(m + 1) * P], cst[:, ONES, 0:1], not direct, True, shared=True)
                last.then_inc(S("mac_summed"), 1)

            def ada0(n):
                ada(0, ADA + 4 * n, a_sums[0][:, n % 4], n)

            def norm(i):
                pe.wait_ge(S("sq"), i + 1)
                if i == 0:
                    pe.wait_ge(S("mods"), 1)
                for k in range(KT):
                    last = mm(pe, ps[:, 0, 0:T], C(MEAN_D), hT[:, k, :], k == 0, k == KT - 1)
                last.then_inc(S("ss"), 1)

            def project(n, b, by_token):
                wait_landed(pe, n)
                for m in range(2):
                    for k in range(KT):
                        if by_token:
                            last = mm(pe, ps[:, b, m * T:(m + 1) * T], hT[:, k, tk(m)], slot(n, KT)[:, k, :], k == 0, k == KT - 1)
                        else:
                            last = mm(pe, ps[:, b, m * T:(m + 1) * T], slot(n, KT)[:, k, m * P:(m + 1) * P], hT[:, k, :], k == 0, k == KT - 1)
                used(last)

            def projections(l):
                done = 0 if l == 0 else len(IN[0])
                for j in range(len(IN[l])):
                    if done + j >= 4:
                        pe.wait_ge(S("proj_free"), done + j - 3)
                    project(pos[f"in{l}"] + j, 1 + j % 4, j in ((6, 7) if l == 0 else range(2, 8)))
                    if l == 0 and j == 2:
                        pe.wait_ge(S("dt_abs"), 1)
                    if l == 0 and j >= 2:
                        ada0(n_first + j - 2)
                if l == 0:
                    for n in (n_ada - 2, n_ada - 1):
                        ada0(n)

            def out_project(l, src):
                for c in range(n_out[l]):
                    n = pos[f"out{l}"] + c
                    wait_landed(pe, n)
                    for k in range(2):
                        t = 2 * c + k
                        for m in range(KT):
                            last = mm(pe, ps[:, 4 + m // 2, (m % 2) * T:(m % 2 + 1) * T], slot(n, 2)[:, k, m * P:(m + 1) * P],
                                      src(t), t == 0 and m % 2 == 0, t == 2 * n_out[l] - 1, shared=True)
                    used(last)

            def even():
                pe.wait_ge(S("h_ready"), 1)
                pe.wait_ge(S("small_in"), SMALL)
                for s in range(NS):
                    for k in range(KT):
                        last = mm(pe, ps[:, 0, T + 32 * s:T + 32 * s + 32], hT[:, k, tk(s)], wdt[:, k, :], k == 0, k == KT - 1)
                last.then_inc(S("dt_raw"), 1)
                projections(0)
                for g in range(5):
                    pe.wait_ge(S("xbc_ready"), (2 + 2 * (g % 2)) if g < 4 else 5)
                    if g >= 3:
                        pe.wait_ge(S("tok_copied"), g - 2)
                    for k in range(4 if g < 4 else 2):
                        in_ = xbc[:, (g % 2) * 4 + k, tk(g // 2)] if g < 4 else xbc[:, 8 + k, tk(0)]
                        last = turn(ps[:, 5 + g % 3, k * P:(k + 1) * P], in_)
                    last.then_inc(S("tok_turned"), 1)
                pe.wait_ge(S("h0_in"), 32)
                pe.wait_ge(S("proj_free"), 16)
                for g in range(4):
                    for k in range(4):
                        last = turn(ps[:, 1 + g, k * P:(k + 1) * P], W(2)[:, (4 * g + k) * P:(4 * g + k + 1) * P])
                    last.then_inc(S("h0_turned"), 1)
                pe.wait_ge(S("dtA"), 1)
                pe.wait_ge(S("tok_copied"), 5)
                for d in range(2):
                    last = mm(pe, ps[:, 7, 256 + 16 * d:272 + 16 * d], C(LT if d else GT), tiny[:, DTA + 16 * d:DTA + 16 * d + 16], True, True)
                last.then_inc(S("te_raw"), 1)
                unit = 0
                for s in range(NS):
                    pe.wait_ge(S("xbc_ready"), 6)
                    pe.wait_ge(*((S("cbm"), 1) if s else (S("mods"), 2)))
                    for g in range(2):
                        last = mm(pe, ps[:, 0, g * P:(g + 1) * P], xbc[:, 8 + g, tk(s)], xbc[:, 10 + g, tk(s)], True, True)
                    last.then_inc(S("cb_raw"), 1)
                    for d in range(2):
                        pe.wait_ge(S("U_ready"), 2 * s + d + 1)
                        for w in range(1 + s):
                            for q in range(4):
                                if unit < 4:
                                    pe.wait_ge(S("h0_copied"), unit + 1)
                                elif unit < 8 or unit >= 12:
                                    pe.wait_ge(S("seg_exp"), unit - 3)
                                else:
                                    pe.wait_ge(S("st_copied"), q + 1)
                                mm(pe, ps[:, 1 + unit % 4, :], C(ONES) if w else C(LT if d else GT),
                                   U[:, q * 512:(q + 1) * 512], True, True).then_inc(S("seg_raw"), 1)
                                unit += 1
                    if s == 0:
                        pe.wait_ge(S("xw_ready"), 1)
                        pe.wait_ge(S("tok_copied"), 5)
                        pe.wait_ge(S("seg_exp"), 8)
                        for i in range(16):
                            g = (i % 8) // 4
                            last = mm(pe, ps[:, 1 + i // 4, (i % 4) * P:(i % 4 + 1) * P], W(3)[:, i * P:(i + 1) * P],
                                      btok[:, g * P:(g + 1) * P], True, True)
                            if i % 4 == 3:
                                last.then_inc(S("st_raw"), 1)
                    pe.wait_ge(S("M_ready"), s + 1)
                    if s:
                        pe.wait_ge(S("y_gated"), 1)
                    for h in range(HEADS):
                        out = ps[64 * (h % 2):64 * (h % 2) + 64, 5 + h // 8, (h // 2 % 4) * P:(h // 2 % 4 + 1) * P]
                        terms = [(W(4)[:, d * D + h * HP:d * D + (h + 1) * HP], W(d)[:, h * P:(h + 1) * P]) for d in range(2)]
                        if s:
                            terms += [(hTf[:, d * D + h * HP:d * D + (h + 1) * HP], W(2 + d)[:, h * P:(h + 1) * P]) for d in range(2)]
                        for n, (a, b) in enumerate(terms):
                            last = mm(pe, out, a, b, n == 0, n == len(terms) - 1)
                    last.then_inc(S("y_raw"), 1)
                pe.wait_ge(S("ysq"), 1)
                for k in range(KT):
                    last = mm(pe, ps[:, 0, 0:T], C(MEAN_D), W(4)[:, k * T:(k + 1) * T], k == 0, k == KT - 1)
                last.then_inc(S("yss"), 1)

                pe.wait_ge(S("seg_exp"), 24)
                pe.wait_ge(S("keys_twice"), 3)
                for n in range(3):
                    for j in range(KVH):
                        last = turn(ps[:, 1 + n, j * P:(j + 1) * P], W(5)[:, (4 * n + j) * P:(4 * n + j + 1) * P])
                    last.then_inc(S("keys_turned"), 1)
                pe.wait_ge(S("keys_copied"), 2)
                pe.wait_ge(S("y_gated"), 2)
                mm(pe, ps[:, 4, :], C(ROT), KTL, True, True)
                for b in range(2):
                    last = mm(pe, ps[:, 5 + b, :], C(ROT), qT[:, 4 * b:4 * b + 4, tk(1)], True, True)
                last.then_inc(S("rotated"), 1)
                pe.wait_ge(S("keys_copied"), 3)
                pe.wait_ge(S("rope"), 1)
                pe.wait_ge(S("yssd"), 1)
                for g in range(3):
                    if g:
                        pe.wait_ge(S("yatt"), g + 1)
                    nh = 8 if g else 16
                    for i in range(nh):
                        h = 8 * (g - 1) + i if g else i
                        b, j = 64 * (h % 2), (h // 4) * P
                        i = place(i, nh)
                        if g == 0:
                            last = mm(pe, ps[:, i // 4, (i % 4) * P:(i % 4 + 1) * P], qT[b:b + 64, h // 2, tk(0)], KTC[b:b + 64, j:j + P], True, True)
                        else:
                            mm(pe, ps[:, i // 2, (i % 2) * T:(i % 2) * T + P], qT[b:b + 64, h // 2, tk(1)], KTP[b:b + 64, j:j + P], True, True)
                            last = mm(pe, ps[:, i // 2, (i % 2) * T + P:(i % 2) * T + T], QR[b:b + 64, (h // 2) * P:(h // 2 + 1) * P], KR[b:b + 64, j:j + P], True, True)
                    last.then_inc(S("scores"), 1)
                    pe.wait_ge(S("probs"), g + 1)
                    if g:
                        pe.wait_ge(S("pT_copied"), 4 * g)
                    for i in range(16):
                        last = turn(ps[:, 4 + i // 4, (i % 4) * P:(i % 4 + 1) * P], W(0)[:, i * P:(i + 1) * P])
                    last.then_inc(S("probs_turned"), 1)
                    pe.wait_ge(S("pT_copied"), 4 * (g + 1))
                    for i in range(nh):
                        h = 8 * (g - 1) + i if g else i
                        v0 = (h // 4) * 64
                        out = ps[64 * (h % 2):64 * (h % 2) + 64, (i // 8) if g == 0 else 0, (h // 2 % 4) * P:(h // 2 % 4 + 1) * P]
                        i = place(i, nh)
                        if g == 0:
                            last = mm(pe, out, kv[:, 0, 256 + v0:320 + v0], W(1)[:, i * P:(i + 1) * P], True, True)
                        else:
                            mm(pe, out, ckv[:, 1, v0:v0 + 64], W(1)[:, 2 * i * P:(2 * i + 1) * P], True, False)
                            last = mm(pe, out, kv[:, 1, 256 + v0:320 + v0], W(1)[:, (2 * i + 1) * P:(2 * i + 2) * P], False, True)
                    last.then_inc(S("att_raw"), 1)
                pe.wait_ge(S("yatt"), 4)
                out_project(0, lambda t: zs[:, t, :] if t < KT else yatt[:, t - KT, :])

            def odd():
                pe.wait_ge(S("h_ready"), 3)
                for d in range(2):
                    for k in range(KT):
                        last = mm(pe, ps[0:16, 0, d * T:(d + 1) * T], wlr[:, k, 16 * d:16 * d + 16], hT[:, k, :], k == 0, k == KT - 1)
                last.then_inc(S("lr_raw"), 1)
                projections(1)
                pe.wait_ge(S("proj_free"), 16 + 4)
                for s in range(NS):
                    for h in range(GH):
                        last = turn(ps[:, 5 + s, h * P:(h + 1) * P], kv[:, s, h * P:(h + 1) * P])
                    last.then_inc(S("gk_turned"), 1)
                pe.wait_ge(S("gk_copied"), 2)
                pe.wait_ge(S("lr"), 1)
                for c in range(4):
                    b, d = (5 + c) % 8, c % 2
                    mm(pe, ps[:, b, :], lr[:, d * T + (c // 2) * P:d * T + (c // 2 + 1) * P], wg[:, d, :], True, True).then_inc(S("gate_raw"), 1)
                pe.wait_ge(S("proj_free"), 28)
                pe.wait_ge(S("g_ready"), 4)
                for c in range(4):
                    for h in range(GH):
                        last = mm(pe, ps[:, c, h * P:(h + 1) * P], W(0)[:, c * 512 + h * P:c * 512 + (h + 1) * P], C(BGE if c % 2 else BLE), True, True)
                    last.then_inc(S("cs_raw"), 1)
                for c in range(4):
                    mm(pe, ps[:, 4 + c, :], C(BLT if c % 2 else BGT), W(0)[:, c * 512:(c + 1) * 512], True, True).then_inc(S("rest_raw"), 1)
                pe.wait_ge(S("ecs"), 8)
                pe.wait_ge(S("qk_ready"), 4)
                for c in range(4):
                    for h in range(GH):
                        for ch in range(2):
                            r, o = c * 512 + h * P + CH * ch, h * P + CH * ch
                            last = mm(pe, ps[CH * ch:CH * ch + CH, c, o:o + CH], W(4)[:, r:r + CH], W(3)[:, r:r + CH], True, True)
                    last.then_inc(S("gatt_raw"), 1)
                pe.wait_ge(S("kdec"), 4)
                for n, (s, d, ch) in enumerate(COMBOS):
                    if n >= 2:
                        pe.wait_ge(S("state"), n - 1)
                    for h in range(GH):
                        r = (2 * s + d) * 512 + h * P
                        last = mm(pe, ps[:, 4 + 2 * (n % 2) + h // 2, (h % 2) * T:(h % 2 + 1) * T], W(0)[CH * ch:CH * ch + CH, r:r + P],
                                  xtok[CH * ch:CH * ch + CH, s, h * GV:(h + 1) * GV], True, True)
                    last.then_inc(S("kv_raw"), 1)
                pe.wait_ge(S("gatt"), 2)
                pe.wait_ge(S("state"), 6)
                for s in range(NS):
                    for h in range(GH):
                        for v in range(2):
                            i = 2 * h + v
                            b, o = 2 * s + i // 4, (i % 4) * P
                            terms = [(xtok[:, s, h * GV + v * P:h * GV + (v + 1) * P], ATT[:, s, h, :], 0, P)]
                            for d in range(2):
                                for ch in range(2):
                                    q = W(3)[:, (2 * s + d) * 512 + h * P + CH * ch:(2 * s + d) * 512 + h * P + CH * ch + CH]
                                    so = d * D + h * GV + v * P
                                    if ch != d:
                                        st = (W(2) if s == 0 else xbf)[:, so:so + P]
                                    elif s:
                                        st = W(5)[:, so:so + P]
                                    else:
                                        continue
                                    terms.append((st, q, CH * ch, CH))
                            for n, (a, q, c0, w) in enumerate(terms):
                                last = mm(pe, ps[:, b, o + c0:o + c0 + w], a, q, n == 0, n == len(terms) - 1, shared=True)
                    last.then_inc(S("gy_raw"), 1)
                pe.wait_ge(S("gsq"), 1)
                for h in range(GH):
                    for v in range(2):
                        last = mm(pe, ps[:, 4 + h // 2, (h % 2) * T:(h % 2 + 1) * T], C(MEAN_V), W(3)[:, (2 * h + v) * T:(2 * h + v + 1) * T], v == 0, v == 1)
                last.then_inc(S("gss"), 1)
                pe.wait_ge(S("gyn"), 1)
                out_project(1, lambda t: yatt[:, t, :])

            def moe(l):
                pe.wait_ge(S("h_ready"), 2 * l + 2)
                for s in range(NS):
                    for k in range(KT):
                        last = mm(pe, ps[:, 0, T + 32 * s:T + 32 * s + 20], hT[:, k, tk(s)], wr[:, l, k, :], k == 0, k == KT - 1)
                last.then_inc(S("logits"), 1)
                pe.wait_ge(S("zeroed"), 1)
                for b in range(8):
                    mm(pe, ps[:, 4 + b // 2, (b % 2) * T:(b % 2 + 1) * T], C(IDENT), zero, b % 2 == 0, True, shared=True)
                pe.wait_ge(S("sel"), l + 1)
                sel = [tiny[:, SEL + 16 * s:SEL + 16 * s + 16] for s in range(NS)]
                mm(pe, ps[:, 1, 0:16], C(LT), sel[0], True, True)
                mm(pe, ps[:, 1, 16:32], C(ONES), sel[0], True, False)
                mm(pe, ps[:, 1, 16:32], C(LT), sel[1], False, True)
                mm(pe, ps[:, 1, 32:48], C(ONES), sel[0], True, False)
                mm(pe, ps[:, 1, 32:48], C(ONES), sel[1], False, True).then_inc(S("rank_raw"), 1)
                for g in range(4):
                    if g == 1:
                        pe.wait_ge(S("rank_read"), l + 1)
                    for k in range(4):
                        last = turn(ps[:, g, k * P:(k + 1) * P], hT[:, (g % 2) * 4 + k, tk(g // 2)])
                    last.then_inc(S("htok_raw"), 1)
                pe.wait_ge(S("disp"), l + 1)
                for q in range(4):
                    pe.wait_ge(S("htok"), 4 * l + q + 1)
                    for i in range(4 * q, 4 * q + 4):
                        last = turn(ps[:, q, (i % 4) * P:(i % 4 + 1) * P], DISW[:, (i % 2) * D + (i // 2) * P:(i % 2) * D + (i // 2 + 1) * P])
                    last.then_inc(S("ct_raw"), 1)
                pe.wait_ge(S("ct"), 4 * l + 4)
                base = pos[f"moe{l}"]

                def gate_or_up(bank, xs, n0, wait, mark):
                    na = len(xs)
                    for c in range(2):
                        for a in range(na):
                            wait(n0 + c * na + a)
                        for k in range(4):
                            for a, x in enumerate(xs):
                                last = mm(pe, ps[a * CAP:(a + 1) * CAP, bank, :], x[:, 4 * c + k, :], slot(n0 + c * na + a, 4)[:, k, :],
                                          c == 0 and k == 0, c == 1 and k == 3)
                                if k == 3:
                                    mark(last)

                def down(bank, xs, n0, wait, mark):
                    na = len(xs)
                    for c in range(2):
                        for a in range(na):
                            wait(n0 + c * na + a)
                        for k in range(2):
                            for b in range(2):
                                for a, x in enumerate(xs):
                                    last = mm(pe, ps[a * CAP:(a + 1) * CAP, bank + b, :], x[:, 2 * c + k, :],
                                              slot(n0 + c * na + a, 2)[:, k, b * 512:(b + 1) * 512], c == 0 and k == 0, c == 1 and k == 1)
                                    if k == 1 and b == 1:
                                        mark(last)

                def gather(i):
                    for k in range(KT):
                        for s in range(NS):
                            last = mm(pe, ps[:, k // 4, (k % 4) * P:(k % 4 + 1) * P], xtok[:, s, k * P:(k + 1) * P],
                                      DISP[:, bass.ds(i * P + s * D, P)], s == 0, s == 1)
                    last.then_inc(S("gathered"), 1)

                def scatter(i):
                    for m in range(KT):
                        last = mm(pe, ps[:, 4 + m // 2, (m % 2) * T:(m % 2 + 1) * T], YS[:, m * P:(m + 1) * P],
                                  CT[:, bass.ds(i, 1), :], False, False, shared=True)
                    last.then_inc(S("scattered"), 1)

                def pair(i, first=False, final=False):
                    def wait(n):
                        wait_landed(pe, n, i * (2 * PER_EXPERT // RING))
                    done = i + (l * PAIRS)
                    pe.wait_ge(S("hg"), done * 2 + 2)
                    x = [HG[:, :, a * CAP:(a + 1) * CAP] for a in range(2)]
                    gate_or_up(2, x, base, wait, used)
                    if l == 0:
                        pe.wait_ge(S("mods"), i + 2)
                    gate_or_up(3, x, base + 4, wait, used)
                    if not first:
                        pe.wait_ge(S("ys"), done * 2)
                    if not final:
                        gather(i + 1)
                    pe.wait_ge(S("hact"), done + 1)
                    for f in range(FT):
                        last = turn(ps[:, 2, f * P:(f + 1) * P], HACT[:, f * P:(f + 1) * P])
                    last.then_inc(S("ht_raw"), 1)
                    if l == 0:
                        for c in range(per_pair):
                            ada(3, 4 * c, a_sums[1][:, c], n_ada + c, i)
                    if not first:
                        scatter(i - 1)
                    pe.wait_ge(S("ht"), done + 1)
                    if not final:
                        pe.wait_ge(S("hg"), done * 2 + 4)
                    down(0, [HT[:, :, a * CAP:(a + 1) * CAP] for a in range(2)], base + 8, wait, used)

                gather(0)
                pair(0, first=True)
                with pe.Fori(1, PAIRS - 1) as i:
                    pair(i)
                pair(PAIRS - 1, final=True)
                pe.wait_ge(S("ys"), (l + 1) * PAIRS * 2)
                scatter(PAIRS - 1)

                pe.wait_ge(S("need"), l + 1)
                most = pe.value_load(need[0:1, l:l + 1], min_val=0, max_val=T)
                with pe.If(most > CAP):
                    pe.sem_inc(S(f"o{l}_used"), PER_EXPERT)
                    with pe.Fori(0, NE) as e:
                        with pe.Fori(1, T // CAP) as r:
                            it = e * (T // CAP - 1) + r

                            def wait(n):
                                pe.wait_ge(S(f"o{l}_landed{n % RING}"), it * 16)

                            def mark(ins):
                                ins.then_inc(S(f"o{l}_used"), 1)
                            pe.wait_ge(S(f"o{l}_v"), it * O_STEPS + (1 - O_STEPS))
                            for k in range(KT):
                                for s in range(NS):
                                    last = mm(pe, ps[:, 0, k * CAP:(k + 1) * CAP], xtok[:, s, k * P:(k + 1) * P],
                                              O_DISP[:, s * CAP:(s + 1) * CAP], s == 0, s == 1)
                            last.then_inc(S(f"o{l}_p"), 1)
                            for s in range(NS):
                                last = mm(pe, ps[0:CAP, 1, tk(s)], O_DISW[:, s * CAP:(s + 1) * CAP], C(IDENT), True, True)
                            last.then_inc(S(f"o{l}_p"), 1)
                            pe.wait_ge(S(f"o{l}_v"), it * O_STEPS + (3 - O_STEPS))
                            gate_or_up(2, [O_HG], 0, wait, mark)
                            gate_or_up(3, [O_HG], 2, wait, mark)
                            pe.wait_ge(S(f"o{l}_v"), it * O_STEPS + (4 - O_STEPS))
                            for f in range(FT):
                                last = mm(pe, ps[:, 1, f * CAP:(f + 1) * CAP], O_ACT[:, f * P:(f + 1) * P], cst[0:CAP, IDENT, 0:CAP], True, True)
                            last.then_inc(S(f"o{l}_p"), 1)
                            pe.wait_ge(S(f"o{l}_v"), it * O_STEPS + (5 - O_STEPS))
                            down(2, [O_HT], 4, wait, mark)
                            pe.wait_ge(S(f"o{l}_v"), it * O_STEPS)
                            for m in range(KT):
                                last = mm(pe, ps[:, 4 + m // 2, (m % 2) * T:(m % 2 + 1) * T], O_YS[:, m * P:(m + 1) * P],
                                          O_CT, False, False, shared=True)
                            last.then_inc(S(f"o{l}_p"), 1)

            pe.wait_ge(S("csilu"), 2)
            for n in range(n_first):
                ada0(n)
            norm(0)
            even()
            norm(1)
            moe(0)
            norm(2)
            odd()
            norm(3)
            moe(1)
            norm(4)
            pe.wait_ge(S("h_ready"), 5)
            for g in range(4):
                for k in range(4):
                    last = turn(ps[:, 1 + g, k * P:(k + 1) * P], hT[:, (g % 2) * 4 + k, tk(g // 2)])
                last.then_inc(S("y_turned"), 1)

        @block.scalar
        def _(act):
            def load(dst, src, name):
                act.dma_start(dst, src).then_inc(S(name), 16)

            load(cst[:, :, :], A["consts"], "consts_in")
            for lo, src in ((BADA, A["b_ada"].rearrange("l (r p) -> (l r) p", p=P)),
                            (NMIX, A["norm_mix_w"].rearrange("l (r p) -> (l r) p", p=P)),
                            (NFFN, A["norm_ffn_w"].rearrange("l (r p) -> (l r) p", p=P)),
                            (CONVW, A["conv_w"][0].rearrange("t (r p) -> (t r) p", p=P)),
                            (CONVB, A["conv_b"][0].rearrange("(r p) -> r p", p=P)),
                            (SSDN, A["ssd_norm_w"][0].rearrange("(r p) -> r p", p=P)),
                            (GLAN, A["gla_norm_w"][0].rearrange("(r p) -> r p", p=P)),
                            (FINN, A["final_norm_w"].rearrange("(r p) -> r p", p=P)),
                            (CVEC, A["c"][0].rearrange("(r p) -> r p", p=P)),
                            (CCTX, A["c_ctx"].rearrange("(r p) -> r p", p=P))):
                load(rows[lo % P:lo % P + src.shape[0], lo // P, :], src, "rows_in")
            load(xtok[:, 0, :], A["x_prompt"][0], "x_in")
            load(xtok[:, 1, :], A["x_sample"][0], "x_in")
            for d, name in enumerate(("state_ssd_fwd", "state_ssd_bwd")):
                load(W(2)[:, d * D:(d + 1) * D].rearrange("p (i n) -> p i n", i=8),
                     A[name][0, 0].rearrange("(i a) q n -> (a q) i n", a=2), "h0_in")
            act.wait_ge(S("feat_ready"), 1)
            act.activation(csilu[:, :, 0], feat[:, CCTX:CCTX + KT], ACT.Silu).then_inc(S("csilu"), 1)
            act.activation(csilu[:, :, 1], feat[:, CVEC:CVEC + KT], ACT.Silu).then_inc(S("csilu"), 1)

            def norm(i):
                act.wait_ge(S("x_ready"), i + 1)
                if i == 3:
                    act.wait_ge(S("gla_stored"), 32)
                act.activation(hT[:, :, :], xT[:, :, :], ACT.Square).then_inc(S("sq"), 1)
                act.wait_ge(S("eps"), 1)
                act.wait_ge(S("ss"), i + 1)
                act.activation(rstd[:, 0, :], ps[:, 0, 0:T], ACT.Sqrt, bias=eps[:, :]).then_inc(S("rms"), 1)

            def even():
                act.wait_ge(S("dt_abs"), 1)
                act.activation(tiny[:, DTE:DTE + 64], tiny[:, DTT:DTT + 64], ACT.Exp, scale=-1.0).then_inc(S("dt_exp"), 1)
                act.activation(alog[:, :], alog[:, :], ACT.Exp).then_inc(S("dt_exp"), 1)
                act.wait_ge(S("dt_u"), 1)
                act.activation(tiny[:, DTL:DTL + 64], tiny[:, DTU:DTU + 64], ACT.Ln).then_inc(S("dt_ln"), 1)
                for j in range(16):
                    act.wait_ge(S("slot_used"), pos["in0"] + j + 1)
                    b = ps[:, 1 + j % 4, :]
                    b2 = b.rearrange("p (a t) -> p a t", a=2)
                    if j == 0:
                        act.wait_ge(S("pad_zero"), 1)
                    dst, src, f = ((xpad[:, 2 * j:2 * j + 2, :, 2:2 + P], b.rearrange("p (a s t) -> p a s t", a=2, s=NS), ACT.Copy) if j < 6 else
                                   (kv[:, :, (j - 6) * 256:(j - 5) * 256], b2, ACT.Copy) if j < 8 else
                                   (qT[:, 2 * (j - 8):2 * (j - 8) + 2, :], b2, ACT.Copy) if j < 12 else
                                   (zs[:, 2 * (j - 12):2 * (j - 12) + 2, :], b2, ACT.Silu))
                    act.activation(dst, src, f).then_inc(S("proj_free"), 1)
                    if 6 <= j < 12:
                        p = 2 * (j - 6)
                        act.wait_ge(S("conv_done"), p + 2)
                        act.activation(xbc[:, p:p + 2, :], xbc[:, p:p + 2, :], ACT.Silu).then_inc(S("xbc_ready"), 1)
                    if j == 7:
                        act.wait_ge(S("proj_free"), 8)
                        act.dma_start(O[2][0, 0].rearrange("t h d -> t (h d)"), kv[:, 0, 0:256]).then_inc(S("cache_stored"), 16)
                        act.dma_start(O[3][0, 0].rearrange("t h d -> t (h d)"), kv[:, 0, 256:512]).then_inc(S("cache_stored"), 16)
                for g in range(5):
                    act.wait_ge(S("tok_turned"), g + 1)
                    dst = xtok[:, g // 2, (g % 2) * 512:(g % 2 + 1) * 512] if g < 4 else btok[:, :]
                    act.activation(dst, ps[:, 5 + g % 3, 0:512 if g < 4 else 256], ACT.Copy).then_inc(S("tok_copied"), 1)
                for g in range(4):
                    act.wait_ge(S("h0_turned"), g + 1)
                    act.activation(hTf[:, g * 512:(g + 1) * 512], ps[:, 1 + g, :], ACT.Copy).then_inc(S("h0_copied"), 1)
                act.wait_ge(S("te_raw"), 1)
                act.activation(tiny[:, TE:TE + 32], ps[:, 7, 256:288], ACT.Exp).then_inc(S("te_exp"), 1)
                unit = 0
                for s in range(NS):
                    if s:
                        act.wait_ge(S("y_raw"), 1)
                    for d in range(2):
                        for w in range(1 + s):
                            for q in range(4):
                                act.wait_ge(S("seg_raw"), unit + 1)
                                act.activation(W(2 * w + d)[:, q * 512:(q + 1) * 512], ps[:, 1 + unit % 4, :], ACT.Exp).then_inc(S("seg_exp"), 1)
                                unit += 1
                    if s == 0:
                        for q in range(4):
                            act.wait_ge(S("st_raw"), q + 1)
                            act.activation(yaf[:, q * 512:(q + 1) * 512], ps[:, 1 + q, :], ACT.Copy).then_inc(S("st_copied"), 1)
                        act.wait_ge(S("st_copied"), 4)
                        for d in range(2):
                            act.dma_start(O[4 + d][0, 0].rearrange("(i a) q n -> (a q) i n", a=2),
                                          yaf[:, d * D:(d + 1) * D].rearrange("p (i n) -> p i n", i=8)).then_inc(S("ssd_stored"), 16)
                act.wait_ge(S("y_gated"), 2)
                act.activation(W(4), zs[:, :, :].rearrange("p k t -> p (k t)"), ACT.Square).then_inc(S("ysq"), 1)
                act.wait_ge(S("yss"), 1)
                act.activation(rstd[:, 1, :], ps[:, 0, 0:T], ACT.Sqrt, bias=eps[:, :]).then_inc(S("yrms"), 1)
                for n, dst in enumerate((KTC, KTL, KTP)):
                    act.wait_ge(S("keys_turned"), n + 1)
                    act.activation(dst, ps[:, 1 + n, :], ACT.Copy).then_inc(S("keys_copied"), 1)
                for g in range(3):
                    nh, w = (8, 256) if g else (16, 128)
                    act.wait_ge(S("negm"), g + 1)
                    sc = ps[:, 0:4, :].rearrange("p b (h w) -> p (b h) w", w=w)
                    pr = W(0).rearrange("p (h w) -> p h w", w=w)
                    if g:
                        act.wait_ge(S("probs_turned"), g)
                    for h in range(nh):
                        act.activation(pr[:, h, :], sc[:, h, :], ACT.Exp, scale=SCALE, bias=tiny[:, NEGM + h:NEGM + h + 1],
                                       accum_out=tiny[:, RSUM + h:RSUM + h + 1]).then_inc(S("p_exp"), 1)
                    act.activation(tiny[:, SNKE:SNKE + nh], tiny[:, SNKD:SNKD + nh], ACT.Exp).then_inc(S("p_exp"), 1)
                    act.wait_ge(S("probs_turned"), g + 1)
                    if g:
                        act.wait_ge(S("att_raw"), g)
                    for q in range(4):
                        act.activation(W(1)[:, q * 512:(q + 1) * 512], ps[:, 4 + q, :], ACT.Copy).then_inc(S("pT_copied"), 1)
                    act.wait_ge(S("att_raw"), g + 1)
                    if g == 0:
                        act.wait_ge(S("ssd_stored"), 32)
                        for b in range(2):
                            act.activation(yatt[:, 4 * b:4 * b + 4, tk(0)], ps[:, b, :].rearrange("p (a t) -> p a t", a=4), ACT.Copy).then_inc(S("yatt"), 1)
                    else:
                        act.activation(yatt[:, 4 * (g - 1):4 * g, tk(1)], ps[:, 0, :].rearrange("p (a t) -> p a t", a=4), ACT.Copy).then_inc(S("yatt"), 1)

            def odd():
                for d, name in enumerate(("state_gla_fwd", "state_gla_bwd")):
                    load(W(5)[:, d * D:(d + 1) * D].rearrange("p (h v) -> p h v", h=GH),
                         A[name][0, 0].rearrange("h k v -> k h v"), "s0_in")
                act.wait_ge(S("lr_raw"), 1)
                act.wait_ge(S("lr_ones"), 1)
                act.activation(lr[0:LOWRANK, :], ps[0:16, 0, :], ACT.Copy).then_inc(S("lr"), 1)
                for j in range(12):
                    act.wait_ge(S("slot_used"), pos["in1"] + j + 1)
                    b2 = ps[:, 1 + j % 4, :].rearrange("p (a t) -> p a t", a=2)
                    dst, f = ((qT[:, 2 * j:2 * j + 2, :], ACT.Copy) if j < 2 else
                              (kv[:, :, (j - 2) * 256:(j - 1) * 256], ACT.Copy) if j < 4 else
                              (xtok[:, :, (j - 4) * 256:(j - 3) * 256], ACT.Copy) if j < 8 else
                              (zs[:, 2 * (j - 8):2 * (j - 8) + 2, :], ACT.Silu))
                    act.activation(dst, b2, f).then_inc(S("proj_free"), 1)
                act.wait_ge(S("gate_abs"), 4)
                act.activation(W(1), W(1), ACT.Exp, scale=-1.0).then_inc(S("gate_exp"), 1)
                act.wait_ge(S("gate_exp"), 1)
                act.activation(W(1), W(1), ACT.Ln, bias=1.0).then_inc(S("gate_exp"), 1)
                act.wait_ge(S("g_ready"), 4)
                for c in range(4):
                    act.wait_ge(S("cs_raw"), c + 1)
                    act.activation(W(1)[:, c * 512:(c + 1) * 512], ps[:, c, :], ACT.Exp).then_inc(S("ecs"), 1)
                    act.activation(W(2)[:, c * 512:(c + 1) * 512], ps[:, c, :], ACT.Exp, scale=-1.0).then_inc(S("ecs"), 1)
                act.wait_ge(S("rest_raw"), 4)
                for c in range(4):
                    act.activation(W(0)[:, c * 512:(c + 1) * 512], ps[:, 4 + c, :], ACT.Exp).then_inc(S("kde"), 1)
                act.wait_ge(S("state"), 4)
                for d in range(2):
                    act.dma_start(O[6 + d][0, 0].rearrange("h k v -> k h v"),
                                  hTf[:, d * D:(d + 1) * D].rearrange("p (h v) -> p h v", h=GH)).then_inc(S("gla_stored"), 16)
                act.wait_ge(S("gy"), 2)
                act.activation(W(3), yaf, ACT.Square).then_inc(S("gsq"), 1)
                act.wait_ge(S("gss"), 1)
                act.activation(rstd[:, :, :].rearrange("p (b h) t -> p b (h t)", b=2), ps[:, 4:6, :], ACT.Sqrt, bias=eps[:, :]).then_inc(S("grms"), 1)

            def moe(l):
                act.wait_ge(S("g_sub"), l + 1)
                act.activation(tiny[:, GEX:GEX + 8], tiny[:, GEX:GEX + 8], ACT.Exp).then_inc(S("g_exp"), 1)
                act.wait_ge(S("e_sub"), l + 1)
                act.activation(tiny[:, EL:EL + 8], tiny[:, EL:EL + 8], ACT.Exp).then_inc(S("e_exp"), 1)
                for g in range(4):
                    act.wait_ge(S("htok_raw"), 4 * l + g + 1)
                    act.activation(xtok[:, g // 2, (g % 2) * 512:(g % 2 + 1) * 512], ps[:, g, :], ACT.Copy).then_inc(S("htok"), 1)
                for q in range(4):
                    act.wait_ge(S("ct_raw"), 4 * l + q + 1)
                    act.activation(W(0)[:, q * 512:(q + 1) * 512], ps[:, q, :], ACT.Copy).then_inc(S("ct"), 1)
                base = pos[f"moe{l}"]
                def hg(n):
                    act.wait_ge(S("gathered"), n)
                    act.activation(W(1)[:, 0:512], ps[:, 0, :], ACT.Copy).then_inc(S("hg"), 1)

                def ys(i):
                    act.wait_ge(S("slot_used"), i * (2 * PER_EXPERT) + (base + 12))
                    act.activation(YS[:, 0:512], ps[:, 0, :], ACT.Copy).then_inc(S("ys"), 1)

                def pair(i, first=False, final=False):
                    done = i + (l * PAIRS)
                    if not first:
                        ys(i - 1)
                    act.wait_ge(S("slot_used"), i * (2 * PER_EXPERT) + (base + 4))
                    act.activation(SIL, ps[:, 2, :], ACT.Silu).then_inc(S("sil"), 1)
                    if not final:
                        hg(done + 2)
                    act.wait_ge(S("ht_raw"), done + 1)
                    act.activation(HT, ps[:, 2, :].rearrange("p (f c) -> p f c", f=FT), ACT.Copy).then_inc(S("ht"), 1)

                hg(l * PAIRS + 1)
                pair(0, first=True)
                with act.Fori(1, PAIRS - 1) as i:
                    pair(i)
                pair(PAIRS - 1, final=True)
                ys(PAIRS - 1)
                act.wait_ge(S("need"), l + 1)
                most = act.value_load(need[0:1, l:l + 1], min_val=0, max_val=T)
                with act.If(most > CAP):
                    with act.Fori(1, NE * (T // CAP - 1) + 1) as it:
                        act.wait_ge(S(f"o{l}_used"), it * PER_EXPERT + 2)
                        act.activation(O_SIL, ps[0:CAP, 2, :], ACT.Silu).then_inc(S(f"o{l}_a"), 1)

            norm(0)
            even()
            norm(1)
            moe(0)
            norm(2)
            odd()
            norm(3)
            moe(1)
            norm(4)
            for g in range(4):
                act.wait_ge(S("y_turned"), g + 1)
                act.activation(xtok[:, g // 2, (g % 2) * 512:(g % 2 + 1) * 512], ps[:, 1 + g, :], ACT.Copy).then_inc(S("y_tok"), 1)
            act.wait_ge(S("cache_stored"), 32)

        @block.vector
        def _(dve):
            step = stepper(dve, "dve_step")
            tt, ts, stt = dve.tensor_tensor, dve.tensor_scalar, dve.scalar_tensor_tensor

            def t2(c, n, s=NS):
                return tiny[:, c:c + s * n].rearrange("p (s n) -> p s n", s=s)

            dve.memset(eps[:, :], EPS).then_inc(S("eps"), 1)
            for i in range(4):
                dve.memset(pref[:, i:i + 1], float(4 - i)).then_inc(S("pref"), 1)
            dve.wait_ge(S("rows_turned"), 1)
            dve.memset(lr[:, :], 1.0).then_inc(S("lr_ones"), 1)
            dve.memset(zero, 0.0).then_inc(S("zeroed"), 1)
            dve.tensor_copy(feat[:, 0:234], ps[:, 0, 0:234]).then_inc(S("feat_ready"), 1)
            for g in range(4):
                dve.wait_ge(S("x_turned"), g + 1)
                step(dve.tensor_copy(xT[:, (g % 2) * 4:(g % 2) * 4 + 4, tk(g // 2)], ps[:, 1 + g, :].rearrange("p (k t) -> p k t", k=4)))
            dve.wait_ge(S("small_in"), SMALL)
            step(dve.tensor_copy(dsk[0:64, :], dskb[0:64, :].rearrange("p (i a) -> p a i", a=2)[:, 0, :]))
            dve.tensor_copy(dsk[64:128, :], dskb[64:128, :].rearrange("p (i a) -> p a i", a=2)[:, 1, :]).then_inc(S("x_ready"), 1)
            dve.wait_ge(S("x_ready"), 1)

            def ada(l, n, rounds=0):
                src = a_slots[l][n % 3].rearrange("p (k n) -> p k n", k=KT)
                dve.wait_ge(S(f"ada_landed{n % 3}"), rounds * 16 + 16 * (n // 3 + 1))
                before = (n - 3) if l == 0 else (n - 2)
                if before > 0:
                    dve.wait_ge(S("mac_summed"), rounds * per_pair + before)
                start = summed(n - 1) if n else 0
                for k in range(dve_tiles(n)):
                    for g in range(NS):
                        out = a_sums[l][:, n % 4 if l == 0 else n % 3, g]
                        c = csilu[:, k, g:g + 1]
                        if k:
                            dve.wait_ge(S("mac"), rounds * (per_pair * KT * NS) + (start + 2 * k + g - 1))
                            ins = stt(out, src[:, k, :], c, out, ALU.mult, ALU.add)
                        else:
                            ins = ts(out, src[:, k, :], c, None, ALU.mult)
                        ins.then_inc(S("mac"), 1)

            def scales(l, c, w):
                return stt(mods[:, l, c:c + 8], mods[:, l, c:c + 8], 1.0,
                           feat[:, w + 8 * l:w + 8 * l + 8][:, :, None].broadcast_to([P, 8, NS]), ALU.add, ALU.mult)

            def ada0_done(n0, n1):
                dve.wait_ge(S("mac_summed"), n1)
                tt(mods[:, 0, 2 * n0:2 * n1], ps[:, 0, ADA + 4 * n0:ADA + 4 * n1].rearrange("p (r s) -> p r s", s=NS),
                   feat[:, BADA + 2 * n0:BADA + 2 * n1][:, :, None].broadcast_to([P, 2 * (n1 - n0), NS]), ALU.add).then_inc(S("mods"), 1)
                dve.wait_ge(S("mods"), 1 if n0 == 0 else 2)
                step(scales(0, *((8, NMIX) if n0 == 0 else (32, NFFN))))

            def norm(i):
                dve.wait_ge(S("rms"), i + 1)
                step(dve.reciprocal(rstd[:, 0, :], rstd[:, 0, :]))
                step(tt(hT[:, :, :], xT[:, :, :], rstd[:, 0:1, :].broadcast_to([P, KT, T]), ALU.mult))
                if i == 4:
                    for k in range(KT):
                        last = ts(hT[:, k, :], hT[:, k, :], feat[:, FINN + k:FINN + k + 1], None, ALU.mult)
                        if k < KT - 1:
                            step(last)
                else:
                    l, c = i // 2, 24 * (i % 2)
                    for k in range(KT):
                        for s in range(NS):
                            last = ts(hT[:, k, tk(s)], hT[:, k, tk(s)], mods[:, l, c + 8 + k, s:s + 1], mods[:, l, c + k, s:s + 1], ALU.mult, ALU.add)
                            if (k, s) != (KT - 1, 1):
                                step(last)
                last.then_inc(S("h_ready"), 1)
                dve.wait_ge(S("h_ready"), i + 1)

            def residual(l, c, count):
                for k in range(KT):
                    for s in range(NS):
                        last = stt(xT[:, k, tk(s)], ps[:, 4 + k // 2, (k % 2) * T + s * P:(k % 2) * T + (s + 1) * P],
                                   mods[:, l, c + k, s:s + 1], xT[:, k, tk(s)], ALU.mult, ALU.add)
                        if (k, s) != (KT - 1, 1):
                            step(last)
                last.then_inc(S("x_ready"), 1)
                dve.wait_ge(S("x_ready"), count)

            def even():
                dve.wait_ge(S("dt_raw"), 1)
                X, TM, EX, U1, LN = (tiny[:, c:c + 64] for c in (DTX, DTT, DTE, DTU, DTL))
                step(tt(t2(DTX, 32), ps[:, 0, T:T + 64].rearrange("p (s n) -> p s n", s=NS), dtb[:, None, :].broadcast_to([P, NS, 32]), ALU.add))
                stt(TM, X, -1.0, X, ALU.mult, ALU.max).then_inc(S("dt_abs"), 1)
                dve.wait_ge(S("dt_exp"), 2)
                ts(U1, EX, 1.0, None, ALU.add).then_inc(S("dt_u"), 1)
                dve.wait_ge(S("dt_u"), 1)
                step(stt(TM, U1, -1.0, EX, ALU.add, ALU.subtract))
                step(dve.reciprocal(EX, U1))
                step(tt(TM, TM, EX, ALU.mult))
                dve.wait_ge(S("dt_ln"), 1)
                step(tt(TM, LN, TM, ALU.subtract))
                step(stt(tiny[:, DT:DT + 64], X, 0.0, TM, ALU.max, ALU.add))
                stt(t2(DTA, 32), t2(DT, 32), -1.0, alog[:, None, :].broadcast_to([P, NS, 32]), ALU.mult, ALU.mult).then_inc(S("dtA"), 1)
                for t in range(2 * len(IN[0])):
                    if t % 2 == 0 and t:
                        ada(0, n_first + t // 2 - 1)
                    if t >= CONV_TILES:
                        continue
                    dve.wait_ge(S("proj_free"), t // 2 + 1)
                    acc = xbc[:, t, :].rearrange("p (s t) -> p s t", s=NS)
                    cw = CONVW + t
                    step(ts(acc, xpad[:, t, :, 0:P], feat[:, cw:cw + 1], feat[:, CONVB + t:CONVB + t + 1], ALU.mult, ALU.add))
                    for j in range(1, TAPS):
                        last = stt(acc, xpad[:, t, :, j:j + P], feat[:, cw + CONV_TILES * j:cw + CONV_TILES * j + 1], acc, ALU.mult, ALU.add)
                        if j < TAPS - 1:
                            step(last)
                    last.then_inc(S("conv_done"), 1)
                ada(0, n_ada - 1)
                ada0_done(n_first, n_ada)
                for s in range(NS):
                    dve.wait_ge(S("tok_copied"), 5)
                    if s:
                        dve.wait_ge(S("y_raw"), 1)
                    for d in range(2):
                        step(tt(W(4)[:, d * D:(d + 1) * D].rearrange("p (h q) -> p h q", h=HEADS), heads(xtok[:, s, :]),
                                tiny[:, DT + 32 * s + 16 * d:DT + 32 * s + 16 * d + 16][:, :, None].broadcast_to([P, HEADS, HP]), ALU.mult))
                    if s == 0:
                        dve.wait_ge(S("te_exp"), 1)
                        for d in range(2):
                            last = tt(W(3)[:, d * D:(d + 1) * D].rearrange("p (h q) -> p h q", h=HEADS), W(4)[:, d * D:(d + 1) * D].rearrange("p (h q) -> p h q", h=HEADS),
                                      tiny[:, TE + 16 * d:TE + 16 * d + 16][:, :, None].broadcast_to([P, HEADS, HP]), ALU.mult)
                            if d == 0:
                                step(last)
                        last.then_inc(S("xw_ready"), 1)
                    dve.wait_ge(S("cb_raw"), s + 1)
                    cb = ps[:, 0, 0:2 * P].rearrange("p (g t) -> p g t", g=2)
                    for d in range(2):
                        last = tt(tiny[:, CBM + 256 * d:CBM + 256 * d + 256].rearrange("p (g t) -> p g t", g=2), cb,
                                  C(GE if d else LE)[:, None, :].broadcast_to([P, 2, P]), ALU.mult)
                        if d == 0:
                            step(last)
                    last.then_inc(S("cbm"), 1)
                    dve.wait_ge(S("cbm"), s + 1)
                    for d in range(2):
                        dve.wait_ge(S("seg_exp"), (8 + 8 * d + 4) if s else 4 * (d + 1))
                        for g in range(2):
                            m = W(d)[:, g * D:(g + 1) * D].rearrange("p (h t) -> p h t", h=8)
                            last = tt(m, m, tiny[:, CBM + 256 * d + P * g:CBM + 256 * d + P * g + P][:, None, :].broadcast_to([P, 8, P]), ALU.mult)
                            if s or (d, g) != (1, 1):
                                step(last)
                        if s:
                            dve.wait_ge(S("seg_exp"), 8 + 8 * d + 8)
                            for g in range(2):
                                m = W(2 + d)[:, g * D:(g + 1) * D].rearrange("p (h t) -> p h t", h=8)
                                last = tt(m, m, xbc[:, 10 + g, tk(1)][:, None, :].broadcast_to([P, 8, P]), ALU.mult)
                                if (d, g) != (1, 1):
                                    step(last)
                    last.then_inc(S("M_ready"), 1)
                    dve.wait_ge(S("y_raw"), s + 1)
                    for i in range(KT):
                        step(stt(xbc[:, i, tk(s)], xbc[:, i, tk(s)], dsk[:, i:i + 1], ps[:, 5 + i // 4, (i % 4) * P:(i % 4 + 1) * P], ALU.mult, ALU.add))
                    dve.wait_ge(S("proj_free"), 16)
                    tt(zs[:, :, tk(s)], zs[:, :, tk(s)], xbc[:, 0:KT, tk(s)], ALU.mult).then_inc(S("y_gated"), 1)
                dve.wait_ge(S("yrms"), 1)
                step(dve.reciprocal(rstd[:, 1, :], rstd[:, 1, :]))
                for k in range(KT):
                    last = stt(zs[:, k, :], zs[:, k, :], feat[:, SSDN + k:SSDN + k + 1], rstd[:, 1, :], ALU.mult, ALU.mult)
                    if k < KT - 1:
                        step(last)
                last.then_inc(S("yssd"), 1)
                dve.wait_ge(S("rotated"), 1)
                dve.wait_ge(S("keys_copied"), 2)
                q8 = QR.rearrange("p (k t) -> p k t", k=KT)
                w8 = W(2)[:, 0:D].rearrange("p (k t) -> p k t", k=KT)
                step(tt(w8, ps[:, 5:7, :].rearrange("p b (k t) -> p (b k) t", k=4), C(SIN)[:, None, :].broadcast_to([P, KT, P]), ALU.mult))
                step(tt(q8, qT[:, :, tk(1)], C(COS)[:, None, :].broadcast_to([P, KT, P]), ALU.mult))
                step(tt(q8, q8, w8, ALU.add))
                k4 = KR.rearrange("p (k t) -> p k t", k=4)
                w4 = W(2)[:, D:D + 512].rearrange("p (k t) -> p k t", k=4)
                step(tt(w4, ps[:, 4, :].rearrange("p (k t) -> p k t", k=4), C(SIN)[:, None, :].broadcast_to([P, 4, P]), ALU.mult))
                step(tt(k4, KTL.rearrange("p (k t) -> p k t", k=4), C(COS)[:, None, :].broadcast_to([P, 4, P]), ALU.mult))
                tt(k4, k4, w4, ALU.add).then_inc(S("rope"), 1)
                done = 0
                for g in range(3):
                    nh, w = (8, 256) if g else (16, 128)
                    h0 = 8 * (g - 1) if g else 0
                    dve.wait_ge(S("scores"), g + 1)
                    sc = ps[:, 0:4, :].rearrange("p b (h w) -> p (b h) w", w=w)
                    step(dve.tensor_reduce(tiny[:, MX:MX + nh], sc, AX.X, ALU.max))
                    sk = sink[:, h0:h0 + nh].rearrange("p (i a) -> p a i", a=2)

                    def eo(c):
                        return tiny[:, c:c + nh].rearrange("p (a i) -> p a i", a=2)
                    step(stt(eo(MX), eo(MX), SCALE, sk, ALU.mult, ALU.max))
                    step(ts(tiny[:, NEGM:NEGM + nh], tiny[:, MX:MX + nh], -1.0, None, ALU.mult))
                    tt(eo(SNKD), sk, eo(MX), ALU.subtract).then_inc(S("negm"), 1)
                    done += nh + 1
                    dve.wait_ge(S("p_exp"), done)
                    step(tt(tiny[:, RINV:RINV + nh], tiny[:, RSUM:RSUM + nh], tiny[:, SNKE:SNKE + nh], ALU.add))
                    step(dve.reciprocal(tiny[:, RINV:RINV + nh], tiny[:, RINV:RINV + nh]))
                    pr = W(0).rearrange("p (h w) -> p h w", w=w)
                    tt(pr, pr, tiny[:, RINV:RINV + nh][:, :, None].broadcast_to([P, nh, w]), ALU.mult).then_inc(S("probs"), 1)
                dve.wait_ge(S("slot_used"), pos["out0"] + n_out[0])
                residual(0, 16, 2)

            def odd():
                step(dve.memset(xpf[:, 0:1024], 0.0))
                for s in range(NS):
                    dve.wait_ge(S("gk_turned"), s + 1)
                    dve.tensor_copy(qT[:, 4:8, tk(s)], ps[:, 5 + s, :].rearrange("p (h t) -> p h t", h=GH)).then_inc(S("gk_copied"), 1)
                for c in range(4):
                    dve.wait_ge(S("gate_raw"), c + 1)
                    x, y = W(0)[:, c * 512:(c + 1) * 512], W(1)[:, c * 512:(c + 1) * 512]
                    step(dve.tensor_copy(x, ps[:, (5 + c) % 8, :]))
                    stt(y, x, -1.0, x, ALU.mult, ALU.max).then_inc(S("gate_abs"), 1)
                dve.wait_ge(S("gate_exp"), 2)
                for c in range(4):
                    x, y = W(0)[:, c * 512:(c + 1) * 512], W(1)[:, c * 512:(c + 1) * 512]
                    stt(x, x, 0.0, y, ALU.min, ALU.subtract).then_inc(S("g_ready"), 1)
                dve.wait_ge(S("gk_copied"), 2)
                dve.wait_ge(S("proj_free"), 16 + 4)
                for c in range(4):
                    dve.wait_ge(S("ecs"), 2 * c + 2)
                    s = c // 2

                    def h4(i):
                        return W(i)[:, c * 512:(c + 1) * 512].rearrange("p (h t) -> p h t", h=GH)
                    step(stt(h4(3), qT[:, 0:4, tk(s)], GLA_SCALE, h4(1), ALU.mult, ALU.mult))
                    tt(h4(4), qT[:, 4:8, tk(s)], h4(2), ALU.mult).then_inc(S("qk_ready"), 1)
                for c in range(4):
                    dve.wait_ge(S("kde"), c + 1)
                    x = W(0)[:, c * 512:(c + 1) * 512]
                    tt(x, x, kv[:, c // 2, :], ALU.mult).then_inc(S("kdec"), 1)
                for s in range(NS):
                    for d in range(2):
                        dve.wait_ge(S("gatt_raw"), 2 * s + d + 1)
                        for ch in range(2):
                            r = slice(CH * ch, CH * ch + CH)
                            src = ps[r, 2 * s + d, :].rearrange("p (h t) -> p h t", h=GH)[:, :, r]
                            step(tt((ATB if d else ATT)[r, s, :, r], src, cst[r, GE if d else LE, r][:, None, :].broadcast_to([CH, GH, CH]), ALU.mult))
                    for ch in range(2):
                        r = slice(CH * ch, CH * ch + CH)
                        last = tt(ATT[r, s, :, r], ATT[r, s, :, r], ATB[r, s, :, r], ALU.add)
                        if ch == 0:
                            step(last)
                    last.then_inc(S("gatt"), 1)
                dve.wait_ge(S("s0_in"), 32)
                for n, (s, d, ch) in enumerate(COMBOS):
                    dve.wait_ge(S("kv_raw"), n + 1)
                    b = 4 + 2 * (n % 2)
                    first = ch == d
                    dst = (W(2) if s == 0 else xbf) if first else hTf
                    if s == 0 and first:
                        dve.tensor_copy(dst[:, d * D:(d + 1) * D].rearrange("p (b w) -> p b w", b=2), ps[:, b:b + 2, :]).then_inc(S("state"), 1)
                        dve.wait_ge(S("state"), n + 1)
                    else:
                        before = W(5) if s else W(2)
                        for h in range(GH):
                            o = d * D + h * GV
                            dec = (2 * s + d) * 512 + h * P + CH * ch + (0 if d else CH - 1)
                            last = stt(dst[:, o:o + GV], before[:, o:o + GV], W(1)[:, dec:dec + 1],
                                       ps[:, b + h // 2, (h % 2) * T:(h % 2 + 1) * T], ALU.mult, ALU.add)
                            if h < GH - 1:
                                step(last)
                        last.then_inc(S("state"), 1)
                for s in range(NS):
                    dve.wait_ge(S("gy_raw"), s + 1)
                    dve.tensor_copy(yatt[:, :, tk(s)], ps[:, 2 * s:2 * s + 2, :].rearrange("p b (k t) -> p (b k) t", k=4)).then_inc(S("gy"), 1)
                dve.wait_ge(S("grms"), 1)
                step(dve.reciprocal(rstd[:, :, :], rstd[:, :, :]))
                for i in range(KT):
                    step(stt(yatt[:, i, :], yatt[:, i, :], feat[:, GLAN + i % 2:GLAN + i % 2 + 1], rstd[:, i // 2, :], ALU.mult, ALU.mult))
                dve.wait_ge(S("proj_free"), 28)
                tt(yatt[:, :, :], yatt[:, :, :], zs[:, :, :], ALU.mult).then_inc(S("gyn"), 1)
                dve.wait_ge(S("slot_used"), pos["out1"] + n_out[1])
                residual(1, 16, 4)

            def first_of_max(dst, src, mx):
                p4 = pref[:, None, :].broadcast_to([P, NS, 4])
                step(tt(t2(VAL, 4), src, mx.broadcast_to([P, NS, 4]), ALU.is_equal))
                step(tt(t2(VAL, 4), t2(VAL, 4), p4, ALU.mult))
                step(dve.tensor_reduce(tiny[:, VMX:VMX + 2], t2(VAL, 4), AX.X, ALU.max))
                step(tt(dst, t2(VAL, 4), t2(VMX, 1).broadcast_to([P, NS, 4]), ALU.is_equal))

            def moe(l):
                dve.wait_ge(S("pref"), 4)
                dve.wait_ge(S("logits"), l + 1)
                lg = t2(LG, 20)
                step(tt(lg, ps[:, 0, T:T + 64].rearrange("p (s n) -> p s n", s=NS)[:, :, 0:20], br[:, l:l + 1, :].broadcast_to([P, NS, 20]), ALU.add))
                step(dve.tensor_reduce(tiny[:, GMAX:GMAX + 2], lg[:, :, 0:4], AX.X, ALU.max))
                tt(t2(GEX, 4), lg[:, :, 0:4], t2(GMAX, 1).broadcast_to([P, NS, 4]), ALU.subtract).then_inc(S("g_sub"), 1)
                first_of_max(t2(OHG, 4), lg[:, :, 0:4], t2(GMAX, 1))
                for s in range(NS):
                    ep = tiny[:, EPR + 16 * s:EPR + 16 * s + 16]
                    step(tt(ep.rearrange("p (e g) -> p g e", g=4), lg[:, s, 4:20].rearrange("p (g e) -> p g e", g=4),
                            tiny[:, OHG + 4 * s:OHG + 4 * s + 4][:, :, None].broadcast_to([P, 4, 4]), ALU.mult))
                step(dve.tensor_reduce(tiny[:, EL:EL + 8], tiny[:, EPR:EPR + 32].rearrange("p (e g) -> p e g", g=4), AX.X, ALU.add))
                step(dve.tensor_reduce(tiny[:, EMX:EMX + 2], t2(EL, 4), AX.X, ALU.max))
                tt(t2(EL, 4), t2(EL, 4), t2(EMX, 1).broadcast_to([P, NS, 4]), ALU.subtract).then_inc(S("e_sub"), 1)
                dve.wait_ge(S("g_exp"), l + 1)
                step(dve.tensor_reduce(tiny[:, GPR:GPR + 2], t2(GEX, 4), AX.X, ALU.add))
                step(dve.reciprocal(tiny[:, GPR:GPR + 2], tiny[:, GPR:GPR + 2]))
                dve.wait_ge(S("e_exp"), l + 1)
                step(dve.tensor_reduce(tiny[:, EMX:EMX + 2], t2(EL, 4), AX.X, ALU.max))
                first_of_max(t2(OH1, 4), t2(EL, 4), t2(EMX, 1))
                step(stt(t2(P2, 4), t2(OH1, 4), -2.0, t2(EL, 4), ALU.mult, ALU.add))
                step(dve.tensor_reduce(tiny[:, M2:M2 + 2], t2(P2, 4), AX.X, ALU.max))
                first_of_max(t2(OH2, 4), t2(P2, 4), t2(M2, 1))
                step(tt(tiny[:, DEN:DEN + 2], tiny[:, EMX:EMX + 2], tiny[:, M2:M2 + 2], ALU.add))
                step(dve.reciprocal(tiny[:, DEN:DEN + 2], tiny[:, DEN:DEN + 2]))
                step(tt(tiny[:, DEN:DEN + 2], tiny[:, DEN:DEN + 2], tiny[:, GPR:GPR + 2], ALU.mult))
                step(tt(t2(OH1, 4), t2(OH1, 4), t2(OH2, 4), ALU.add))
                step(tt(t2(LOC, 4), t2(OH1, 4), t2(EL, 4), ALU.mult))
                step(tt(t2(LOC, 4), t2(LOC, 4), t2(DEN, 1).broadcast_to([P, NS, 4]), ALU.mult))
                for s in range(NS):
                    step(tt(tiny[:, CMB + 16 * s:CMB + 16 * s + 16].rearrange("p (g e) -> p g e", g=4),
                            tiny[:, OHG + 4 * s:OHG + 4 * s + 4][:, :, None].broadcast_to([P, 4, 4]),
                            tiny[:, LOC + 4 * s:LOC + 4 * s + 4][:, None, :].broadcast_to([P, 4, 4]), ALU.mult))
                    last = tt(tiny[:, SEL + 16 * s:SEL + 16 * s + 16].rearrange("p (g e) -> p g e", g=4),
                              tiny[:, OHG + 4 * s:OHG + 4 * s + 4][:, :, None].broadcast_to([P, 4, 4]),
                              tiny[:, OH1 + 4 * s:OH1 + 4 * s + 4][:, None, :].broadcast_to([P, 4, 4]), ALU.mult)
                    if s == 0:
                        step(last)
                last.then_inc(S("sel"), 1)
                dve.wait_ge(S("sel"), l + 1)
                dve.wait_ge(S("rank_raw"), l + 1)
                step(stt(tiny[:, RK:RK + 32], tiny[:, SEL:SEL + 32], -FAR, ps[:, 1, 0:32], ALU.mult, ALU.add))
                dve.tensor_reduce(tiny[:, CNT:CNT + 1], ps[:, 1, 32:48], AX.X, ALU.max).then_inc(S("rank_read"), 1)
                dve.wait_ge(S("rank_read"), l + 1)
                dve.tensor_copy(need[:, l:l + 1], tiny[:, CNT:CNT + 1]).then_inc(S("need"), 1)
                for s in range(NS):
                    d3 = DISP[:, s * D:(s + 1) * D].rearrange("p (e c) -> p e c", e=NE)
                    step(tt(d3, cst[:, IOTA, None, 0:CAP].broadcast_to([P, NE, CAP]),
                            tiny[:, RK + 16 * s:RK + 16 * s + 16][:, :, None].broadcast_to([P, NE, CAP]), ALU.is_equal))
                    last = tt(DISW[:, s * D:(s + 1) * D].rearrange("p (e c) -> p e c", e=NE), d3,
                              tiny[:, CMB + 16 * s:CMB + 16 * s + 16][:, :, None].broadcast_to([P, NE, CAP]), ALU.mult)
                    if s == 0:
                        step(last)
                last.then_inc(S("disp"), 1)
                base = pos[f"moe{l}"]
                def hg(n):
                    dve.wait_ge(S("gathered"), n)
                    dve.tensor_copy(W(1)[:, 512:1024], ps[:, 1, :]).then_inc(S("hg"), 1)

                def ys(i):
                    dve.wait_ge(S("slot_used"), i * (2 * PER_EXPERT) + (base + 12))
                    dve.tensor_copy(YS[:, 512:1024], ps[:, 1, :]).then_inc(S("ys"), 1)

                def pair(i, first=False, final=False):
                    done = i + (l * PAIRS)
                    if not first:
                        ys(i - 1)
                    if l == 0:
                        for c in range(per_pair):
                            ada(1, n_ada + c, i)
                    dve.wait_ge(S("sil"), done + 1)
                    dve.wait_ge(S("slot_used"), i * (2 * PER_EXPERT) + (base + 8))
                    tt(HACT, SIL, ps[:, 3, :], ALU.mult).then_inc(S("hact"), 1)
                    if not final:
                        hg(done + 2)
                    if l == 0:
                        n = 2 * per_pair
                        dve.wait_ge(S("mac_summed"), i * per_pair + (n_ada + per_pair))
                        tt(mods[:, 1, bass.ds(i * n, n), :], ps[:, 3, 0:2 * n].rearrange("p (r s) -> p r s", s=NS),
                           feat[:, bass.ds(i * n + (BADA + 48), n)][:, :, None].broadcast_to([P, n, NS]), ALU.add).then_inc(S("mods"), 1)

                hg(l * PAIRS + 1)
                pair(0, first=True)
                with dve.Fori(1, PAIRS - 1) as i:
                    pair(i)
                pair(PAIRS - 1, final=True)
                ys(PAIRS - 1)
                if l == 0:
                    dve.wait_ge(S("mods"), 2 + PAIRS)
                    step(scales(1, 8, NMIX))
                    step(scales(1, 32, NFFN))
                dve.wait_ge(S("scattered"), PAIRS * (l + 1))
                dve.wait_ge(S("need"), l + 1)
                most = dve.value_load(need[0:1, l:l + 1], min_val=0, max_val=T)
                with dve.If(most > CAP):
                    with dve.Fori(0, NE) as e:
                        with dve.Fori(1, T // CAP) as r:
                            it = e * (T // CAP - 1) + r
                            rk = tiny[:, RK:RK + 32].rearrange("p (s e) -> p s e", s=NS)[:, :, bass.ds(e, 1)]
                            cw = tiny[:, CMB:CMB + 32].rearrange("p (s e) -> p s e", s=NS)[:, :, bass.ds(e, 1)]
                            iota = cst[:, IOTA:IOTA + 2, :].rearrange("p a b -> p (a b)")[:, bass.ds(r * CAP, CAP)]
                            dp, dw = (x.rearrange("p (s c) -> p s c", s=NS) for x in (O_DISP, O_DISW))
                            tt(dp, iota[:, None, :].broadcast_to([P, NS, CAP]), rk.broadcast_to([P, NS, CAP]), ALU.is_equal).then_inc(S(f"o{l}_d"), 1)
                            dve.wait_ge(S(f"o{l}_d"), it)
                            tt(dw, dp, cw.broadcast_to([P, NS, CAP]), ALU.mult).then_inc(S(f"o{l}_v"), 1)
                            dve.wait_ge(S(f"o{l}_p"), it * 4 + (1 - 4))
                            dve.tensor_copy(O_HG, ps[:, 0, :].rearrange("p (k c) -> p k c", k=KT)).then_inc(S(f"o{l}_v"), 1)
                            dve.wait_ge(S(f"o{l}_p"), it * 4 + (2 - 4))
                            dve.tensor_copy(O_CT, ps[0:CAP, 1, 0:T]).then_inc(S(f"o{l}_v"), 1)
                            dve.wait_ge(S(f"o{l}_a"), it)
                            dve.wait_ge(S(f"o{l}_used"), it * PER_EXPERT + 4)
                            tt(O_ACT, O_SIL, ps[0:CAP, 3, :], ALU.mult).then_inc(S(f"o{l}_v"), 1)
                            dve.wait_ge(S(f"o{l}_p"), it * 4 + (3 - 4))
                            dve.tensor_copy(O_HT, ps[:, 1, 0:T].rearrange("p (f c) -> p f c", f=FT)).then_inc(S(f"o{l}_v"), 1)
                            dve.wait_ge(S(f"o{l}_used"), it * PER_EXPERT + PER_EXPERT)
                            dve.tensor_copy(O_YS, ps[0:CAP, 2:4, :].rearrange("p a b -> p (a b)")).then_inc(S(f"o{l}_v"), 1)
                            dve.wait_ge(S(f"o{l}_p"), it * 4)
                residual(l, 40, 2 * l + 3)

            dve.wait_ge(S("csilu"), 2)
            for n in range(n_first):
                ada(0, n)
            ada0_done(0, n_first)
            norm(0)
            even()
            norm(1)
            moe(0)
            norm(2)
            odd()
            norm(3)
            moe(1)
            norm(4)


_INS = ['x_prompt', 'x_sample', 'cache_k_attn', 'cache_v_attn', 'state_ssd_fwd', 'state_ssd_bwd', 'state_gla_fwd',
        'state_gla_bwd', 'c', 'c_ctx', 'w_ada', 'b_ada', 'norm_mix_w', 'norm_ffn_w', 'w_in_even', 'conv_w', 'conv_b',
        'dt_bias_fwd', 'dt_bias_bwd', 'a_log_fwd', 'a_log_bwd', 'd_skip', 'ssd_norm_w', 'attn_sink', 'w_out_even',
        'w_in_odd', 'w_gk2_fwd', 'b_gk_fwd', 'w_gk2_bwd', 'b_gk_bwd', 'gla_norm_w', 'w_out_odd', 'w_router_group',
        'b_router_group', 'w_router_expert', 'b_router_expert', 'w_gate_exp', 'w_up_exp', 'w_down_exp', 'final_norm_w']
_OUTS = [(1, 128, 1024), (1, 128, 1024), (1, 1, 128, 4, 64), (1, 1, 128, 4, 64), (1, 1, 16, 64, 128), (1, 1, 16, 64, 128),
         (1, 1, 4, 128, 256), (1, 1, 4, 128, 256)]


def kernel(**inputs):
    import concourse.bacc as _bacc
    from concourse.bass_utils import run_bass_kernel_spmd as _run

    nc = _bacc.Bacc("TRN2", target_bir_lowering=False, num_devices=1)
    arrays, args = {}, {}
    for name in _INS:
        a = np.ascontiguousarray(inputs[name])
        arrays[f"in_{name}_dram"] = a
        args[name] = nc.dram_tensor(f"in_{name}_dram", a.shape, F32, kind="ExternalInput").ap()
    arrays["in_consts_dram"] = constants()
    args["consts"] = nc.dram_tensor("in_consts_dram", (P, NCONST, P), F32, kind="ExternalInput").ap()
    outs = [nc.dram_tensor(f"out_{i}_dram", shape, F32, kind="ExternalOutput").ap() for i, shape in enumerate(_OUTS)]
    build(nc, args, outs)
    r = _run(nc, [arrays], core_ids=[0])
    return tuple(r.results[0][f"out_{i}_dram"] for i in range(len(_OUTS)))
```

```python
from contextlib import ExitStack

import numpy as np
import concourse.bass as bass
from concourse import mybir

F32 = mybir.dt.float32
ACT = mybir.ActivationFunctionType
ALU = mybir.AluOpType
AX = mybir.AxisListType

P = 128
D = 1024
KT = D // P
T = 256
NS = 2
GRID_W = 64
EPS = 1e-6
HEADS, HP, NST = 16, 64, 128
CONV_TILES = 12
TAPS = 5
KVH = 4
SCALE = 0.125
LOWRANK = 16
GH, GK, GV, CH = 4, 128, 256, 64
GLA_SCALE = float(GK) ** -0.5
NE, FE = 16, 512
FT = FE // P
CHUNK = 2048
RING = 6
PER_EXPERT = 6
PAIRS = NE // 2
CAP = 64
PAIR_ORDER = [(a, c) for c in range(PER_EXPERT) for a in range(2)]
assert 2 * PER_EXPERT % RING == 0 and RING >= PER_EXPERT
COMBOS = ((0, 0, 0), (0, 0, 1), (0, 1, 1), (0, 1, 0), (1, 0, 0), (1, 1, 1))

BADA, NMIX, NFFN = 0, 96, 112
CONVW, CONVB, SSDN, GLAN, FINN, CVEC, CCTX = 128, 188, 200, 208, 210, 218, 226

(IDENT, ONES, MEAN_D, MEAN_V, LE, GE, GT, LT, BLE, BGE, BGT, BLT, COS, SIN, ROT, IOTA) = range(16)
NCONST = 17
ADA = 384
FAR = 1024.0


def constants():
    i = np.arange(P)
    k, m = i[:, None], i[None, :]
    c = np.zeros((NCONST, P, P), np.float32)
    same = (k // CH) == (m // CH)
    c[IDENT] = k == m
    c[ONES] = 1.0
    c[MEAN_D] = 1.0 / D
    c[MEAN_V] = 1.0 / GV
    c[LE], c[GE], c[GT], c[LT] = k <= m, k >= m, k > m, k < m
    for n, cond in ((BLE, k <= m), (BGE, k >= m), (BGT, k > m), (BLT, k < m)):
        c[n] = (cond & same) / 16.0
    c[IOTA], c[IOTA + 1] = m - FAR, m + P - FAR
    quarter = 16
    inv = (np.float32(10000.0) ** (-np.arange(quarter, dtype=np.float32) / np.float32(quarter))).astype(np.float32)
    d = i % 64
    pos = np.where(d[:, None] < 32, m // GRID_W, m % GRID_W).astype(np.float32)
    ang = (pos * inv[d % quarter][:, None]).astype(np.float32)
    c[COS], c[SIN] = np.cos(ang), np.sin(ang)
    for q in range(P):
        if q % 32 < quarter:
            c[ROT][q + quarter, q] = -1.0
        else:
            c[ROT][q - quarter, q] = 1.0
    return np.ascontiguousarray(c.transpose(1, 0, 2))



DTX, DTA, DTT, DTE, DTU, DTL, DT, TE, WS = 0, 64, 128, 192, 256, 320, 384, 448, 480
CBM = 512
MX, NEGM, RSUM, SNKD, SNKE, RINV = 0, 16, 32, 48, 64, 80
(LG, GMAX, OHG, GEX, EPR, EL, EMX, OH1, P2, M2, OH2, DEN, GPR, LOC, CMB, VAL, VMX, SEL, RK, CNT) = \
    (0, 40, 48, 56, 64, 96, 104, 120, 128, 136, 144, 152, 156, 160, 192, 224, 232, 256, 288, 320)


def build(nc, A, O):
    with ExitStack() as ctx:
        def sb(name, shape):
            return ctx.enter_context(nc.sbuf_tensor(name, shape, F32))

        sems = {}

        def S(name):
            if name not in sems:
                sems[name] = ctx.enter_context(nc.semaphore(name))
            return sems[name]

        ring = sb("ring", [P, RING, CHUNK])
        cst = sb("cst", [P, NCONST, P])
        xT = sb("xT", [P, KT, T])
        hT = sb("hT", [P, KT, T])
        rows = sb("rows", [P, 2, P])
        feat = sb("feat", [P, 2 * P])
        csilu = sb("csilu", [P, KT, NS])
        mods = sb("mods", [P, 2, 48, NS])
        rstd = sb("rstd", [P, GH, T])
        xpad = sb("xpad", [P, CONV_TILES, NS, P + TAPS - 1])
        xbc = sb("xbc", [P, CONV_TILES, T])
        zs = sb("zs", [P, KT, T])
        yatt = sb("yatt", [P, KT, T])
        qT = sb("qT", [P, KT, T])
        kv = sb("kv", [P, NS, 512])
        xtok = sb("xtok", [P, NS, D])
        btok = sb("btok", [P, 2 * P])
        wide = sb("wide", [P, 6, 2048])
        wdt = sb("wdt", [P, KT, 32])
        wlr = sb("wlr", [P, KT, 32])
        wr = sb("wr", [P, 2, KT, 20])
        br = sb("br", [P, 2, 20])
        dtb = sb("dtb", [P, 32])
        alog = sb("alog", [P, 32])
        dskb = sb("dskb", [P, HEADS])
        dsk = sb("dsk", [P, KT])
        sink = sb("sink", [P, HEADS])
        ckv = sb("ckv", [P, 2, 256])
        wg = sb("wg", [LOWRANK + 1, 2, 512])
        lr = sb("lr", [LOWRANK + 1, 2 * T])
        tiny = sb("tiny", [P, 1024])
        need = ctx.enter_context(nc.sbuf_tensor("need", [P, 2], mybir.dt.int32))
        pref = sb("pref", [P, 4])
        eps = sb("eps", [P, 1])
        ps = ctx.enter_context(nc.psum_tensor("ps", [P, 8, 512], F32))

        zero = rows[:, :, :].rearrange("p a b -> p (a b)")

        def C(n):
            return cst[:, n, :]

        def W(i):
            return wide[:, i, :]

        xpf = xpad[:, :, :, :].rearrange("p a b c -> p (a b c)")
        hTf = hT[:, :, :].rearrange("p k t -> p (k t)")
        xbf = xbc[:, :, :].rearrange("p k t -> p (k t)")
        yaf = yatt[:, :, :].rearrange("p k t -> p (k t)")
        U = xpf[:, 0:2048]
        KTC, KTL, KTP = xpf[:, 0:512], xpf[:, 512:1024], xpf[:, 1024:1536]
        QR, KR = xpf[:, 1536:2560], xpf[:, 2560:3072]
        ATT = xpf[:, 0:1024].rearrange("p (s h t) -> p s h t", s=NS, h=GH)
        ATB = xpf[:, 1024:2048].rearrange("p (s h t) -> p s h t", s=NS, h=GH)
        CT = W(0).rearrange("p (i t) -> p i t", i=PAIRS)
        DISP, DISW = W(2), W(3)
        HG = W(1)[:, 0:1024].rearrange("p (k c) -> p k c", k=KT)
        YS = W(1)[:, 1024:2048]
        HACT, SIL = W(4)[:, 0:FE], W(4)[:, FE:2 * FE]
        HT = W(5)[:, 0:FE].rearrange("p (f c) -> p f c", f=FT)
        O_HG = W(4)[:, 1024:1536].rearrange("p (k c) -> p k c", k=KT)
        O_ACT, O_SIL = W(5)[0:CAP, 512:1024], W(5)[0:CAP, 1024:1536]
        O_HT = W(4)[:, 1536:1792].rearrange("p (f c) -> p f c", f=FT)
        O_CT = W(5)[0:CAP, 1536:1792]
        O_DISP, O_DISW = W(5)[:, 1792:1920], W(5)[:, 1920:2048]
        O_YS = W(1)[0:CAP, 0:1024]

        def tk(s):
            return slice(s * P, (s + 1) * P)

        def heads(ap, n=HEADS):
            return ap.rearrange("p (h w) -> p h w", h=n)

        w_in = (A["w_in_even"][0], A["w_in_odd"][0])
        w_out = (A["w_out_even"][0], A["w_out_odd"][0])
        IN = ([1024 + 256 * i for i in range(6)] + [3616, 3872] + [2592 + 256 * i for i in range(4)]
              + [256 * i for i in range(4)],
              [256 * i for i in range(12)])
        n_ada = 6 * D // 256
        n_first = 2 * D // 256
        n_out = (w_out[0].shape[0] // 256, w_out[1].shape[0] // 256)
        n_early = 8
        n_loop = n_ada + n_early
        per_pair = (n_ada - n_early) // PAIRS
        a_slots = ((W(0), W(1), W(3)), (xtok[:, :, :].rearrange("p s d -> p (s d)"), hTf, W(3)), (zs[:, :, :].rearrange("p k t -> p (k t)"), yaf))
        a_sums = (W(4).rearrange("p (c g n) -> p c g n", c=4, g=NS), xbf[:, 0:2 * 512].rearrange("p (c g n) -> p c g n", c=2, g=NS))

        def a_slot(n):
            x = a_slots[2][n - n_loop] if n >= n_loop else a_slots[n // n_ada][n % 3]
            return x.rearrange("p (k n) -> p k n", k=KT)

        def a_sum(n):
            return a_sums[1][:, n - n_loop] if n >= n_loop else a_sums[0][:, n % 4]

        def a_landed(n, rounds=0):
            if n >= n_loop:
                c = n - n_loop
                return S(f"ada_landed{c}"), rounds * 16 + 16 * (len(range(c, n_loop, 3)) + 1)
            return S(f"ada_landed{n % 3}"), 16 * (n // 3 + 1)

        def dve_tiles(n):
            return 5 if n < n_first else 7 if n < n_ada else KT

        def summed(n, rounds=0):
            return rounds * (per_pair * KT * NS) + NS * sum(dve_tiles(x) for x in range(n + 1))

        pos, at = {}, 0
        for name, n in (("in0", len(IN[0])), ("out0", n_out[0]), ("moe0", NE * PER_EXPERT), ("in1", len(IN[1])), ("out1", n_out[1]), ("moe1", NE * PER_EXPERT)):
            pos[name] = at
            at += n

        def slot(n, k):
            return ring[:, n % RING, :].rearrange("p (k n) -> p k n", k=k)

        def wait_landed(pe, n, rounds=0):
            pe.wait_ge(S(f"landed{n % RING}"), rounds * 16 + 16 * (n // RING + 1))

        def stepper(eng, name):
            count = [0]

            def step(ins):
                count[0] += 1
                ins.then_inc(S(name), 1)
                eng.wait_ge(S(name), count[0])
            return step

        def place(i, n):
            return (i % 2) * (n // 2) + i // 2

        def mm(pe, out, lhsT, rhs, first, last, shared=False):
            return pe.matmul(out, lhsT, rhs, start=first, stop=last, skip_group_check=shared)

        block = ctx.enter_context(nc.Block())

        @block.sync
        def _(sp):
            def load(n, src, k, rounds=0):
                sp.dma_start(slot(n, k), src).then_inc(S(f"landed{n % RING}"), 16)

            def wait_free(n, rounds=0):
                sp.wait_ge(S("slot_used"), rounds * RING + (n + 1 - RING))

            def ada(n, rounds=0):
                if n >= n_loop:
                    sp.wait_ge(S("mac"), summed(n - per_pair, rounds))
                elif n == n_ada:
                    sp.wait_ge(S("yss"), 1)
                elif n > n_ada + 2:
                    sp.wait_ge(S("mac"), summed(n - 3))
                elif 3 <= n < n_ada:
                    sp.wait_ge(S("mac_summed"), n - 2)
                l, c = n // n_ada, n % n_ada + rounds * per_pair
                src = A["w_ada"][l].rearrange("(k p) n -> p k n", p=P)[:, :, bass.ds(c * 256, 256)]
                sp.dma_start(a_slot(n), src).then_inc(a_landed(n)[0], 16)

            def w_in_load(l, j):
                n = pos[f"in{l}"] + j
                if n >= RING:
                    wait_free(n)
                load(n, w_in[l][:, IN[l][j]:IN[l][j] + 256].rearrange("(k p) n -> p k n", p=P), KT)

            sp.wait_ge(S("rows_in"), 160)
            for n in range(n_first):
                ada(n)
            for j in range(len(IN[0])):
                w_in_load(0, j)
                if j >= 1 and n_first + j - 1 < n_ada:
                    ada(n_first + j - 1)
            ada(n_ada - 1)
            for l in range(2):
                if l:
                    for j in range(len(IN[1])):
                        w_in_load(1, j)
                for j in range(n_out[l]):
                    if l == 0 and j == RING:
                        for n in range(n_ada, n_ada + 6):
                            ada(n)
                    wait_free(pos[f"out{l}"] + j)
                    load(pos[f"out{l}"] + j, w_out[l][256 * j:256 * j + 256, :].rearrange("(k p) n -> p k n", p=P), 2)
                base = pos[f"moe{l}"]
                wgu = [A[w][l].rearrange("e (k p) f -> p e k f", p=P) for w in ("w_gate_exp", "w_up_exp")]
                wd = A["w_down_exp"][l].rearrange("e (j k p) d -> p e j k d", p=P, k=2)

                def expert(e, c, n):
                    if c < 4:
                        src = wgu[c // 2][:, bass.ds(e, 1), 4 * (c % 2):4 * (c % 2) + 4, :]
                        return slot(n, 4), src.rearrange("p a k f -> p (a k) f")
                    src = wd[:, bass.ds(e, 1), c - 4, :, :]
                    return slot(n, 2), src.rearrange("p a k d -> p (a k) d")

                if l == 0:
                    for n in range(n_ada + 6, n_loop):
                        ada(n)
                    sp.wait_ge(S("slot_used"), pos["out0"] + n_out[0])
                with sp.Fori(0, PAIRS) as i:
                    for n, (a, c) in enumerate(PAIR_ORDER):
                        if l == 0 and n in (2, 4):
                            ada(n_loop + n // 2 - 1, i)
                        wait_free(base + n, i * (2 * PER_EXPERT // RING))
                        dst, src = expert(i * 2 + a, c, base + n)
                        sp.dma_start(dst, src).then_inc(S(f"landed{(base + n) % RING}"), 16)
                sp.wait_ge(S("need"), l + 1)
                most = sp.value_load(need[0:1, l:l + 1], min_val=0, max_val=T)
                with sp.If(most > CAP):
                    sp.wait_ge(S("slot_used"), base + NE * PER_EXPERT)
                    with sp.Fori(0, NE) as e:
                        with sp.Fori(1, T // CAP) as r:
                            it = e * (T // CAP - 1) + r
                            for c in range(PER_EXPERT):
                                sp.wait_ge(S(f"o{l}_used"), it * PER_EXPERT + (c + 1 - PER_EXPERT))
                                dst, src = expert(e, c, c)
                                sp.dma_start(dst, src).then_inc(S(f"o{l}_landed{c}"), 16)
                    sp.wait_ge(S(f"o{l}_used"), (NE * (T // CAP - 1) + 1) * PER_EXPERT)
            for s in range(NS):
                sp.wait_ge(S("y_tok"), 2 * s + 2)
                sp.dma_start(O[s][0], xtok[:, s, :]).then_inc(S("y_stored"), 16)
            sp.wait_ge(S("y_stored"), 32)

        SET_UP = 7
        O_STEPS = 6
        SMALL = 16 * (7 + 8 + 2 + 1 + 4)

        @block.gpsimd
        def _(pool):
            def load(dst, src):
                pool.dma_start(dst, src).then_inc(S("small_in"), 16)

            def spread(src, n):
                return src.rearrange("(a n) -> a n", a=1).broadcast_to([P, n])

            pool.memset(xpf, 0.0).then_inc(S("pad_zero"), 1)
            load(wdt[:, :, :], w_in[0][:, 2560:2592].rearrange("(k p) n -> p k n", p=P))
            load(dtb[:, 0:16], spread(A["dt_bias_fwd"][0], 16))
            load(dtb[:, 16:32], spread(A["dt_bias_bwd"][0], 16))
            load(alog[:, 0:16], spread(A["a_log_fwd"][0], 16))
            load(alog[:, 16:32], spread(A["a_log_bwd"][0], 16))
            load(dskb[:, :], spread(A["d_skip"][0], 16))
            load(sink[:, :], spread(A["attn_sink"][0], 16))
            for l in range(2):
                load(wr[:, l, :, 0:4], A["w_router_group"][l].rearrange("(k p) n -> p k n", p=P))
                load(wr[:, l, :, 4:20], A["w_router_expert"][l].rearrange("(k p) n -> p k n", p=P))
                load(br[:, l, 0:4], spread(A["b_router_group"][l], 4))
                load(br[:, l, 4:20], spread(A["b_router_expert"][l], 16))
            load(ckv[:, 0, :], A["cache_k_attn"][0, 0].rearrange("t h d -> t (h d)"))
            load(ckv[:, 1, :], A["cache_v_attn"][0, 0].rearrange("t h d -> t (h d)"))
            load(wlr[:, :, :], w_in[1][:, 3072:3104].rearrange("(k p) n -> p k n", p=P))
            load(wg[0:16, 0, :], A["w_gk2_fwd"][0])
            load(wg[0:16, 1, :], A["w_gk2_bwd"][0])
            load(wg[16:17, 0, :], A["b_gk_fwd"])
            load(wg[16:17, 1, :], A["b_gk_bwd"])
            pool.wait_ge(S("proj_free"), 8)
            pool.wait_ge(S("small_in"), SMALL)
            for n, keys in enumerate((kv[:, 0, 0:256], kv[:, 1, 0:256], ckv[:, 0, :])):
                pool.tensor_copy(W(5)[:, n * 512:(n + 1) * 512].rearrange("p (j a d) -> p j a d", j=KVH, a=2),
                                 keys.rearrange("p (j d) -> p j d", j=KVH)[:, :, None, :].broadcast_to([P, KVH, 2, 64])).then_inc(S("keys_twice"), 1)
            after = (0, 4, 8, 16)
            pool.wait_ge(S("dtA"), 1)
            pool.wait_ge(S("conv_done"), CONV_TILES)
            pool.wait_ge(S("consts_in"), 16)
            for n in range(4):
                if n:
                    pool.wait_ge(S("seg_raw"), after[n])
                a0 = DTA + 16 * n
                pool.tensor_tensor(heads(U), C(GE if n % 2 else LE)[:, None, :].broadcast_to([P, HEADS, P]),
                                   tiny[:, a0:a0 + 16][:, :, None].broadcast_to([P, HEADS, P]),
                                   ALU.mult).then_inc(S("U_ready"), 1)

        @block.tensor
        def _(pe):
            def used(ins):
                ins.then_inc(S("slot_used"), 1)

            def turn(out, in_, n=P):
                return pe.transpose(out, in_, cst[0:n, IDENT, 0:n])

            pe.wait_ge(S("ident_in"), 16)
            pe.wait_ge(S("rows_in"), 160)
            turn(ps[:, 0, 0:P], rows[:, 0, :])
            turn(ps[:, 0, P:P + 106], rows[0:106, 1, :], 106).then_inc(S("rows_turned"), 1)
            pe.wait_ge(S("x_in"), 32)
            for g in range(4):
                for k in range(4):
                    last = turn(ps[:, 1 + g, k * P:(k + 1) * P], xtok[:, g // 2, ((g % 2) * 4 + k) * P:((g % 2) * 4 + k + 1) * P])
                last.then_inc(S("x_turned"), 1)

            def ada(bank, col, n, rounds=0):
                direct = range(dve_tiles(n), KT)
                sums = a_sum(n)
                if direct:
                    w = a_slot(n)
                    pe.wait_ge(*a_landed(n))
                for m in range(2):
                    for k in direct:
                        mm(pe, ps[:, bank, col + 2 * m:col + 2 * m + 2], w[:, k, m * P:(m + 1) * P], csilu[:, k, :], k == direct[0], False, shared=True)
                    if m == 0:
                        pe.wait_ge(S("mac"), summed(n, rounds))
                    for g in range(NS):
                        last = mm(pe, ps[:, bank, col + 2 * m + g:col + 2 * m + g + 1], sums[:, g, m * P:(m + 1) * P], cst[:, ONES, 0:1], not direct, True, shared=True)
                last.then_inc(S("mac_summed"), 1)

            def ada0(n):
                ada(0, ADA + 4 * n, n)

            def norm(i):
                if i == 0:
                    pe.wait_ge(S("mods"), 1)
                for k in range(KT):
                    pe.wait_ge(S("sq"), KT * i + k + 1)
                    last = mm(pe, ps[:, 0, 0:T], C(MEAN_D), hT[:, k, :], k == 0, k == KT - 1)
                last.then_inc(S("ss"), 1)

            def wait_h(i, k):
                pe.wait_ge(S("h_ready"), (i * KT + k + 1) * NS)

            def project(n, b, by_token):
                wait_landed(pe, n)
                for m in range(2):
                    for k in range(KT):
                        if by_token:
                            last = mm(pe, ps[:, b, m * T:(m + 1) * T], hT[:, k, tk(m)], slot(n, KT)[:, k, :], k == 0, k == KT - 1)
                        else:
                            last = mm(pe, ps[:, b, m * T:(m + 1) * T], slot(n, KT)[:, k, m * P:(m + 1) * P], hT[:, k, :], k == 0, k == KT - 1)
                used(last)

            def projections(l):
                done = 0 if l == 0 else len(IN[0])
                for j in range(len(IN[l])):
                    if done + j >= 4:
                        pe.wait_ge(S("proj_free"), done + j - 3)
                    project(pos[f"in{l}"] + j, 1 + j % 4, j in ((6, 7) if l == 0 else range(2, 8)))
                    if l == 0 and j == 2:
                        pe.wait_ge(S("dt_abs"), 1)
                    if l == 0 and j >= 2:
                        ada0(n_first + j - 2)
                if l == 0:
                    for n in (n_ada - 2, n_ada - 1):
                        ada0(n)

            def out_project(l, src):
                for c in range(n_out[l]):
                    if l == 0:
                        ada(3, 4 * c, n_ada + c)
                    n = pos[f"out{l}"] + c
                    wait_landed(pe, n)
                    for k in range(2):
                        t = 2 * c + k
                        if l:
                            pe.wait_ge(S("grms"), 2)
                            pe.wait_ge(S("gyn"), t + 1)
                        for m in range(KT):
                            last = mm(pe, ps[:, 4 + m // 2, (m % 2) * T:(m % 2 + 1) * T], slot(n, 2)[:, k, m * P:(m + 1) * P],
                                      src(t), t == 0 and m % 2 == 0, t == 2 * n_out[l] - 1, shared=True)
                    used(last)

            def even():
                pe.wait_ge(S("small_in"), SMALL)
                for s in range(NS):
                    for k in range(KT):
                        wait_h(0, k)
                        last = mm(pe, ps[:, 0, T + 32 * s:T + 32 * s + 32], hT[:, k, tk(s)], wdt[:, k, :], k == 0, k == KT - 1)
                last.then_inc(S("dt_raw"), 1)
                projections(0)
                for g in range(5):
                    pe.wait_ge(S("xbc_ready"), (2 + 2 * (g % 2)) if g < 4 else 5)
                    if g >= 3:
                        pe.wait_ge(S("tok_copied"), g - 2)
                    for k in range(4 if g < 4 else 2):
                        in_ = xbc[:, (g % 2) * 4 + k, tk(g // 2)] if g < 4 else xbc[:, 8 + k, tk(0)]
                        last = turn(ps[:, 5 + g % 3, k * P:(k + 1) * P], in_)
                    last.then_inc(S("tok_turned"), 1)
                pe.wait_ge(S("h0_in"), 32)
                pe.wait_ge(S("proj_free"), 16)
                for g in range(4):
                    for k in range(4):
                        last = turn(ps[:, 1 + g, k * P:(k + 1) * P], W(2)[:, (4 * g + k) * P:(4 * g + k + 1) * P])
                    last.then_inc(S("h0_turned"), 1)
                pe.wait_ge(S("dtA"), 1)
                pe.wait_ge(S("tok_copied"), 5)
                for d in range(2):
                    last = mm(pe, ps[:, 7, 256 + 16 * d:272 + 16 * d], C(LT if d else GT), tiny[:, DTA + 16 * d:DTA + 16 * d + 16], True, True)
                last.then_inc(S("te_raw"), 1)
                unit = 0
                for s in range(NS):
                    pe.wait_ge(S("xbc_ready"), 6)
                    pe.wait_ge(*((S("cbm"), 1) if s else (S("mods"), 2)))
                    for g in range(2):
                        last = mm(pe, ps[:, 0, g * P:(g + 1) * P], xbc[:, 8 + g, tk(s)], xbc[:, 10 + g, tk(s)], True, True)
                    last.then_inc(S("cb_raw"), 1)
                    for d in range(2):
                        pe.wait_ge(S("U_ready"), 2 * s + d + 1)
                        for w in range(1 + s):
                            for q in range(4):
                                if unit < 4:
                                    pe.wait_ge(S("h0_copied"), unit + 1)
                                elif unit < 8 or unit >= 12:
                                    pe.wait_ge(S("seg_exp"), unit - 3)
                                else:
                                    pe.wait_ge(S("st_copied"), q + 1)
                                mm(pe, ps[:, 1 + unit % 4, :], C(ONES) if w else C(LT if d else GT),
                                   U[:, q * 512:(q + 1) * 512], True, True).then_inc(S("seg_raw"), 1)
                                unit += 1
                    if s == 0:
                        pe.wait_ge(S("xw_ready"), 1)
                        pe.wait_ge(S("tok_copied"), 5)
                        pe.wait_ge(S("seg_exp"), 8)
                        for i in range(16):
                            g = (i % 8) // 4
                            last = mm(pe, ps[:, 1 + i // 4, (i % 4) * P:(i % 4 + 1) * P], W(3)[:, i * P:(i + 1) * P],
                                      btok[:, g * P:(g + 1) * P], True, True)
                            if i % 4 == 3:
                                last.then_inc(S("st_raw"), 1)
                    pe.wait_ge(S("M_ready"), s + 1)
                    if s:
                        pe.wait_ge(S("y_gated"), 1)
                    def y_terms(h):
                        terms = [(W(4)[:, d * D + h * HP:d * D + (h + 1) * HP], W(d)[:, h * P:(h + 1) * P]) for d in range(2)]
                        if s:
                            terms += [(hTf[:, d * D + h * HP:d * D + (h + 1) * HP], W(2 + d)[:, h * P:(h + 1) * P]) for d in range(2)]
                        return terms
                    for h0 in range(0, HEADS, 2):
                        n_terms = len(y_terms(h0))
                        for n in range(n_terms):
                            for h in (h0, h0 + 1):
                                out = ps[64 * (h % 2):64 * (h % 2) + 64, 5 + h // 8, (h // 2 % 4) * P:(h // 2 % 4 + 1) * P]
                                a, b = y_terms(h)[n]
                                last = mm(pe, out, a, b, n == 0, n == n_terms - 1)
                    last.then_inc(S("y_raw"), 1)
                pe.wait_ge(S("seg_exp"), 24)
                pe.wait_ge(S("keys_twice"), 3)
                for n in range(3):
                    for j in range(KVH):
                        last = turn(ps[:, 1 + n, j * P:(j + 1) * P], W(5)[:, (4 * n + j) * P:(4 * n + j + 1) * P])
                    last.then_inc(S("keys_turned"), 1)
                pe.wait_ge(S("ysq"), 1)
                for k in range(KT):
                    last = mm(pe, ps[:, 0, 0:T], C(MEAN_D), W(4)[:, k * T:(k + 1) * T], k == 0, k == KT - 1)
                last.then_inc(S("yss"), 1)
                pe.wait_ge(S("keys_copied"), 2)
                pe.wait_ge(S("y_gated"), 2)
                mm(pe, ps[:, 4, :], C(ROT), KTL, True, True)
                for b in range(2):
                    last = mm(pe, ps[:, 5 + b, :], C(ROT), qT[:, 4 * b:4 * b + 4, tk(1)], True, True)
                last.then_inc(S("rotated"), 1)
                pe.wait_ge(S("keys_copied"), 3)
                pe.wait_ge(S("yrms"), 1)
                for g in range(3):
                    if g:
                        pe.wait_ge(S("yatt"), g + 1)
                        pe.wait_ge(S("rope"), 1)
                    nh = 8 if g else 16
                    for i in range(nh):
                        h = 8 * (g - 1) + i if g else i
                        b, j = 64 * (h % 2), (h // 4) * P
                        i = place(i, nh)
                        if g == 0:
                            last = mm(pe, ps[:, i // 4, (i % 4) * P:(i % 4 + 1) * P], qT[b:b + 64, h // 2, tk(0)], KTC[b:b + 64, j:j + P], True, True)
                        else:
                            mm(pe, ps[:, i // 2, (i % 2) * T:(i % 2) * T + P], qT[b:b + 64, h // 2, tk(1)], KTP[b:b + 64, j:j + P], True, True)
                            last = mm(pe, ps[:, i // 2, (i % 2) * T + P:(i % 2) * T + T], QR[b:b + 64, (h // 2) * P:(h // 2 + 1) * P], KR[b:b + 64, j:j + P], True, True)
                    last.then_inc(S("scores"), 1)
                    if g:
                        pe.wait_ge(S("pT_low"), 2 * g)
                        pe.wait_ge(S("pT_high"), 2 * g)
                    for i in range(16):
                        if i % 8 == 0:
                            pe.wait_ge(S("probs"), 2 * g + i // 8 + 1)
                        last = turn(ps[:, 4 + i // 4, (i % 4) * P:(i % 4 + 1) * P], W(0)[:, i * P:(i + 1) * P])
                        if i % 8 == 7:
                            last.then_inc(S("probs_turned"), 1)
                    pe.wait_ge(S("pT_low"), 2 * (g + 1))
                    pe.wait_ge(S("pT_high"), 2 * (g + 1))
                    for i0 in range(0, nh, 2):
                        for n in range(2 if g else 1):
                            for i in (i0, i0 + 1):
                                h = 8 * (g - 1) + i if g else i
                                v0 = (h // 4) * 64
                                out = ps[64 * (h % 2):64 * (h % 2) + 64, (i // 8) if g == 0 else 0, (h // 2 % 4) * P:(h // 2 % 4 + 1) * P]
                                q = place(i, nh) * (2 if g else 1) + n
                                v = ckv[:, 1, v0:v0 + 64] if g and n == 0 else kv[:, min(g, 1), 256 + v0:320 + v0]
                                last = mm(pe, out, v, W(1)[:, q * P:(q + 1) * P], n == 0, n == 1 or g == 0)
                    last.then_inc(S("att_raw"), 1)
                pe.wait_ge(S("yatt"), 4)
                pe.wait_ge(S("yssd"), 1)
                out_project(0, lambda t: zs[:, t, :] if t < KT else yatt[:, t - KT, :])

            def odd():
                for d in range(2):
                    for k in range(KT):
                        wait_h(2, k)
                        last = mm(pe, ps[0:16, 0, d * T:(d + 1) * T], wlr[:, k, 16 * d:16 * d + 16], hT[:, k, :], k == 0, k == KT - 1)
                last.then_inc(S("lr_raw"), 1)
                projections(1)
                pe.wait_ge(S("proj_free"), 16 + 4)
                for s in range(NS):
                    for h in range(GH):
                        last = turn(ps[:, 5 + s, h * P:(h + 1) * P], kv[:, s, h * P:(h + 1) * P])
                    last.then_inc(S("gk_turned"), 1)
                pe.wait_ge(S("gk_copied"), 2)
                pe.wait_ge(S("lr"), 1)
                for c in range(4):
                    b, d = (5 + c) % 8, c % 2
                    mm(pe, ps[:, b, :], lr[:, d * T + (c // 2) * P:d * T + (c // 2 + 1) * P], wg[:, d, :], True, True).then_inc(S("gate_raw"), 1)
                pe.wait_ge(S("proj_free"), 28)
                for c in range(4):
                    pe.wait_ge(S("g_ready"), c + 1)
                    for h in range(GH):
                        last = mm(pe, ps[:, c, h * P:(h + 1) * P], W(0)[:, c * 512 + h * P:c * 512 + (h + 1) * P], C(BGE if c % 2 else BLE), True, True)
                    last.then_inc(S("cs_raw"), 1)
                for c in range(4):
                    mm(pe, ps[:, 4 + c, :], C(BLT if c % 2 else BGT), W(0)[:, c * 512:(c + 1) * 512], True, True).then_inc(S("rest_raw"), 1)
                pe.wait_ge(S("ecs"), 8)
                pe.wait_ge(S("qk_ready"), 4)
                for c in range(4):
                    for h in range(GH):
                        for ch in range(2):
                            r, o = c * 512 + h * P + CH * ch, h * P + CH * ch
                            last = mm(pe, ps[CH * ch:CH * ch + CH, c, o:o + CH], W(4)[:, r:r + CH], W(3)[:, r:r + CH], True, True)
                    last.then_inc(S("gatt_raw"), 1)
                pe.wait_ge(S("kdec"), 4)
                for n, (s, d, ch) in enumerate(COMBOS):
                    if n >= 2:
                        pe.wait_ge(S("state"), n - 1)
                    for h in range(GH):
                        r = (2 * s + d) * 512 + h * P
                        last = mm(pe, ps[:, 4 + 2 * (n % 2) + h // 2, (h % 2) * T:(h % 2 + 1) * T], W(0)[CH * ch:CH * ch + CH, r:r + P],
                                  xtok[CH * ch:CH * ch + CH, s, h * GV:(h + 1) * GV], True, True)
                    last.then_inc(S("kv_raw"), 1)
                pe.wait_ge(S("gatt"), 2)
                pe.wait_ge(S("state"), 6)
                for s in range(NS):
                    for h in range(GH):
                        for v in range(2):
                            i = 2 * h + v
                            b, o = 2 * s + i // 4, (i % 4) * P
                            terms = [(xtok[:, s, h * GV + v * P:h * GV + (v + 1) * P], ATT[:, s, h, :], 0, P)]
                            for d in range(2):
                                for ch in range(2):
                                    q = W(3)[:, (2 * s + d) * 512 + h * P + CH * ch:(2 * s + d) * 512 + h * P + CH * ch + CH]
                                    so = d * D + h * GV + v * P
                                    if ch != d:
                                        st = (W(2) if s == 0 else xbf)[:, so:so + P]
                                    elif s:
                                        st = W(5)[:, so:so + P]
                                    else:
                                        continue
                                    terms.append((st, q, CH * ch, CH))
                            for n, (a, q, c0, w) in enumerate(terms):
                                last = mm(pe, ps[:, b, o + c0:o + c0 + w], a, q, n == 0, n == len(terms) - 1, shared=True)
                    last.then_inc(S("gy_raw"), 1)
                pe.wait_ge(S("gsq"), 1)
                for h in range(GH):
                    for v in range(2):
                        last = mm(pe, ps[:, 4 + h // 2, (h % 2) * T:(h % 2 + 1) * T], C(MEAN_V), W(3)[:, (2 * h + v) * T:(2 * h + v + 1) * T], v == 0, v == 1)
                    if h % 2:
                        last.then_inc(S("gss"), 1)
                out_project(1, lambda t: yatt[:, t, :])

            def moe(l):
                for s in range(NS):
                    for k in range(KT):
                        wait_h(2 * l + 1, k)
                        last = mm(pe, ps[:, 0, T + 32 * s:T + 32 * s + 20], hT[:, k, tk(s)], wr[:, l, k, :], k == 0, k == KT - 1)
                last.then_inc(S("logits"), 1)
                pe.wait_ge(S("set_up"), SET_UP)
                for b in range(8):
                    mm(pe, ps[:, 4 + b // 2, (b % 2) * T:(b % 2 + 1) * T], C(IDENT), zero, b % 2 == 0, True, shared=True)
                pe.wait_ge(S("sel"), l + 1)
                sel = [tiny[:, SEL + 16 * s:SEL + 16 * s + 16] for s in range(NS)]
                mm(pe, ps[:, 1, 0:16], C(LT), sel[0], True, True)
                mm(pe, ps[:, 1, 16:32], C(ONES), sel[0], True, False)
                mm(pe, ps[:, 1, 16:32], C(LT), sel[1], False, True)
                mm(pe, ps[:, 1, 32:48], C(ONES), sel[0], True, False)
                mm(pe, ps[:, 1, 32:48], C(ONES), sel[1], False, True).then_inc(S("rank_raw"), 1)
                if l == 0:
                    pe.wait_ge(S("mods"), 3)
                for g in range(4):
                    if g == 1:
                        pe.wait_ge(S("rank_read"), l + 1)
                    for k in range(4):
                        last = turn(ps[:, g, k * P:(k + 1) * P], hT[:, (g % 2) * 4 + k, tk(g // 2)])
                    last.then_inc(S("htok_raw"), 1)
                base = pos[f"moe{l}"]

                def gate_or_up(bank, xs, n0, wait, mark):
                    na = len(xs)
                    for c in range(2):
                        for a in range(na):
                            wait(n0 + c * na + a)
                        for k in range(4):
                            for a, x in enumerate(xs):
                                last = mm(pe, ps[a * CAP:(a + 1) * CAP, bank, :], x[:, 4 * c + k, :], slot(n0 + c * na + a, 4)[:, k, :],
                                          c == 0 and k == 0, c == 1 and k == 3)
                                if k == 3:
                                    mark(last)

                def down(bank, xs, n0, wait, mark):
                    na = len(xs)
                    for c in range(2):
                        for a in range(na):
                            wait(n0 + c * na + a)
                        for k in range(2):
                            for b in range(2):
                                for a, x in enumerate(xs):
                                    last = mm(pe, ps[a * CAP:(a + 1) * CAP, bank + b, :], x[:, 2 * c + k, :],
                                              slot(n0 + c * na + a, 2)[:, k, b * 512:(b + 1) * 512], c == 0 and k == 0, c == 1 and k == 1)
                                    if k == 1 and b == 1:
                                        mark(last)

                def gather(i):
                    for k in range(KT):
                        for s in range(NS):
                            last = mm(pe, ps[:, k // 4, (k % 4) * P:(k % 4 + 1) * P], xtok[:, s, k * P:(k + 1) * P],
                                      DISP[:, bass.ds(i * P + s * D, P)], s == 0, s == 1)
                    last.then_inc(S("gathered"), 1)

                def scatter(i):
                    for m in range(KT):
                        last = mm(pe, ps[:, 4 + m // 2, (m % 2) * T:(m % 2 + 1) * T], YS[:, m * P:(m + 1) * P],
                                  CT[:, bass.ds(i, 1), :], False, False, shared=True)
                    last.then_inc(S("scattered"), 1)

                def pair(i, first=False, final=False):
                    def wait(n):
                        wait_landed(pe, n, i * (2 * PER_EXPERT // RING))
                    done = i + (l * PAIRS)
                    pe.wait_ge(S("hg"), done * 2 + 2)
                    x = [HG[:, :, a * CAP:(a + 1) * CAP] for a in range(2)]
                    if first:
                        pe.wait_ge(S("ct"), 4 * l + 1)
                    gate_or_up(2, x, base, wait, used)
                    if first:
                        pe.wait_ge(S("ct"), 4 * l + 2)
                    if l == 0:
                        pe.wait_ge(S("mods"), i + 3)
                    gate_or_up(3, x, base + 4, wait, used)
                    if first:
                        pe.wait_ge(S("ct"), 4 * l + 4)
                    else:
                        pe.wait_ge(S("ys"), done * 2)
                    if not final:
                        gather(i + 1)
                    pe.wait_ge(S("hact"), done + 1)
                    for f in range(FT):
                        last = turn(ps[:, 2, f * P:(f + 1) * P], HACT[:, f * P:(f + 1) * P])
                    last.then_inc(S("ht_raw"), 1)
                    if l == 0:
                        for c in range(per_pair):
                            ada(3, 4 * c, n_loop + c, i)
                    if not first:
                        scatter(i - 1)
                    pe.wait_ge(S("ht"), done + 1)
                    if not final:
                        pe.wait_ge(S("hg"), done * 2 + 4)
                    down(0, [HT[:, :, a * CAP:(a + 1) * CAP] for a in range(2)], base + 8, wait, used)

                pe.wait_ge(S("disp"), l + 1)
                pe.wait_ge(S("htok"), 4 * l + 4)
                gather(0)
                for q in range(4):
                    if q == 2:
                        pe.wait_ge(S("hg"), l * PAIRS * 2 + 2)
                    for i in range(4 * q, 4 * q + 4):
                        last = turn(ps[:, (q + 2) % 4, (i % 4) * P:(i % 4 + 1) * P], DISW[:, (i % 2) * D + (i // 2) * P:(i % 2) * D + (i // 2 + 1) * P])
                    last.then_inc(S("ct_raw"), 1)
                pair(0, first=True)
                with pe.Fori(1, PAIRS - 1) as i:
                    pair(i)
                pair(PAIRS - 1, final=True)
                pe.wait_ge(S("ys"), (l + 1) * PAIRS * 2)
                scatter(PAIRS - 1)

                pe.wait_ge(S("need"), l + 1)
                most = pe.value_load(need[0:1, l:l + 1], min_val=0, max_val=T)
                with pe.If(most > CAP):
                    pe.sem_inc(S(f"o{l}_used"), PER_EXPERT)
                    with pe.Fori(0, NE) as e:
                        with pe.Fori(1, T // CAP) as r:
                            it = e * (T // CAP - 1) + r

                            def wait(n):
                                pe.wait_ge(S(f"o{l}_landed{n % RING}"), it * 16)

                            def mark(ins):
                                ins.then_inc(S(f"o{l}_used"), 1)
                            pe.wait_ge(S(f"o{l}_v"), it * O_STEPS + (1 - O_STEPS))
                            for k in range(KT):
                                for s in range(NS):
                                    last = mm(pe, ps[:, 0, k * CAP:(k + 1) * CAP], xtok[:, s, k * P:(k + 1) * P],
                                              O_DISP[:, s * CAP:(s + 1) * CAP], s == 0, s == 1)
                            last.then_inc(S(f"o{l}_p"), 1)
                            for s in range(NS):
                                last = mm(pe, ps[0:CAP, 1, tk(s)], O_DISW[:, s * CAP:(s + 1) * CAP], C(IDENT), True, True)
                            last.then_inc(S(f"o{l}_p"), 1)
                            pe.wait_ge(S(f"o{l}_v"), it * O_STEPS + (3 - O_STEPS))
                            gate_or_up(2, [O_HG], 0, wait, mark)
                            gate_or_up(3, [O_HG], 2, wait, mark)
                            pe.wait_ge(S(f"o{l}_v"), it * O_STEPS + (4 - O_STEPS))
                            for f in range(FT):
                                last = mm(pe, ps[:, 1, f * CAP:(f + 1) * CAP], O_ACT[:, f * P:(f + 1) * P], cst[0:CAP, IDENT, 0:CAP], True, True)
                            last.then_inc(S(f"o{l}_p"), 1)
                            pe.wait_ge(S(f"o{l}_v"), it * O_STEPS + (5 - O_STEPS))
                            down(2, [O_HT], 4, wait, mark)
                            pe.wait_ge(S(f"o{l}_v"), it * O_STEPS)
                            for m in range(KT):
                                last = mm(pe, ps[:, 4 + m // 2, (m % 2) * T:(m % 2 + 1) * T], O_YS[:, m * P:(m + 1) * P],
                                          O_CT, False, False, shared=True)
                            last.then_inc(S(f"o{l}_p"), 1)

            pe.wait_ge(S("csilu"), 2)
            pe.wait_ge(S("consts_in"), 16)
            for n in range(n_first):
                ada0(n)
            norm(0)
            even()
            norm(1)
            moe(0)
            norm(2)
            odd()
            norm(3)
            moe(1)
            norm(4)
            pe.wait_ge(S("y_normed"), KT)
            for g in range(4):
                for k in range(4):
                    last = turn(ps[:, 1 + g, k * P:(k + 1) * P], hT[:, (g % 2) * 4 + k, tk(g // 2)])
                last.then_inc(S("y_turned"), 1)

        @block.scalar
        def _(act):
            def load(dst, src, name):
                act.dma_start(dst, src).then_inc(S(name), 16)

            for lo, src in ((BADA, A["b_ada"].rearrange("l (r p) -> (l r) p", p=P)),
                            (NMIX, A["norm_mix_w"].rearrange("l (r p) -> (l r) p", p=P)),
                            (NFFN, A["norm_ffn_w"].rearrange("l (r p) -> (l r) p", p=P)),
                            (CONVW, A["conv_w"][0].rearrange("t (r p) -> (t r) p", p=P)),
                            (CONVB, A["conv_b"][0].rearrange("(r p) -> r p", p=P)),
                            (SSDN, A["ssd_norm_w"][0].rearrange("(r p) -> r p", p=P)),
                            (GLAN, A["gla_norm_w"][0].rearrange("(r p) -> r p", p=P)),
                            (FINN, A["final_norm_w"].rearrange("(r p) -> r p", p=P)),
                            (CVEC, A["c"][0].rearrange("(r p) -> r p", p=P)),
                            (CCTX, A["c_ctx"].rearrange("(r p) -> r p", p=P))):
                load(rows[lo % P:lo % P + src.shape[0], lo // P, :], src, "rows_in")
            load(cst[:, IDENT:IDENT + 1, :], A["consts"][:, IDENT:IDENT + 1, :], "ident_in")
            load(cst[:, IDENT + 1:, :], A["consts"][:, IDENT + 1:, :], "consts_in")
            load(xtok[:, 0, :], A["x_prompt"][0], "x_in")
            load(xtok[:, 1, :], A["x_sample"][0], "x_in")
            act.wait_ge(S("feat_ready"), 1)
            act.activation(csilu[:, :, 0], feat[:, CCTX:CCTX + KT], ACT.Silu).then_inc(S("csilu"), 1)
            act.activation(csilu[:, :, 1], feat[:, CVEC:CVEC + KT], ACT.Silu).then_inc(S("csilu"), 1)
            for d, name in enumerate(("state_ssd_fwd", "state_ssd_bwd")):
                load(W(2)[:, d * D:(d + 1) * D].rearrange("p (i n) -> p i n", i=8),
                     A[name][0, 0].rearrange("(i a) q n -> (a q) i n", a=2), "h0_in")

            def norm(i):
                if i == 3:
                    act.wait_ge(S("gla_stored"), 32)
                for k in range(KT):
                    act.wait_ge(S("x_ready"), KT * i + k + 1 if i else 1)
                    act.activation(hT[:, k, :], xT[:, k, :], ACT.Square).then_inc(S("sq"), 1)
                act.wait_ge(S("set_up"), 1)
                act.wait_ge(S("ss"), i + 1)
                act.activation(rstd[:, 0, :], ps[:, 0, 0:T], ACT.Sqrt, bias=eps[:, :]).then_inc(S("rms"), 1)
                if i < 4:
                    l, c = i // 2, 24 * (i % 2)
                    for k in range(KT):
                        act.wait_ge(S("h_scaled"), i * KT + k + 1)
                        for s in range(NS):
                            act.activation(hT[:, k, tk(s)], hT[:, k, tk(s)], ACT.Identity, bias=mods[:, l, c + k, s:s + 1]).then_inc(S("h_ready"), 1)

            def even():
                act.wait_ge(S("dt_abs"), 1)
                act.activation(tiny[:, DTE:DTE + 64], tiny[:, DTT:DTT + 64], ACT.Exp, scale=-1.0).then_inc(S("dt_exp"), 1)
                act.activation(alog[:, :], alog[:, :], ACT.Exp).then_inc(S("dt_exp"), 1)
                act.wait_ge(S("dt_u"), 1)
                act.activation(tiny[:, DTL:DTL + 64], tiny[:, DTU:DTU + 64], ACT.Ln).then_inc(S("dt_ln"), 1)
                for j in range(16):
                    act.wait_ge(S("slot_used"), pos["in0"] + j + 1)
                    b = ps[:, 1 + j % 4, :]
                    b2 = b.rearrange("p (a t) -> p a t", a=2)
                    if j == 0:
                        act.wait_ge(S("pad_zero"), 1)
                    dst, src, f = ((xpad[:, 2 * j:2 * j + 2, :, 2:2 + P], b.rearrange("p (a s t) -> p a s t", a=2, s=NS), ACT.Copy) if j < 6 else
                                   (kv[:, :, (j - 6) * 256:(j - 5) * 256], b2, ACT.Copy) if j < 8 else
                                   (qT[:, 2 * (j - 8):2 * (j - 8) + 2, :], b2, ACT.Copy) if j < 12 else
                                   (zs[:, 2 * (j - 12):2 * (j - 12) + 2, :], b2, ACT.Silu))
                    act.activation(dst, src, f).then_inc(S("proj_free"), 1)
                    if 6 <= j < 12:
                        p = 2 * (j - 6)
                        act.wait_ge(S("conv_done"), p + 2)
                        act.activation(xbc[:, p:p + 2, :], xbc[:, p:p + 2, :], ACT.Silu).then_inc(S("xbc_ready"), 1)
                    if j == 7:
                        act.wait_ge(S("proj_free"), 8)
                        act.dma_start(O[2][0, 0].rearrange("t h d -> t (h d)"), kv[:, 0, 0:256]).then_inc(S("cache_stored"), 16)
                        act.dma_start(O[3][0, 0].rearrange("t h d -> t (h d)"), kv[:, 0, 256:512]).then_inc(S("cache_stored"), 16)
                for g in range(5):
                    act.wait_ge(S("tok_turned"), g + 1)
                    dst = xtok[:, g // 2, (g % 2) * 512:(g % 2 + 1) * 512] if g < 4 else btok[:, :]
                    act.activation(dst, ps[:, 5 + g % 3, 0:512 if g < 4 else 256], ACT.Copy).then_inc(S("tok_copied"), 1)
                for g in range(4):
                    act.wait_ge(S("h0_turned"), g + 1)
                    act.activation(hTf[:, g * 512:(g + 1) * 512], ps[:, 1 + g, :], ACT.Copy).then_inc(S("h0_copied"), 1)
                act.wait_ge(S("te_raw"), 1)
                act.activation(tiny[:, TE:TE + 32], ps[:, 7, 256:288], ACT.Exp).then_inc(S("te_exp"), 1)
                unit = 0
                for s in range(NS):
                    if s:
                        act.wait_ge(S("y_raw"), 1)
                    for d in range(2):
                        for w in range(1 + s):
                            for q in range(4):
                                act.wait_ge(S("seg_raw"), unit + 1)
                                act.activation(W(2 * w + d)[:, q * 512:(q + 1) * 512], ps[:, 1 + unit % 4, :], ACT.Exp).then_inc(S("seg_exp"), 1)
                                unit += 1
                    if s == 0:
                        for q in range(4):
                            act.wait_ge(S("st_raw"), q + 1)
                            act.activation(yaf[:, q * 512:(q + 1) * 512], ps[:, 1 + q, :], ACT.Copy).then_inc(S("st_copied"), 1)
                        act.wait_ge(S("st_copied"), 4)
                        for d in range(2):
                            act.dma_start(O[4 + d][0, 0].rearrange("(i a) q n -> (a q) i n", a=2),
                                          yaf[:, d * D:(d + 1) * D].rearrange("p (i n) -> p i n", i=8)).then_inc(S("ssd_stored"), 16)
                for n, dst in enumerate((KTC, KTL, KTP)):
                    act.wait_ge(S("keys_turned"), n + 1)
                    act.activation(dst, ps[:, 1 + n, :], ACT.Copy).then_inc(S("keys_copied"), 1)
                act.wait_ge(S("y_gated"), 2)
                act.activation(W(4), zs[:, :, :].rearrange("p k t -> p (k t)"), ACT.Square).then_inc(S("ysq"), 1)
                act.wait_ge(S("yss"), 1)
                act.activation(rstd[:, 1, :], ps[:, 0, 0:T], ACT.Sqrt, bias=eps[:, :]).then_inc(S("yrms"), 1)
                for g in range(3):
                    nh, w = (8, 256) if g else (16, 128)
                    act.wait_ge(S("negm"), g + 1)
                    sc = ps[:, 0:4, :].rearrange("p b (h w) -> p (b h) w", w=w)
                    pr = W(0).rearrange("p (h w) -> p h w", w=w)
                    if g:
                        act.wait_ge(S("probs_turned"), 2 * g)
                    for h in range(nh):
                        act.activation(pr[:, h, :], sc[:, h, :], ACT.Exp, scale=SCALE, bias=tiny[:, NEGM + h:NEGM + h + 1],
                                       accum_out=tiny[:, RSUM + h:RSUM + h + 1]).then_inc(S("p_exp"), 1)
                    act.activation(tiny[:, SNKE:SNKE + nh], tiny[:, SNKD:SNKD + nh], ACT.Exp).then_inc(S("p_exp"), 1)
                    act.wait_ge(S("probs_turned"), 2 * g + 1)
                    if g:
                        act.wait_ge(S("att_raw"), g)
                    for q in range(2):
                        act.activation(W(1)[:, q * 512:(q + 1) * 512], ps[:, 4 + q, :], ACT.Copy).then_inc(S("pT_low"), 1)
                    act.wait_ge(S("att_raw"), g + 1)
                    if g == 0:
                        act.wait_ge(S("ssd_stored"), 32)
                        for b in range(2):
                            act.activation(yatt[:, 4 * b:4 * b + 4, tk(0)], ps[:, b, :].rearrange("p (a t) -> p a t", a=4), ACT.Copy).then_inc(S("yatt"), 1)
                    else:
                        act.activation(yatt[:, 4 * (g - 1):4 * g, tk(1)], ps[:, 0, :].rearrange("p (a t) -> p a t", a=4), ACT.Copy).then_inc(S("yatt"), 1)

            def odd():
                for d, name in enumerate(("state_gla_fwd", "state_gla_bwd")):
                    load(W(5)[:, d * D:(d + 1) * D].rearrange("p (h v) -> p h v", h=GH),
                         A[name][0, 0].rearrange("h k v -> k h v"), "s0_in")
                act.wait_ge(S("lr_raw"), 1)
                act.wait_ge(S("set_up"), SET_UP)
                act.activation(lr[0:LOWRANK, :], ps[0:16, 0, :], ACT.Copy).then_inc(S("lr"), 1)
                for j in range(12):
                    act.wait_ge(S("slot_used"), pos["in1"] + j + 1)
                    b2 = ps[:, 1 + j % 4, :].rearrange("p (a t) -> p a t", a=2)
                    dst, f = ((qT[:, 2 * j:2 * j + 2, :], ACT.Copy) if j < 2 else
                              (kv[:, :, (j - 2) * 256:(j - 1) * 256], ACT.Copy) if j < 4 else
                              (xtok[:, :, (j - 4) * 256:(j - 3) * 256], ACT.Copy) if j < 8 else
                              (zs[:, 2 * (j - 8):2 * (j - 8) + 2, :], ACT.Silu))
                    act.activation(dst, b2, f).then_inc(S("proj_free"), 1)
                halves = [W(1)[:, a * D:(a + 1) * D] for a in range(2)]
                for a, x in enumerate(halves):
                    act.wait_ge(S("gate_abs"), 2 * a + 2)
                    act.activation(x, x, ACT.Exp, scale=-1.0).then_inc(S("gate_exp"), 1)
                for a, x in enumerate(halves):
                    act.wait_ge(S("gate_exp"), a + 1)
                    act.activation(x, x, ACT.Ln, bias=1.0).then_inc(S("gate_ln"), 1)
                act.wait_ge(S("g_ready"), 4)
                for c in range(4):
                    act.wait_ge(S("cs_raw"), c + 1)
                    act.activation(W(1)[:, c * 512:(c + 1) * 512], ps[:, c, :], ACT.Exp).then_inc(S("ecs"), 1)
                    act.activation(W(2)[:, c * 512:(c + 1) * 512], ps[:, c, :], ACT.Exp, scale=-1.0).then_inc(S("ecs"), 1)
                act.wait_ge(S("rest_raw"), 4)
                for c in range(4):
                    act.activation(W(0)[:, c * 512:(c + 1) * 512], ps[:, 4 + c, :], ACT.Exp).then_inc(S("kde"), 1)
                act.wait_ge(S("state"), 4)
                for d in range(2):
                    act.dma_start(O[6 + d][0, 0].rearrange("h k v -> k h v"),
                                  hTf[:, d * D:(d + 1) * D].rearrange("p (h v) -> p h v", h=GH)).then_inc(S("gla_stored"), 16)
                act.wait_ge(S("gy"), 2)
                act.activation(W(3), yaf, ACT.Square).then_inc(S("gsq"), 1)
                for b in range(2):
                    act.wait_ge(S("gss"), b + 1)
                    act.activation(rstd[:, 2 * b:2 * b + 2, :].rearrange("p h t -> p (h t)"), ps[:, 4 + b, :], ACT.Sqrt, bias=eps[:, :]).then_inc(S("grms"), 1)

            def moe(l):
                act.wait_ge(S("g_sub"), l + 1)
                act.activation(tiny[:, GEX:GEX + 8], tiny[:, GEX:GEX + 8], ACT.Exp).then_inc(S("g_exp"), 1)
                act.wait_ge(S("e_sub"), l + 1)
                act.activation(tiny[:, EL:EL + 8], tiny[:, EL:EL + 8], ACT.Exp).then_inc(S("e_exp"), 1)
                for g in range(4):
                    act.wait_ge(S("htok_raw"), 4 * l + g + 1)
                    act.activation(xtok[:, g // 2, (g % 2) * 512:(g % 2 + 1) * 512], ps[:, g, :], ACT.Copy).then_inc(S("htok"), 1)
                base = pos[f"moe{l}"]
                def hg(n):
                    act.wait_ge(S("gathered"), n)
                    act.activation(W(1)[:, 0:512], ps[:, 0, :], ACT.Copy).then_inc(S("hg"), 1)

                def ys(i):
                    act.wait_ge(S("slot_used"), i * (2 * PER_EXPERT) + (base + 12))
                    act.activation(YS[:, 0:512], ps[:, 0, :], ACT.Copy).then_inc(S("ys"), 1)

                def pair(i, first=False, final=False):
                    done = i + (l * PAIRS)
                    if not first:
                        ys(i - 1)
                    act.wait_ge(S("slot_used"), i * (2 * PER_EXPERT) + (base + 4))
                    act.activation(SIL, ps[:, 2, :], ACT.Silu).then_inc(S("sil"), 1)
                    if not final:
                        hg(done + 2)
                    act.wait_ge(S("ht_raw"), done + 1)
                    act.activation(HT, ps[:, 2, :].rearrange("p (f c) -> p f c", f=FT), ACT.Copy).then_inc(S("ht"), 1)

                hg(l * PAIRS + 1)
                for q in range(4):
                    act.wait_ge(S("ct_raw"), 4 * l + q + 1)
                    act.activation(W(0)[:, q * 512:(q + 1) * 512], ps[:, (q + 2) % 4, :], ACT.Copy).then_inc(S("ct"), 1)
                pair(0, first=True)
                with act.Fori(1, PAIRS - 1) as i:
                    pair(i)
                pair(PAIRS - 1, final=True)
                ys(PAIRS - 1)
                act.wait_ge(S("need"), l + 1)
                most = act.value_load(need[0:1, l:l + 1], min_val=0, max_val=T)
                with act.If(most > CAP):
                    with act.Fori(1, NE * (T // CAP - 1) + 1) as it:
                        act.wait_ge(S(f"o{l}_used"), it * PER_EXPERT + 2)
                        act.activation(O_SIL, ps[0:CAP, 2, :], ACT.Silu).then_inc(S(f"o{l}_a"), 1)

            norm(0)
            even()
            norm(1)
            moe(0)
            norm(2)
            odd()
            norm(3)
            moe(1)
            norm(4)
            for g in range(4):
                act.wait_ge(S("y_turned"), g + 1)
                act.activation(xtok[:, g // 2, (g % 2) * 512:(g % 2 + 1) * 512], ps[:, 1 + g, :], ACT.Copy).then_inc(S("y_tok"), 1)
            act.wait_ge(S("cache_stored"), 32)

        @block.vector
        def _(dve):
            step = stepper(dve, "dve_step")
            tt, ts, stt = dve.tensor_tensor, dve.tensor_scalar, dve.scalar_tensor_tensor

            def t2(c, n, s=NS):
                return tiny[:, c:c + s * n].rearrange("p (s n) -> p s n", s=s)

            dve.memset(eps[:, :], EPS).then_inc(S("set_up"), 1)
            for i in range(4):
                dve.memset(pref[:, i:i + 1], float(4 - i)).then_inc(S("set_up"), 1)
            dve.wait_ge(S("rows_turned"), 1)
            dve.memset(lr[:, :], 1.0).then_inc(S("set_up"), 1)
            dve.memset(zero, 0.0).then_inc(S("set_up"), 1)
            dve.tensor_copy(feat[:, 0:234], ps[:, 0, 0:234]).then_inc(S("feat_ready"), 1)
            for g in range(4):
                dve.wait_ge(S("x_turned"), g + 1)
                last = dve.tensor_copy(xT[:, (g % 2) * 4:(g % 2) * 4 + 4, tk(g // 2)], ps[:, 1 + g, :].rearrange("p (k t) -> p k t", k=4))
                if g < 3:
                    step(last)
            last.then_inc(S("x_ready"), KT)
            dve.wait_ge(S("x_ready"), KT)

            def ada(n, rounds=0):
                src = a_slot(n)
                dve.wait_ge(*a_landed(n, rounds))
                before = (n - per_pair + 1) if n >= n_loop else (n - 3)
                if before > 0:
                    dve.wait_ge(S("mac_summed"), rounds * per_pair + before)
                start = summed(n - 1) if n else 0
                for k in range(dve_tiles(n)):
                    for g in range(NS):
                        out = a_sum(n)[:, g]
                        c = csilu[:, k, g:g + 1]
                        if k:
                            dve.wait_ge(S("mac"), rounds * (per_pair * KT * NS) + (start + 2 * k + g - 1))
                            ins = stt(out, src[:, k, :], c, out, ALU.mult, ALU.add)
                        else:
                            ins = ts(out, src[:, k, :], c, None, ALU.mult)
                        ins.then_inc(S("mac"), 1)

            def scales(l, c, w):
                return stt(mods[:, l, c:c + 8], mods[:, l, c:c + 8], 1.0,
                           feat[:, w + 8 * l:w + 8 * l + 8][:, :, None].broadcast_to([P, 8, NS]), ALU.add, ALU.mult)

            def ada0_done(n0, n1):
                dve.wait_ge(S("mac_summed"), n1)
                tt(mods[:, 0, 2 * n0:2 * n1], ps[:, 0, ADA + 4 * n0:ADA + 4 * n1].rearrange("p (r s) -> p r s", s=NS),
                   feat[:, BADA + 2 * n0:BADA + 2 * n1][:, :, None].broadcast_to([P, 2 * (n1 - n0), NS]), ALU.add).then_inc(S("mods"), 1)
                dve.wait_ge(S("mods"), 1 if n0 == 0 else 2)
                step(scales(0, *((8, NMIX) if n0 == 0 else (32, NFFN))))

            def norm(i):
                dve.wait_ge(S("rms"), i + 1)
                step(dve.reciprocal(rstd[:, 0, :], rstd[:, 0, :]))
                for k in range(KT):
                    if i == 4:
                        stt(hT[:, k, :], xT[:, k, :], feat[:, FINN + k:FINN + k + 1], rstd[:, 0, :], ALU.mult, ALU.mult).then_inc(S("y_normed"), 1)
                        continue
                    l, c = i // 2, 24 * (i % 2)
                    for s in range(NS):
                        last = stt(hT[:, k, tk(s)], xT[:, k, tk(s)], mods[:, l, c + 8 + k, s:s + 1], rstd[:, 0, tk(s)], ALU.mult, ALU.mult)
                        if s == 0:
                            step(last)
                    last.then_inc(S("h_scaled"), 1)

            def residual(l, c, count):
                for k in range(KT):
                    for s in range(NS):
                        last = stt(xT[:, k, tk(s)], ps[:, 4 + k // 2, (k % 2) * T + s * P:(k % 2) * T + (s + 1) * P],
                                   mods[:, l, c + k, s:s + 1], xT[:, k, tk(s)], ALU.mult, ALU.add)
                        if s == 0:
                            step(last)
                    last.then_inc(S("x_ready"), 1)
                dve.wait_ge(S("x_ready"), count * KT)

            def even():
                dve.wait_ge(S("dt_raw"), 1)
                X, TM, EX, U1, LN = (tiny[:, c:c + 64] for c in (DTX, DTT, DTE, DTU, DTL))
                step(tt(t2(DTX, 32), ps[:, 0, T:T + 64].rearrange("p (s n) -> p s n", s=NS), dtb[:, None, :].broadcast_to([P, NS, 32]), ALU.add))
                stt(TM, X, -1.0, X, ALU.mult, ALU.max).then_inc(S("dt_abs"), 1)
                dve.wait_ge(S("dt_exp"), 2)
                ts(U1, EX, 1.0, None, ALU.add).then_inc(S("dt_u"), 1)
                dve.wait_ge(S("dt_u"), 1)
                step(stt(TM, U1, -1.0, EX, ALU.add, ALU.subtract))
                step(dve.reciprocal(EX, U1))
                step(tt(TM, TM, EX, ALU.mult))
                dve.wait_ge(S("dt_ln"), 1)
                step(tt(TM, LN, TM, ALU.subtract))
                step(stt(tiny[:, DT:DT + 64], X, 0.0, TM, ALU.max, ALU.add))
                stt(t2(DTA, 32), t2(DT, 32), -1.0, alog[:, None, :].broadcast_to([P, NS, 32]), ALU.mult, ALU.mult).then_inc(S("dtA"), 1)
                for t in range(2 * len(IN[0])):
                    if t % 2 == 0 and t:
                        ada(n_first + t // 2 - 1)
                    if t >= CONV_TILES:
                        continue
                    dve.wait_ge(S("proj_free"), t // 2 + 1)
                    acc = xbc[:, t, :].rearrange("p (s t) -> p s t", s=NS)
                    cw = CONVW + t
                    step(ts(acc, xpad[:, t, :, 0:P], feat[:, cw:cw + 1], feat[:, CONVB + t:CONVB + t + 1], ALU.mult, ALU.add))
                    for j in range(1, TAPS):
                        last = stt(acc, xpad[:, t, :, j:j + P], feat[:, cw + CONV_TILES * j:cw + CONV_TILES * j + 1], acc, ALU.mult, ALU.add)
                        if j < TAPS - 1:
                            step(last)
                    last.then_inc(S("conv_done"), 1)
                ada(n_ada - 1)
                ada0_done(n_first, n_ada)
                for s in range(NS):
                    dve.wait_ge(S("tok_copied"), 5)
                    if s:
                        dve.wait_ge(S("y_raw"), 1)
                    for d in range(2):
                        step(tt(W(4)[:, d * D:(d + 1) * D].rearrange("p (h q) -> p h q", h=HEADS), heads(xtok[:, s, :]),
                                tiny[:, DT + 32 * s + 16 * d:DT + 32 * s + 16 * d + 16][:, :, None].broadcast_to([P, HEADS, HP]), ALU.mult))
                    if s == 0:
                        dve.wait_ge(S("te_exp"), 1)
                        for d in range(2):
                            last = tt(W(3)[:, d * D:(d + 1) * D].rearrange("p (h q) -> p h q", h=HEADS), W(4)[:, d * D:(d + 1) * D].rearrange("p (h q) -> p h q", h=HEADS),
                                      tiny[:, TE + 16 * d:TE + 16 * d + 16][:, :, None].broadcast_to([P, HEADS, HP]), ALU.mult)
                            if d == 0:
                                step(last)
                        last.then_inc(S("xw_ready"), 1)
                    dve.wait_ge(S("cb_raw"), s + 1)
                    cb = ps[:, 0, 0:2 * P].rearrange("p (g t) -> p g t", g=2)
                    for d in range(2):
                        last = tt(tiny[:, CBM + 256 * d:CBM + 256 * d + 256].rearrange("p (g t) -> p g t", g=2), cb,
                                  C(GE if d else LE)[:, None, :].broadcast_to([P, 2, P]), ALU.mult)
                        if d == 0:
                            step(last)
                    last.then_inc(S("cbm"), 1)
                    dve.wait_ge(S("cbm"), s + 1)
                    for d in range(2):
                        dve.wait_ge(S("seg_exp"), (8 + 8 * d + 4) if s else 4 * (d + 1))
                        for g in range(2):
                            m = W(d)[:, g * D:(g + 1) * D].rearrange("p (h t) -> p h t", h=8)
                            last = tt(m, m, tiny[:, CBM + 256 * d + P * g:CBM + 256 * d + P * g + P][:, None, :].broadcast_to([P, 8, P]), ALU.mult)
                            if s or (d, g) != (1, 1):
                                step(last)
                        if s:
                            dve.wait_ge(S("seg_exp"), 8 + 8 * d + 8)
                            for g in range(2):
                                m = W(2 + d)[:, g * D:(g + 1) * D].rearrange("p (h t) -> p h t", h=8)
                                last = tt(m, m, xbc[:, 10 + g, tk(1)][:, None, :].broadcast_to([P, 8, P]), ALU.mult)
                                if (d, g) != (1, 1):
                                    step(last)
                    last.then_inc(S("M_ready"), 1)
                    dve.wait_ge(S("y_raw"), s + 1)
                    for i in range(KT):
                        step(stt(xbc[:, i, tk(s)], xbc[:, i, tk(s)], dsk[:, i:i + 1], ps[:, 5 + i // 4, (i % 4) * P:(i % 4 + 1) * P], ALU.mult, ALU.add))
                    dve.wait_ge(S("proj_free"), 16)
                    tt(zs[:, :, tk(s)], zs[:, :, tk(s)], xbc[:, 0:KT, tk(s)], ALU.mult).then_inc(S("y_gated"), 1)
                def ssd_norm():
                    dve.wait_ge(S("yrms"), 1)
                    step(dve.reciprocal(rstd[:, 1, :], rstd[:, 1, :]))
                    for k in range(KT):
                        last = stt(zs[:, k, :], zs[:, k, :], feat[:, SSDN + k:SSDN + k + 1], rstd[:, 1, :], ALU.mult, ALU.mult)
                        if k < KT - 1:
                            step(last)
                    last.then_inc(S("yssd"), 1)

                def rope():
                    dve.wait_ge(S("rotated"), 1)
                    dve.wait_ge(S("keys_copied"), 2)
                    q8 = QR.rearrange("p (k t) -> p k t", k=KT)
                    w8 = W(2)[:, 0:D].rearrange("p (k t) -> p k t", k=KT)
                    step(tt(w8, ps[:, 5:7, :].rearrange("p b (k t) -> p (b k) t", k=4), C(SIN)[:, None, :].broadcast_to([P, KT, P]), ALU.mult))
                    step(tt(q8, qT[:, :, tk(1)], C(COS)[:, None, :].broadcast_to([P, KT, P]), ALU.mult))
                    step(tt(q8, q8, w8, ALU.add))
                    k4 = KR.rearrange("p (k t) -> p k t", k=4)
                    w4 = W(2)[:, D:D + 512].rearrange("p (k t) -> p k t", k=4)
                    step(tt(w4, ps[:, 4, :].rearrange("p (k t) -> p k t", k=4), C(SIN)[:, None, :].broadcast_to([P, 4, P]), ALU.mult))
                    step(tt(k4, KTL.rearrange("p (k t) -> p k t", k=4), C(COS)[:, None, :].broadcast_to([P, 4, P]), ALU.mult))
                    tt(k4, k4, w4, ALU.add).then_inc(S("rope"), 1)

                done = 0
                for g in range(3):
                    nh, w = (8, 256) if g else (16, 128)
                    h0 = 8 * (g - 1) if g else 0
                    dve.wait_ge(S("scores"), g + 1)
                    sc = ps[:, 0:4, :].rearrange("p b (h w) -> p (b h) w", w=w)
                    step(dve.tensor_reduce(tiny[:, MX:MX + nh], sc, AX.X, ALU.max))
                    sk = sink[:, h0:h0 + nh].rearrange("p (i a) -> p a i", a=2)

                    def eo(c):
                        return tiny[:, c:c + nh].rearrange("p (a i) -> p a i", a=2)
                    step(stt(eo(MX), eo(MX), SCALE, sk, ALU.mult, ALU.max))
                    step(ts(tiny[:, NEGM:NEGM + nh], tiny[:, MX:MX + nh], -1.0, None, ALU.mult))
                    tt(eo(SNKD), sk, eo(MX), ALU.subtract).then_inc(S("negm"), 1)
                    if g == 0:
                        rope()
                    elif g == 1:
                        ssd_norm()
                    done += nh + 1
                    dve.wait_ge(S("p_exp"), done)
                    step(tt(tiny[:, RINV:RINV + nh], tiny[:, RSUM:RSUM + nh], tiny[:, SNKE:SNKE + nh], ALU.add))
                    step(dve.reciprocal(tiny[:, RINV:RINV + nh], tiny[:, RINV:RINV + nh]))
                    pr = W(0).rearrange("p (h w) -> p h w", w=w)
                    for a in (0, nh // 2):
                        tt(pr[:, a:a + nh // 2], pr[:, a:a + nh // 2], tiny[:, RINV + a:RINV + a + nh // 2][:, :, None].broadcast_to([P, nh // 2, w]), ALU.mult).then_inc(S("probs"), 1)
                    dve.wait_ge(S("probs_turned"), 2 * g + 2)
                    if g:
                        dve.wait_ge(S("att_raw"), g)
                    for q in (2, 3):
                        dve.tensor_copy(W(1)[:, q * 512:(q + 1) * 512], ps[:, 4 + q, :]).then_inc(S("pT_high"), 1)
                    if g == 0:
                        dve.wait_ge(S("yrms"), 1)
                    ada(n_ada + g)
                for n in range(n_ada + 3, n_loop):
                    ada(n)
                dve.wait_ge(S("mac_summed"), n_loop)
                tt(mods[:, 1, 0:2 * n_early], ps[:, 3, 0:4 * n_early].rearrange("p (r s) -> p r s", s=NS),
                   feat[:, BADA + 48:BADA + 48 + 2 * n_early][:, :, None].broadcast_to([P, 2 * n_early, NS]), ALU.add).then_inc(S("mods"), 1)
                dve.wait_ge(S("slot_used"), pos["out0"] + n_out[0])
                residual(0, 16, 2)

            def odd():
                step(dve.memset(xpf[:, 0:1024], 0.0))
                for s in range(NS):
                    dve.wait_ge(S("gk_turned"), s + 1)
                    dve.tensor_copy(qT[:, 4:8, tk(s)], ps[:, 5 + s, :].rearrange("p (h t) -> p h t", h=GH)).then_inc(S("gk_copied"), 1)
                for c in range(4):
                    dve.wait_ge(S("gate_raw"), c + 1)
                    x, y = W(0)[:, c * 512:(c + 1) * 512], W(1)[:, c * 512:(c + 1) * 512]
                    step(dve.tensor_copy(x, ps[:, (5 + c) % 8, :]))
                    stt(y, x, -1.0, x, ALU.mult, ALU.max).then_inc(S("gate_abs"), 1)
                for c in range(4):
                    x, y = W(0)[:, c * 512:(c + 1) * 512], W(1)[:, c * 512:(c + 1) * 512]
                    dve.wait_ge(S("gate_ln"), c // 2 + 1)
                    stt(x, x, 0.0, y, ALU.min, ALU.subtract).then_inc(S("g_ready"), 1)
                dve.wait_ge(S("gk_copied"), 2)
                dve.wait_ge(S("proj_free"), 16 + 4)
                for c in range(4):
                    dve.wait_ge(S("ecs"), 2 * c + 2)
                    s = c // 2

                    def h4(i):
                        return W(i)[:, c * 512:(c + 1) * 512].rearrange("p (h t) -> p h t", h=GH)
                    step(stt(h4(3), qT[:, 0:4, tk(s)], GLA_SCALE, h4(1), ALU.mult, ALU.mult))
                    tt(h4(4), qT[:, 4:8, tk(s)], h4(2), ALU.mult).then_inc(S("qk_ready"), 1)
                for c in range(4):
                    dve.wait_ge(S("kde"), c + 1)
                    x = W(0)[:, c * 512:(c + 1) * 512]
                    tt(x, x, kv[:, c // 2, :], ALU.mult).then_inc(S("kdec"), 1)
                for s in range(NS):
                    for d in range(2):
                        dve.wait_ge(S("gatt_raw"), 2 * s + d + 1)
                        for ch in range(2):
                            r = slice(CH * ch, CH * ch + CH)
                            src = ps[r, 2 * s + d, :].rearrange("p (h t) -> p h t", h=GH)[:, :, r]
                            step(tt((ATB if d else ATT)[r, s, :, r], src, cst[r, GE if d else LE, r][:, None, :].broadcast_to([CH, GH, CH]), ALU.mult))
                    for ch in range(2):
                        r = slice(CH * ch, CH * ch + CH)
                        last = tt(ATT[r, s, :, r], ATT[r, s, :, r], ATB[r, s, :, r], ALU.add)
                        if ch == 0:
                            step(last)
                    last.then_inc(S("gatt"), 1)
                dve.wait_ge(S("s0_in"), 32)
                for n, (s, d, ch) in enumerate(COMBOS):
                    dve.wait_ge(S("kv_raw"), n + 1)
                    b = 4 + 2 * (n % 2)
                    first = ch == d
                    dst = (W(2) if s == 0 else xbf) if first else hTf
                    if s == 0 and first:
                        dve.tensor_copy(dst[:, d * D:(d + 1) * D].rearrange("p (b w) -> p b w", b=2), ps[:, b:b + 2, :]).then_inc(S("state"), 1)
                        dve.wait_ge(S("state"), n + 1)
                    else:
                        before = W(5) if s else W(2)
                        for h in range(GH):
                            o = d * D + h * GV
                            dec = (2 * s + d) * 512 + h * P + CH * ch + (0 if d else CH - 1)
                            last = stt(dst[:, o:o + GV], before[:, o:o + GV], W(1)[:, dec:dec + 1],
                                       ps[:, b + h // 2, (h % 2) * T:(h % 2 + 1) * T], ALU.mult, ALU.add)
                            if h < GH - 1:
                                step(last)
                        last.then_inc(S("state"), 1)
                for s in range(NS):
                    dve.wait_ge(S("gy_raw"), s + 1)
                    dve.tensor_copy(yatt[:, :, tk(s)], ps[:, 2 * s:2 * s + 2, :].rearrange("p b (k t) -> p (b k) t", k=4)).then_inc(S("gy"), 1)
                dve.wait_ge(S("proj_free"), 28)
                for i in range(KT):
                    if i % 2 == 0:
                        dve.wait_ge(S("grms"), i // 4 + 1)
                        step(dve.reciprocal(rstd[:, i // 2, :], rstd[:, i // 2, :]))
                    step(stt(yatt[:, i, :], yatt[:, i, :], feat[:, GLAN + i % 2:GLAN + i % 2 + 1], rstd[:, i // 2, :], ALU.mult, ALU.mult))
                    tt(yatt[:, i, :], yatt[:, i, :], zs[:, i, :], ALU.mult).then_inc(S("gyn"), 1)
                dve.wait_ge(S("slot_used"), pos["out1"] + n_out[1])
                residual(1, 16, 4)

            def first_of_max(dst, src, mx):
                p4 = pref[:, None, :].broadcast_to([P, NS, 4])
                step(tt(t2(VAL, 4), src, mx.broadcast_to([P, NS, 4]), ALU.is_equal))
                step(tt(t2(VAL, 4), t2(VAL, 4), p4, ALU.mult))
                step(dve.tensor_reduce(tiny[:, VMX:VMX + 2], t2(VAL, 4), AX.X, ALU.max))
                step(tt(dst, t2(VAL, 4), t2(VMX, 1).broadcast_to([P, NS, 4]), ALU.is_equal))

            def moe(l):
                dve.wait_ge(S("set_up"), 5)
                dve.wait_ge(S("logits"), l + 1)
                lg = t2(LG, 20)
                step(tt(lg, ps[:, 0, T:T + 64].rearrange("p (s n) -> p s n", s=NS)[:, :, 0:20], br[:, l:l + 1, :].broadcast_to([P, NS, 20]), ALU.add))
                step(dve.tensor_reduce(tiny[:, GMAX:GMAX + 2], lg[:, :, 0:4], AX.X, ALU.max))
                tt(t2(GEX, 4), lg[:, :, 0:4], t2(GMAX, 1).broadcast_to([P, NS, 4]), ALU.subtract).then_inc(S("g_sub"), 1)
                first_of_max(t2(OHG, 4), lg[:, :, 0:4], t2(GMAX, 1))
                for s in range(NS):
                    ep = tiny[:, EPR + 16 * s:EPR + 16 * s + 16]
                    step(tt(ep.rearrange("p (e g) -> p g e", g=4), lg[:, s, 4:20].rearrange("p (g e) -> p g e", g=4),
                            tiny[:, OHG + 4 * s:OHG + 4 * s + 4][:, :, None].broadcast_to([P, 4, 4]), ALU.mult))
                step(dve.tensor_reduce(tiny[:, EL:EL + 8], tiny[:, EPR:EPR + 32].rearrange("p (e g) -> p e g", g=4), AX.X, ALU.add))
                step(dve.tensor_reduce(tiny[:, EMX:EMX + 2], t2(EL, 4), AX.X, ALU.max))
                tt(t2(EL, 4), t2(EL, 4), t2(EMX, 1).broadcast_to([P, NS, 4]), ALU.subtract).then_inc(S("e_sub"), 1)
                dve.wait_ge(S("g_exp"), l + 1)
                step(dve.tensor_reduce(tiny[:, GPR:GPR + 2], t2(GEX, 4), AX.X, ALU.add))
                step(dve.reciprocal(tiny[:, GPR:GPR + 2], tiny[:, GPR:GPR + 2]))
                dve.wait_ge(S("e_exp"), l + 1)
                step(dve.tensor_reduce(tiny[:, EMX:EMX + 2], t2(EL, 4), AX.X, ALU.max))
                first_of_max(t2(OH1, 4), t2(EL, 4), t2(EMX, 1))
                step(stt(t2(P2, 4), t2(OH1, 4), -2.0, t2(EL, 4), ALU.mult, ALU.add))
                step(dve.tensor_reduce(tiny[:, M2:M2 + 2], t2(P2, 4), AX.X, ALU.max))
                first_of_max(t2(OH2, 4), t2(P2, 4), t2(M2, 1))
                step(tt(tiny[:, DEN:DEN + 2], tiny[:, EMX:EMX + 2], tiny[:, M2:M2 + 2], ALU.add))
                step(dve.reciprocal(tiny[:, DEN:DEN + 2], tiny[:, DEN:DEN + 2]))
                step(tt(tiny[:, DEN:DEN + 2], tiny[:, DEN:DEN + 2], tiny[:, GPR:GPR + 2], ALU.mult))
                step(tt(t2(OH1, 4), t2(OH1, 4), t2(OH2, 4), ALU.add))
                step(tt(t2(LOC, 4), t2(OH1, 4), t2(EL, 4), ALU.mult))
                step(tt(t2(LOC, 4), t2(LOC, 4), t2(DEN, 1).broadcast_to([P, NS, 4]), ALU.mult))
                for s in range(NS):
                    step(tt(tiny[:, CMB + 16 * s:CMB + 16 * s + 16].rearrange("p (g e) -> p g e", g=4),
                            tiny[:, OHG + 4 * s:OHG + 4 * s + 4][:, :, None].broadcast_to([P, 4, 4]),
                            tiny[:, LOC + 4 * s:LOC + 4 * s + 4][:, None, :].broadcast_to([P, 4, 4]), ALU.mult))
                    last = tt(tiny[:, SEL + 16 * s:SEL + 16 * s + 16].rearrange("p (g e) -> p g e", g=4),
                              tiny[:, OHG + 4 * s:OHG + 4 * s + 4][:, :, None].broadcast_to([P, 4, 4]),
                              tiny[:, OH1 + 4 * s:OH1 + 4 * s + 4][:, None, :].broadcast_to([P, 4, 4]), ALU.mult)
                    if s == 0:
                        step(last)
                last.then_inc(S("sel"), 1)
                dve.wait_ge(S("sel"), l + 1)
                dve.wait_ge(S("rank_raw"), l + 1)
                step(stt(tiny[:, RK:RK + 32], tiny[:, SEL:SEL + 32], -FAR, ps[:, 1, 0:32], ALU.mult, ALU.add))
                dve.tensor_reduce(tiny[:, CNT:CNT + 1], ps[:, 1, 32:48], AX.X, ALU.max).then_inc(S("rank_read"), 1)
                dve.wait_ge(S("rank_read"), l + 1)
                dve.tensor_copy(need[:, l:l + 1], tiny[:, CNT:CNT + 1]).then_inc(S("need"), 1)
                for s in range(NS):
                    d3 = DISP[:, s * D:(s + 1) * D].rearrange("p (e c) -> p e c", e=NE)
                    step(tt(d3, cst[:, IOTA, None, 0:CAP].broadcast_to([P, NE, CAP]),
                            tiny[:, RK + 16 * s:RK + 16 * s + 16][:, :, None].broadcast_to([P, NE, CAP]), ALU.is_equal))
                    last = tt(DISW[:, s * D:(s + 1) * D].rearrange("p (e c) -> p e c", e=NE), d3,
                              tiny[:, CMB + 16 * s:CMB + 16 * s + 16][:, :, None].broadcast_to([P, NE, CAP]), ALU.mult)
                    if s == 0:
                        step(last)
                last.then_inc(S("disp"), 1)
                base = pos[f"moe{l}"]
                def hg(n):
                    dve.wait_ge(S("gathered"), n)
                    dve.tensor_copy(W(1)[:, 512:1024], ps[:, 1, :]).then_inc(S("hg"), 1)

                def ys(i):
                    dve.wait_ge(S("slot_used"), i * (2 * PER_EXPERT) + (base + 12))
                    dve.tensor_copy(YS[:, 512:1024], ps[:, 1, :]).then_inc(S("ys"), 1)

                def pair(i, first=False, final=False):
                    done = i + (l * PAIRS)
                    if not first:
                        ys(i - 1)
                    if l == 0:
                        for c in range(per_pair):
                            ada(n_loop + c, i)
                    dve.wait_ge(S("sil"), done + 1)
                    dve.wait_ge(S("slot_used"), i * (2 * PER_EXPERT) + (base + 8))
                    tt(HACT, SIL, ps[:, 3, :], ALU.mult).then_inc(S("hact"), 1)
                    if not final:
                        hg(done + 2)
                    if l == 0:
                        n = 2 * per_pair
                        dve.wait_ge(S("mac_summed"), i * per_pair + (n_loop + per_pair))
                        tt(mods[:, 1, bass.ds(i * n + 2 * n_early, n), :], ps[:, 3, 0:2 * n].rearrange("p (r s) -> p r s", s=NS),
                           feat[:, bass.ds(i * n + (BADA + 48 + 2 * n_early), n)][:, :, None].broadcast_to([P, n, NS]), ALU.add).then_inc(S("mods"), 1)

                hg(l * PAIRS + 1)
                pair(0, first=True)
                with dve.Fori(1, PAIRS - 1) as i:
                    pair(i)
                pair(PAIRS - 1, final=True)
                ys(PAIRS - 1)
                if l == 0:
                    dve.wait_ge(S("mods"), 3 + PAIRS)
                    step(scales(1, 8, NMIX))
                    step(scales(1, 32, NFFN))
                dve.wait_ge(S("scattered"), PAIRS * (l + 1))
                dve.wait_ge(S("need"), l + 1)
                most = dve.value_load(need[0:1, l:l + 1], min_val=0, max_val=T)
                with dve.If(most > CAP):
                    with dve.Fori(0, NE) as e:
                        with dve.Fori(1, T // CAP) as r:
                            it = e * (T // CAP - 1) + r
                            rk = tiny[:, RK:RK + 32].rearrange("p (s e) -> p s e", s=NS)[:, :, bass.ds(e, 1)]
                            cw = tiny[:, CMB:CMB + 32].rearrange("p (s e) -> p s e", s=NS)[:, :, bass.ds(e, 1)]
                            iota = cst[:, IOTA:IOTA + 2, :].rearrange("p a b -> p (a b)")[:, bass.ds(r * CAP, CAP)]
                            dp, dw = (x.rearrange("p (s c) -> p s c", s=NS) for x in (O_DISP, O_DISW))
                            tt(dp, iota[:, None, :].broadcast_to([P, NS, CAP]), rk.broadcast_to([P, NS, CAP]), ALU.is_equal).then_inc(S(f"o{l}_d"), 1)
                            dve.wait_ge(S(f"o{l}_d"), it)
                            tt(dw, dp, cw.broadcast_to([P, NS, CAP]), ALU.mult).then_inc(S(f"o{l}_v"), 1)
                            dve.wait_ge(S(f"o{l}_p"), it * 4 + (1 - 4))
                            dve.tensor_copy(O_HG, ps[:, 0, :].rearrange("p (k c) -> p k c", k=KT)).then_inc(S(f"o{l}_v"), 1)
                            dve.wait_ge(S(f"o{l}_p"), it * 4 + (2 - 4))
                            dve.tensor_copy(O_CT, ps[0:CAP, 1, 0:T]).then_inc(S(f"o{l}_v"), 1)
                            dve.wait_ge(S(f"o{l}_a"), it)
                            dve.wait_ge(S(f"o{l}_used"), it * PER_EXPERT + 4)
                            tt(O_ACT, O_SIL, ps[0:CAP, 3, :], ALU.mult).then_inc(S(f"o{l}_v"), 1)
                            dve.wait_ge(S(f"o{l}_p"), it * 4 + (3 - 4))
                            dve.tensor_copy(O_HT, ps[:, 1, 0:T].rearrange("p (f c) -> p f c", f=FT)).then_inc(S(f"o{l}_v"), 1)
                            dve.wait_ge(S(f"o{l}_used"), it * PER_EXPERT + PER_EXPERT)
                            dve.tensor_copy(O_YS, ps[0:CAP, 2:4, :].rearrange("p a b -> p (a b)")).then_inc(S(f"o{l}_v"), 1)
                            dve.wait_ge(S(f"o{l}_p"), it * 4)
                residual(l, 40, 2 * l + 3)

            dve.wait_ge(S("csilu"), 2)
            for n in range(n_first):
                ada(n)
            ada0_done(0, n_first)
            dve.wait_ge(S("small_in"), SMALL)
            step(dve.tensor_copy(dsk[0:64, :], dskb[0:64, :].rearrange("p (i a) -> p a i", a=2)[:, 0, :]))
            step(dve.tensor_copy(dsk[64:128, :], dskb[64:128, :].rearrange("p (i a) -> p a i", a=2)[:, 1, :]))
            norm(0)
            even()
            norm(1)
            moe(0)
            norm(2)
            odd()
            norm(3)
            moe(1)
            norm(4)


_INS = ['x_prompt', 'x_sample', 'cache_k_attn', 'cache_v_attn', 'state_ssd_fwd', 'state_ssd_bwd', 'state_gla_fwd',
        'state_gla_bwd', 'c', 'c_ctx', 'w_ada', 'b_ada', 'norm_mix_w', 'norm_ffn_w', 'w_in_even', 'conv_w', 'conv_b',
        'dt_bias_fwd', 'dt_bias_bwd', 'a_log_fwd', 'a_log_bwd', 'd_skip', 'ssd_norm_w', 'attn_sink', 'w_out_even',
        'w_in_odd', 'w_gk2_fwd', 'b_gk_fwd', 'w_gk2_bwd', 'b_gk_bwd', 'gla_norm_w', 'w_out_odd', 'w_router_group',
        'b_router_group', 'w_router_expert', 'b_router_expert', 'w_gate_exp', 'w_up_exp', 'w_down_exp', 'final_norm_w']
_OUTS = [(1, 128, 1024), (1, 128, 1024), (1, 1, 128, 4, 64), (1, 1, 128, 4, 64), (1, 1, 16, 64, 128), (1, 1, 16, 64, 128),
         (1, 1, 4, 128, 256), (1, 1, 4, 128, 256)]


def kernel(**inputs):
    import concourse.bacc as _bacc
    from concourse.bass_utils import run_bass_kernel_spmd as _run

    nc = _bacc.Bacc("TRN2", target_bir_lowering=False, num_devices=1)
    arrays, args = {}, {}
    for name in _INS:
        a = np.ascontiguousarray(inputs[name])
        arrays[f"in_{name}_dram"] = a
        args[name] = nc.dram_tensor(f"in_{name}_dram", a.shape, F32, kind="ExternalInput").ap()
    arrays["in_consts_dram"] = constants()
    args["consts"] = nc.dram_tensor("in_consts_dram", (P, NCONST, P), F32, kind="ExternalInput").ap()
    outs = [nc.dram_tensor(f"out_{i}_dram", shape, F32, kind="ExternalOutput").ap() for i, shape in enumerate(_OUTS)]
    build(nc, args, outs)
    r = _run(nc, [arrays], core_ids=[0])
    return tuple(r.results[0][f"out_{i}_dram"] for i in range(len(_OUTS)))
```
